# Optimizing a Trainium2 kernel written in Bass

```python
import jax, jax.numpy as jnp
from jax import lax
import numpy as np

D_MODEL = 1024
BATCH = 1
SEQ = 256
DEPTH = 1
DEC_BATCH = 8
DEC_SEQ = 1
PAST_LEN = 2048
PAGE_SIZE = 128

DN_HEADS = 8
DN_DK = 128
DN_DV = 128
DN_KEY = DN_HEADS * DN_DK
DN_VAL = DN_HEADS * DN_DV
QKV_DIM = 2 * DN_KEY + DN_VAL
SHORT_CONV = 4
CHUNK = 64
CONF_DIM = D_MODEL
CONF_CONV = 31
N_EXPERTS = 32
TOP_K = 4
D_FF = D_MODEL
SWIGLU_LIMIT = 7.0
SWIGLU_ALPHA = 1.702
MOE_BLOCK = 64
NORM_EPS = 1e-6
IN_SPLITS = (QKV_DIM, QKV_DIM + DN_VAL, QKV_DIM + DN_VAL + DN_HEADS, QKV_DIM + DN_VAL + 2 * DN_HEADS,
             QKV_DIM + DN_VAL + 2 * DN_HEADS + 2 * CONF_DIM)
IN_DIM = QKV_DIM + DN_VAL + 2 * DN_HEADS + 2 * CONF_DIM + 2 * D_MODEL

kernel_name = 'hybrid_gdn_conformer_moe_decoder_step'

def rmsnorm(x, g):
    xf = x.astype(jnp.float32)
    y = xf * lax.rsqrt(jnp.mean(xf * xf, axis=-1, keepdims=True) + NORM_EPS)
    return (y * g.astype(jnp.float32)).astype(x.dtype)

def layernorm(x, g, b):
    xf = x.astype(jnp.float32)
    mu = jnp.mean(xf, axis=-1, keepdims=True)
    xc = xf - mu
    y = xc * lax.rsqrt(jnp.mean(xc * xc, axis=-1, keepdims=True) + NORM_EPS)
    return (y * g.astype(jnp.float32) + b.astype(jnp.float32)).astype(x.dtype)

def l2norm(x):
    return x * lax.rsqrt(jnp.sum(x * x, axis=-1, keepdims=True) + NORM_EPS)

def causal_dwconv(x_ext, w):
    return lax.conv_general_dilated(x_ext, w[:, None, :].astype(x_ext.dtype), window_strides=(1,),
                                    padding='VALID', dimension_numbers=('NWC', 'WIO', 'NWC'),
                                    feature_group_count=x_ext.shape[-1])

def gated_delta_chunked(q, k, v, g, beta, s0):
    B, T, H, _ = q.shape
    n = T // CHUNK

    def chunks(a):
        a = a.reshape((B, n, CHUNK, H) + a.shape[3:])
        return jnp.moveaxis(a, (1, 3), (0, 2))

    qc, kc, vc, bc = chunks(q), chunks(k), chunks(v), chunks(beta)
    gc = jnp.cumsum(chunks(g), axis=-1)
    idx = jnp.arange(CHUNK)
    causal = idx[:, None] >= idx[None, :]
    decay = jnp.exp(jnp.where(causal, gc[..., :, None] - gc[..., None, :], -jnp.inf))
    kk = jnp.einsum('nbhid,nbhjd->nbhij', kc * bc[..., None], kc) * decay
    a_mat = jnp.where(idx[:, None] > idx[None, :], kk, 0.0) + jnp.eye(CHUNK, dtype=jnp.float32)
    rhs = jnp.concatenate([vc * bc[..., None], kc * (bc * jnp.exp(gc))[..., None]], axis=-1)
    sol = lax.linalg.triangular_solve(a_mat, rhs, left_side=True, lower=True, unit_diagonal=True)
    u, w = sol[..., :DN_DV], sol[..., DN_DV:]

    def step(S, inp):
        qi, ki, ui, wi, gi, di = inp
        v_new = ui - jnp.einsum('bhck,bhkv->bhcv', wi, S)
        intra = jnp.einsum('bhik,bhjk->bhij', qi, ki) * di
        o = (jnp.einsum('bhck,bhkv->bhcv', qi * jnp.exp(gi)[..., None], S)
             + jnp.einsum('bhij,bhjv->bhiv', intra, v_new))
        g_last = gi[..., -1:]
        S = (S * jnp.exp(g_last)[..., None]
             + jnp.einsum('bhck,bhcv->bhkv', ki * jnp.exp(g_last - gi)[..., None], v_new))
        return S, o

    s_fin, oc = lax.scan(step, s0, (qc, kc, u, w, gc, decay))
    o = jnp.moveaxis(oc, (0, 2), (1, 3)).reshape(B, T, H, DN_DV)
    return o, s_fin

def gated_delta_recurrent(q, k, v, g, beta, s0):
    def step(S, inp):
        qt, kt, vt, gt, bt = inp
        S = S * jnp.exp(gt)[..., None, None]
        delta = (vt - jnp.einsum('bhk,bhkv->bhv', kt, S)) * bt[..., None]
        S = S + kt[..., :, None] * delta[..., None, :]
        return S, jnp.einsum('bhk,bhkv->bhv', qt, S)

    xs = (jnp.moveaxis(q, 1, 0), jnp.moveaxis(k, 1, 0), jnp.moveaxis(v, 1, 0),
          jnp.moveaxis(g, 1, 0), jnp.moveaxis(beta, 1, 0))
    s_fin, o = lax.scan(step, s0, xs)
    return jnp.moveaxis(o, 0, 1), s_fin

def token_mixers(h, s_dn, buf_qkv, buf_glu, w_in, w_qkv_conv, a_log, dt_bias, g_dn_norm,
                 w_dw_conv, b_dw_conv, g_ln_conv, b_ln_conv, w_pw_conv, b_pw_conv, w_out, chunked):
    B, T, _ = h.shape
    f32 = jnp.float32
    proj = h @ w_in
    qkv_pre, z, b_logit, a_logit, glu, mgate = jnp.split(proj, IN_SPLITS, axis=-1)
    qkv_ext = jnp.concatenate([buf_qkv.astype(qkv_pre.dtype), qkv_pre], axis=1)
    new_buf_qkv = qkv_ext[:, -(SHORT_CONV - 1):]
    qkv = jax.nn.silu(causal_dwconv(qkv_ext, w_qkv_conv)).astype(f32)
    q, k, v = jnp.split(qkv, (DN_KEY, 2 * DN_KEY), axis=-1)
    q = l2norm(q.reshape(B, T, DN_HEADS, DN_DK)) * (DN_DK ** -0.5)
    k = l2norm(k.reshape(B, T, DN_HEADS, DN_DK))
    v = v.reshape(B, T, DN_HEADS, DN_DV)
    beta = jax.nn.sigmoid(b_logit.astype(f32))
    g = -jnp.exp(a_log.astype(f32)) * jax.nn.softplus(a_logit.astype(f32) + dt_bias.astype(f32))
    s0 = s_dn.astype(f32)
    if chunked:
        o, s_new = gated_delta_chunked(q, k, v, g, beta, s0)
    else:
        o, s_new = gated_delta_recurrent(q, k, v, g, beta, s0)
    zf = z.astype(f32).reshape(B, T, DN_HEADS, DN_DV)
    o = (o * lax.rsqrt(jnp.mean(o * o, axis=-1, keepdims=True) + NORM_EPS)
         * g_dn_norm.astype(f32) * jax.nn.silu(zf))
    dn_out = o.reshape(B, T, DN_VAL).astype(h.dtype)
    u_val, u_gate = jnp.split(glu, 2, axis=-1)
    u = u_val * jax.nn.sigmoid(u_gate)
    u_ext = jnp.concatenate([buf_glu.astype(u.dtype), u], axis=1)
    new_buf_glu = u_ext[:, -(CONF_CONV - 1):]
    cv = causal_dwconv(u_ext, w_dw_conv) + b_dw_conv
    cv = jax.nn.silu(layernorm(cv, g_ln_conv, b_ln_conv))
    cv_out = cv @ w_pw_conv + b_pw_conv
    gate_dn, gate_cv = jnp.split(jax.nn.sigmoid(mgate), 2, axis=-1)
    merged = gate_dn * dn_out + gate_cv * cv_out
    return merged @ w_out, s_new, new_buf_qkv, new_buf_glu

def moe(h, w_router, b_router, w_gate_up, b_gate_up, w_down, b_down):
    T, D = h.shape
    logits = h.astype(jnp.float32) @ w_router.astype(jnp.float32) + b_router.astype(jnp.float32)
    top_val, top_idx = lax.top_k(logits, TOP_K)
    gates = jax.nn.softmax(top_val, axis=-1).astype(h.dtype)
    M = T * TOP_K
    n_blocks = -(-M // MOE_BLOCK) + N_EXPERTS
    flat_e = top_idx.reshape(M)
    flat_tok = jnp.arange(M, dtype=jnp.int32) // TOP_K
    order = jnp.argsort(flat_e)
    sorted_e = flat_e[order]
    counts = jnp.bincount(flat_e, length=N_EXPERTS)
    blocks_per_e = (counts + MOE_BLOCK - 1) // MOE_BLOCK
    cum_blocks = jnp.cumsum(blocks_per_e)
    pad_start = (cum_blocks - blocks_per_e) * MOE_BLOCK
    grp_start = jnp.cumsum(counts) - counts
    dest = pad_start[sorted_e] + jnp.arange(M, dtype=jnp.int32) - grp_start[sorted_e]
    row_tok = jnp.full((n_blocks * MOE_BLOCK,), T, jnp.int32).at[dest].set(flat_tok[order])
    x_pad = jnp.concatenate([h, jnp.zeros((1, D), h.dtype)], axis=0)[row_tok]
    x_pad = x_pad.reshape(n_blocks, MOE_BLOCK, D)
    block_e = jnp.minimum(jnp.searchsorted(cum_blocks, jnp.arange(n_blocks), side='right'), N_EXPERTS - 1)

    def expert_block(args):
        xb, e = args
        gu = xb @ w_gate_up[e] + b_gate_up[e]
        gl, up = jnp.split(gu, 2, axis=-1)
        gl = jnp.minimum(gl, SWIGLU_LIMIT)
        up = jnp.clip(up, -SWIGLU_LIMIT, SWIGLU_LIMIT)
        act = gl * jax.nn.sigmoid(SWIGLU_ALPHA * gl) * (up + 1.0)
        return act @ w_down[e] + b_down[e]

    y_pad = lax.map(expert_block, (x_pad, block_e)).reshape(n_blocks * MOE_BLOCK, D)
    slot_pos = jnp.zeros((M,), jnp.int32).at[order].set(dest)
    y = y_pad[slot_pos].reshape(T, TOP_K, D)
    return jnp.einsum('tkd,tk->td', y, gates)

def trunk(x, c, s_dn, buf_qkv, buf_glu, chunked, p):
    new_s, new_q, new_g = [], [], []
    for l in range(DEPTH):
        ada = jax.nn.silu(c) @ p['w_ada'][l] + p['b_ada'][l]
        sh1, sc1, gt1, sh2, sc2, gt2 = jnp.split(ada[:, None, :], 6, axis=-1)
        h = rmsnorm(x, p['g_pre_mix'][l]) * (1.0 + sc1) + sh1
        m, s, bq, bg = token_mixers(h, s_dn[l], buf_qkv[l], buf_glu[l], p['w_in'][l], p['w_qkv_conv'][l],
                                    p['a_log'][l], p['dt_bias'][l], p['g_dn_norm'][l], p['w_dw_conv'][l],
                                    p['b_dw_conv'][l], p['g_ln_conv'][l], p['b_ln_conv'][l],
                                    p['w_pw_conv'][l], p['b_pw_conv'][l], p['w_out'][l], chunked)
        x = x + gt1 * rmsnorm(m, p['g_post_mix'][l])
        h = rmsnorm(x, p['g_pre_ffn'][l]) * (1.0 + sc2) + sh2
        B, T, D = h.shape
        f = moe(h.reshape(B * T, D), p['w_router'][l], p['b_router'][l], p['w_gate_up'][l],
                p['b_gate_up'][l], p['w_down'][l], p['b_down'][l]).reshape(B, T, D)
        x = x + gt2 * rmsnorm(f, p['g_post_ffn'][l])
        new_s.append(s)
        new_q.append(bq)
        new_g.append(bg)
    return x, jnp.stack(new_s), jnp.stack(new_q), jnp.stack(new_g)

def setup_inputs(seed: int = 0) -> dict:
    key = jax.random.key(seed)
    ks = iter(jax.random.split(key, 40))

    def nrm(shape, s):
        return jax.random.normal(next(ks), shape, jnp.float32) * s

    def gain(shape):
        return 1.0 + nrm(shape, 0.05)

    D = D_MODEL
    return {
        'x_prompt': nrm((BATCH, SEQ, D), 1.0),
        'x_sample': nrm((DEC_BATCH, DEC_SEQ, D), 1.0),
        'c_prompt': nrm((BATCH, D), 1.0),
        'c_sample': nrm((DEC_BATCH, D), 1.0),
        'state_dn': nrm((DEPTH, DEC_BATCH, DN_HEADS, DN_DK, DN_DV), 0.1),
        'state_qkv_conv': nrm((DEPTH, DEC_BATCH, SHORT_CONV - 1, QKV_DIM), 1.0),
        'state_glu_conv': nrm((DEPTH, DEC_BATCH, CONF_CONV - 1, CONF_DIM), 0.5),
        'w_ada': nrm((DEPTH, D, 6 * D), 0.5 * D ** -0.5),
        'b_ada': nrm((DEPTH, 6 * D), 0.02),
        'g_pre_mix': gain((DEPTH, D)),
        'g_post_mix': gain((DEPTH, D)),
        'g_pre_ffn': gain((DEPTH, D)),
        'g_post_ffn': gain((DEPTH, D)),
        'w_in': nrm((DEPTH, D, IN_DIM), D ** -0.5),
        'w_qkv_conv': nrm((DEPTH, SHORT_CONV, QKV_DIM), SHORT_CONV ** -0.5),
        'a_log': jnp.log(jax.random.uniform(next(ks), (DEPTH, DN_HEADS), jnp.float32, 1.0, 16.0)),
        'dt_bias': nrm((DEPTH, DN_HEADS), 0.1),
        'g_dn_norm': gain((DEPTH, DN_DV)),
        'w_dw_conv': nrm((DEPTH, CONF_CONV, CONF_DIM), CONF_CONV ** -0.5),
        'b_dw_conv': nrm((DEPTH, CONF_DIM), 0.02),
        'g_ln_conv': gain((DEPTH, CONF_DIM)),
        'b_ln_conv': nrm((DEPTH, CONF_DIM), 0.02),
        'w_pw_conv': nrm((DEPTH, CONF_DIM, D), CONF_DIM ** -0.5),
        'b_pw_conv': nrm((DEPTH, D), 0.02),
        'w_out': nrm((DEPTH, D, D), D ** -0.5),
        'w_router': nrm((DEPTH, D, N_EXPERTS), D ** -0.5),
        'b_router': nrm((DEPTH, N_EXPERTS), 0.01),
        'w_gate_up': nrm((DEPTH, N_EXPERTS, D, 2 * D_FF), D ** -0.5),
        'b_gate_up': nrm((DEPTH, N_EXPERTS, 2 * D_FF), 0.02),
        'w_down': nrm((DEPTH, N_EXPERTS, D_FF, D), D_FF ** -0.5),
        'b_down': nrm((DEPTH, N_EXPERTS, D), 0.02),
    }

def reference(x_prompt, x_sample, c_prompt, c_sample, state_dn, state_qkv_conv, state_glu_conv,
              w_ada, b_ada, g_pre_mix, g_post_mix, g_pre_ffn, g_post_ffn, w_in, w_qkv_conv, a_log,
              dt_bias, g_dn_norm, w_dw_conv, b_dw_conv, g_ln_conv, b_ln_conv, w_pw_conv, b_pw_conv,
              w_out, w_router, b_router, w_gate_up, b_gate_up, w_down, b_down):
    p = dict(w_ada=w_ada, b_ada=b_ada, g_pre_mix=g_pre_mix, g_post_mix=g_post_mix, g_pre_ffn=g_pre_ffn,
             g_post_ffn=g_post_ffn, w_in=w_in, w_qkv_conv=w_qkv_conv, a_log=a_log, dt_bias=dt_bias,
             g_dn_norm=g_dn_norm, w_dw_conv=w_dw_conv, b_dw_conv=b_dw_conv, g_ln_conv=g_ln_conv,
             b_ln_conv=b_ln_conv, w_pw_conv=w_pw_conv, b_pw_conv=b_pw_conv, w_out=w_out,
             w_router=w_router, b_router=b_router, w_gate_up=w_gate_up, b_gate_up=b_gate_up,
             w_down=w_down, b_down=b_down)
    bp = x_prompt.shape[0]
    s0_p = jnp.zeros((DEPTH, bp, DN_HEADS, DN_DK, DN_DV), jnp.float32)
    bq0_p = jnp.zeros((DEPTH, bp, SHORT_CONV - 1, QKV_DIM), x_prompt.dtype)
    bg0_p = jnp.zeros((DEPTH, bp, CONF_CONV - 1, CONF_DIM), x_prompt.dtype)
    y_prompt, s_p, q_p, g_p = trunk(x_prompt, c_prompt, s0_p, bq0_p, bg0_p, True, p)
    y_sample, s_s, q_s, g_s = trunk(x_sample, c_sample, state_dn, state_qkv_conv, state_glu_conv, False, p)
    return (y_prompt, y_sample,
            s_p.astype(state_dn.dtype), q_p.astype(state_qkv_conv.dtype), g_p.astype(state_glu_conv.dtype),
            s_s.astype(state_dn.dtype), q_s.astype(state_qkv_conv.dtype), g_s.astype(state_glu_conv.dtype))


_drawn_inputs = setup_inputs


def setup_inputs(seed=0):
    import zlib

    import numpy as np

    out = dict(_drawn_inputs(seed))
    spreads = {}
    factors = {'g_post_ffn': 4.042,
     'b_ln_conv': 3.699,
     'b_pw_conv': 3.78,
     'b_router': 2.749,
     'b_gate_up': 8.0,
     'b_down': 8.0}
    for name, (base, spread) in spreads.items():
        noise = np.random.default_rng([zlib.crc32(name.encode()), seed]).standard_normal(out[name].shape)
        drawn = base * np.exp(spread * noise) if base else spread * noise
        out[name] = __import__('jax').numpy.asarray(drawn.astype(out[name].dtype))
    for name, factor in factors.items():
        out[name] = (out[name] * factor).astype(out[name].dtype)
    return out
```

```python
import concourse.bass as bass
from concourse import mybir
from contextlib import ExitStack

F32 = mybir.dt.float32
F32R = mybir.dt.float32r
BF16 = mybir.dt.bfloat16
I32 = mybir.dt.int32
ALU = mybir.AluOpType
ACT = mybir.ActivationFunctionType
AX = mybir.AxisListType

P = 128
D = 1024
KD = D // P
NPR = 256
NDE = 8
NT = NPR + NDE
H = 8
CH = 128
NC = NPR // CH
LEVELS = 7
SC = 4
CC = 31
E = 32
TOPK = 4
CAP = 64
OVF = NT * TOPK // CAP
NBLK = E + OVF
NTAB = NBLK + 1
UNITS = 12
GU = 8
UW = 2048
NSTG = 6
LIMIT, ALPHA = 7.0, 1.702
EPS = 1e-6
FF = 1024
NQKV = 3 * KD
BW = 512
CPB = BW // P
RING = 4

PV = {}
_at = 0
for _name, _n in (("b_ada", 48), ("g_pre_mix", 8), ("g_post_mix", 8), ("g_pre_ffn", 8), ("g_post_ffn", 8),
                  ("w_qkv_conv", NQKV * SC), ("w_dw", KD * CC), ("b_dw", 8), ("g_ln", 8), ("b_ln", 8),
                  ("b_pw", 8), ("g_dn", 1), ("a_log", 8), ("dt_bias", 8), ("b_router", E)):
    PV[_name] = (_at, _at + _n)
    _at += _n
NPV = _at
CV = {}
_at = 0
for _name, _n in (("ident", P), ("upper", P), ("levels", LEVELS * P), ("eps", 4)):
    CV[_name] = (_at, _at + _n)
    _at += _n
NCV = _at

CX = {}
_at = 0
for _name, _n in (("iota", CAP), ("strict_upper", P), ("tokid", 3), ("valid", 3), ("experts", E), ("fold", CAP),
                  ("blocks", OVF)):
    CX[_name] = (_at, _at + _n)
    _at += _n
NCX = _at

QKV_COLS, GLU0 = 3 * D, 4 * D + 2 * H
MG0 = GLU0 + 2 * D
BLOCKS = ([("ada", BW * n) for n in range(4)]
          + [("in", BW * n) for n in range(8)]
          + [("in", GLU0 + BW * n) for n in range(4)]
          + [("in", MG0 + D + BW * n) for n in range(2)]
          + [("ada", BW * n) for n in range(4, 12)]
          + [("in", MG0 + BW * n) for n in range(2)]
          + [("pw", BW * n) for n in range(2)]
          + [("out", BW * n) for n in range(2)])
NB = len(BLOCKS)
C_ADA1, C_QKV, C_Z, C_UV, C_UG, C_GCV, C_ADA2, C_GDN, C_PW, C_OUT = 0, 16, 40, 48, 56, 64, 72, 104, 112, 120


def build(nc, A, O):
    ctx = ExitStack()
    with ctx:
        def sb(name, shape, dt=F32):
            return ctx.enter_context(nc.sbuf_tensor(name, shape, dt))

        def sem(name):
            return ctx.enter_context(nc.semaphore(name))

        lows = ExitStack()
        ringL = lows.enter_context(nc.sbuf_tensor("ringL", [P, RING, KD, BW], F32R))
        workL = lows.enter_context(nc.sbuf_tensor("workL", [P, 8, D], F32R))
        lows.close()
        ring = sb("ring", [P, RING, KD, BW])
        work = sb("work", [P, 8, D])
        hT = sb("hT", [P, KD, NT])
        qT = sb("qT", [P, KD, NT])
        pv = sb("pv", [P, NPV])
        cv = sb("cv", [P, NCV])
        ones = sb("ones", [P, P])
        row = sb("row", [P, 2, NT])
        cg = sb("cg", [P, 4, KD, 1 + NDE])
        phase1 = ExitStack()

        def sb(name, shape, dt=F32):
            return phase1.enter_context(nc.sbuf_tensor(name, shape, dt))
        kT = sb("kT", [P, KD, NT])
        vT = sb("vT", [P, KD, NT])
        zT = sb("zT", [P, KD, NT])
        gcvT = sb("gcvT", [P, KD, NT])
        gdnT = sb("gdnT", [P, KD, NT])
        cvT = sb("cvT", [P, KD, NT])
        uP = sb("uP", [P, KD, CC - 1 + NPR])
        uD = sb("uD", [P, KD, NDE, CC])
        xD = sb("xD", [P, NQKV, NDE, SC])
        q3 = sb("q3", [P, NQKV, SC - 1])
        cT = sb("cT", [P, KD, 1 + NDE])
        adaT = sb("adaT", [P, 6, KD, 1 + NDE])
        wba = sb("wba", [P, KD, 2 * H])
        ba = sb("ba", [P, 3, 2 * H])
        tk = sb("tk", [P, 14, 3, H])
        S = sb("S", [P, H, P])
        egl = sb("egl", [P, H])
        gl = sb("gl", [P, 2, H])
        dcol = sb("dcol", [P, 10, H, NDE])
        ctap = sb("ctap", [P, 2, NDE, CC])
        dcv = sb("dcv", [P, KD, NDE])
        gdn_s = sb("gdn_s", [P, 1])
        kq = sb("kq", [P, H, NDE, 2])
        bc8 = sb("bc8", [NDE, 2, H, NDE])
        drow = sb("drow", [H * NDE, 2, P])
        phase1.close()
        plain = ExitStack()
        stP = plain.enter_context(nc.sbuf_tensor("stP", [P, NSTG, UW], F32))
        plain.close()
        moe = ExitStack()
        ctx.push(moe)

        def sb(name, shape, dt=F32):
            return moe.enter_context(nc.sbuf_tensor(name, shape, dt))
        stH = sb("stH", [P, NSTG, UW], F32R)
        XS = sb("XS", [P, KD, 2 * CAP], F32R)
        AS = sb("AS", [P, KD, 2 * CAP], F32R)
        G = sb("G", [P, UW])
        nl = hT[:, :, :].rearrange("p k n -> p (k n)")[:, 0:4 * KD * CAP].rearrange(
            "p (i k n) -> p i k n", i=4, n=CAP)
        Xg = sb("Xg", [CAP, D])
        qflat = qT[:, :, :].rearrange("p k n -> p (k n)")
        yl = qflat[0:CAP, 0:D]
        yb = qflat[0:CAP, D:2 * D]
        cx = sb("cx", [P, NCX])
        wr = sb("wr", [P, KD, E])
        btab = sb("btab", [P, E * 2 * KD])
        bdn = sb("bdn", [E, D])
        r3 = sb("r3", [P, 12, 3, E])
        top8 = sb("top8", [P, 3, 8])
        s3 = sb("s3", [P, 4, 3])
        eb = sb("eb", [P, 6, E])
        ob = sb("ob", [P, 4, OVF])
        obi = sb("obi", [P, OVF + 1], I32)
        rk = sb("rk", [P, 3, NTAB])
        tg = sb("tg", [P, 3, NTAB, 2])
        rowk = sb("rowk", [P, 3, TOPK])
        rowi = sb("rowi", [P, 3, TOPK], I32)
        tabi = sb("tabi", [CAP, NTAB], I32)
        tabg = sb("tabg", [P, NTAB])
        idxc = sb("idxc", [CAP, 1], I32)
        idxw = sb("idxw", [1, 2], I32)
        gcol = sb("gcol", [P, 1])
        bcol = sb("bcol", [P, 2 * KD])
        GT = cg[0:E, :, :, :].rearrange("e a k n -> e (a k n)")[:, 0:NT]
        ss = sb("ss", [P, 3, 1])
        rs = sb("rs", [P, 3, 1])
        ps = ctx.enter_context(nc.psum_tensor("ps", [P, 8, 512], F32))

        def par(name):
            return pv[:, PV[name][0]:PV[name][1]]

        def con(name):
            return cv[:, CV[name][0]:CV[name][1]]

        ident, upper = con("ident"), con("upper")

        def cxc(name):
            return cx[:, CX[name][0]:CX[name][1]]
        wflat = work[:, :, :].rearrange("p a b -> p (a b)")
        qx = wflat[:, 0:4 * (SC - 1 + NPR)].rearrange("p (s n) -> p s n", s=4)
        qc = wflat[:, 1100:1100 + 4 * NT].rearrange("p (s n) -> p s n", s=4)
        sq = wflat[:, 2200:2200 + 4 * NT].rearrange("p (s n) -> p s n", s=4)
        rt = wflat[:, 3300:3300 + 4 * NT].rearrange("p (s n) -> p s n", s=4)
        tmp = wflat[:, 4400:4400 + NDE * SC * 4].rearrange("p (s b j) -> p s b j", s=4, j=SC)
        bA, bI, bM, bMT, bZ, bB0, bB1, bX = (work[:, i, :].rearrange("p (h n) -> p h n", h=H) for i in range(8))
        bB = (bB0, bB1)
        dmask = qT[0:H * NDE, :, :].rearrange("p k n -> p (k n)")[:, 0:4 * 512].rearrange("p (s n) -> p s n", s=4)
        Sd = wflat.rearrange("p (n v) -> p n v", v=P)

        gu_raw = ring[:, :, :, :].rearrange("p s k n -> p (s k n)").rearrange("p (u n) -> p u n", n=UW)
        dn_raw = work[:, :, :].rearrange("p (u a) n -> p u (a n)", a=2)
        raw = lambda i: gu_raw[:, i, :] if i < GU else dn_raw[:, i - GU, :]
        gu_low = ringL[:, :, :, :].rearrange("p s k n -> p (s k n)").rearrange("p (u n) -> p u n", n=UW)
        dn_low = workL[:, :, :].rearrange("p (u a) n -> p u (a n)", a=2)
        low = lambda i: gu_low[:, i, :] if i < GU else dn_low[:, i - GU, :]
        yg = gu_raw.rearrange("p u n -> p (u n)").rearrange("p (t k n) -> p t k n", k=TOPK, n=D)
        facc = work[:, 0:3, :]
        selb = stP[:, 0:2, :].rearrange("p a n -> p (a n)")[:, 0:3 * 7 * CAP].rearrange(
            "p (t e n) -> p t e n", t=3, e=7)
        prod = stP[:, 3, :][:, 0:OVF * E].rearrange("p (b e) -> p b e", b=OVF)
        wsel = stP[:, 4, :][:, 0:OVF * E].rearrange("p (b e) -> p b e", b=OVF)
        rowbuf = [stP[:, a, i * D:(i + 1) * D] for a in (5, 2) for i in range(2)]
        fbt = [G[:, 0:D], G[:, D:2 * D], nl.rearrange("p i k n -> p (i k n)")[:, 0:D]]
        x1t = work[:, 3:6, :]
        g2t = gu_raw.rearrange("p u n -> p (u n)")[:, 12 * D:15 * D].rearrange("p (t n) -> p t n", n=D)
        sqt = stP[:, 2, 0:D]

        in_c, in_pv, in_cv, in_x, in_mix, in_x2, in_sd = (
            sem(n) for n in ("in_c", "in_pv", "in_cv", "in_x", "in_mix", "in_x2", "in_sd"))
        ring_in = [sem(f"ring_in{i}") for i in range(RING)]
        chunk_done = sem("chunk_done")
        chunk_taken = sem("chunk_taken")
        dve_chain, act_chain = sem("dve_chain"), sem("act_chain")
        memset_done = sem("memset_done")
        c_silu = sem("c_silu")
        h_ready = sem("h_ready")
        conv_done = sem("conv_done"); qkv_ready = sem("qkv_ready")
        l2_sq = sem("l2_sq"); l2_ss = sem("l2_ss"); l2_root = sem("l2_root"); l2_done = sem("l2_done")
        logit_done = sem("logit_done"); logit_copy = sem("logit_copy")
        softplus_in = sem("softplus_in"); gate_in = sem("gate_in"); beta_ready = sem("beta_ready")
        g_ready = sem("g_ready"); ug_ready = sem("ug_ready"); gc_done = sem("gc_done"); gc_ready = sem("gc_ready")
        R_done = sem("R_done"); split_ready = sem("split_ready"); decay_exp = sem("decay_exp")
        decay_ready = sem("decay_ready"); small_exp = sem("small_exp"); R_used = sem("R_used")
        kk_done = sem("kk_done"); qk_done = sem("qk_done"); a_ready = sem("a_ready"); intra_ready = sem("intra_ready")
        qe_ready = sem("qe_ready")
        b_ready = sem("b_ready"); z_done = sem("z_done"); z_copied = sem("z_copied")
        m_done = sem("m_done"); mt_upd = sem("mt_upd"); m_upd = sem("m_upd")
        vk_done = sem("vk_done"); vk_ready = sem("vk_ready"); w_done = sem("w_done"); w_ready = sem("w_ready")
        u_done = sem("u_done"); vn_ready = sem("vn_ready"); o_done = sem("o_done"); o_ready = sem("o_ready")
        s_done = sem("s_done"); s_ready = sem("s_ready")
        ug_sig = sem("ug_sig"); u_ready = sem("u_ready"); conf_done = sem("conf_done"); dcv_done = sem("dcv_done")
        out_st = sem("out_st")
        dec_in = sem("dec_in"); dbc_done = sem("dbc_done"); dbc_copy = sem("dbc_copy")
        sk_done = sem("sk_done"); delta_ready = sem("delta_ready"); drow_done = sem("drow_done")
        drow_copy = sem("drow_copy"); dm_ready = sem("dm_ready"); outer_done = sem("outer_done")
        sd_decayed = sem("sd_decayed"); sd_new = sem("sd_new")
        ln_sum = sem("ln_sum"); ln_centred = sem("ln_centred"); ln_sq = sem("ln_sq"); ln_var = sem("ln_var")
        ln_root = sem("ln_root"); ln_norm = sem("ln_norm"); conf_ready = sem("conf_ready")
        og_sq = sem("og_sq"); og_ss = sem("og_ss"); og_root = sem("og_root"); og_ready = sem("og_ready")
        mg_sig = sem("mg_sig"); merged_ready = sem("merged_ready")
        m_sq = sem("m_sq"); m_ss = sem("m_ss"); m_root = sem("m_root")
        x1_ready = sem("x1_ready")
        h2_ready = sem("h2_ready"); gt_spread = sem("gt_spread")

        in_moe = sem("in_moe")
        raw_in = ring_in + [sem(f"raw_in{i}") for i in range(RING, UNITS)]
        RING_END = 16 * NB // RING
        tm_done = sem("tm_done"); tm_copied = sem("tm_copied"); rows_out = [sem(f"rows_out{i}") for i in range(4)]; fb_out = sem("fb_out")
        rl_done = sem("rl_done"); rl_ready = sem("rl_ready"); rl_exp = sem("rl_exp"); sel_ready = sem("sel_ready")
        rank_done = sem("rank_done"); gate_ready = sem("gate_ready"); gt_done = sem("gt_done"); gt_copied = sem("gt_copied")
        hot_ready = sem("hot_ready"); tab_done = sem("tab_done"); tab_ready = sem("tab_ready"); tab_dup = sem("tab_dup")
        novf_ready = sem("novf_ready"); rows_ready = sem("rows_ready"); bias_done = sem("bias_done"); bias_copied = sem("bias_copied")
        block_chain = sem("block_chain"); zero_out = sem("zero_out")
        hi_done = sem("hi_done"); lo_done = sem("lo_done"); unit_used = sem("unit_used")
        ga_copied = sem("ga_copied"); gd_copied = sem("gd_copied"); fold_done = sem("fold_done")
        t1_ready = sem("t1_ready"); sg_ready = sem("sg_ready"); act_ready = sem("act_ready"); ash_ready = sem("ash_ready")
        as_ready = sem("as_ready"); xt_done = sem("xt_done"); xsh_ready = sem("xsh_ready"); xs_ready = sem("xs_ready")
        idx_ready = sem("idx_ready"); xg_in = sem("xg_in"); yl_ready = sem("yl_ready"); y_ready = sem("y_ready"); y_out = sem("y_out")
        all_done = sem("all_done"); tail_in = [sem(f"tail_in{t}") for t in range(3)]; f_ready = sem("f_ready")
        resid_in = sem("resid_in")
        f_sq = sem("f_sq"); out_ready = sem("out_ready")
        TILES = ((0, P), (P, P), (NPR, NDE))

        def overflow(eng, body):
            eng.wait_ge(novf_ready, 1)
            n = eng.value_load(obi[0:1, OVF:OVF + 1], min_val=0, max_val=OVF)
            with eng.Fori(0, OVF) as b:
                with eng.If(b < n):
                    body(b + E, b)
            return n

        def link(eng, chain, ins):
            chain[1] += 1
            ins.then_inc(chain[0], 1)
            eng.wait_ge(chain[0], chain[1])

        bank = lambda b: ps[:, b, :]
        half = lambda b: ps[:, b, :].rearrange("p (h n) -> p h n", h=4)
        two = lambda b: ps[:, b:b + 2, :].rearrange("p b (h n) -> p (b h) n", h=4)
        block = ctx.enter_context(nc.Block())

        @block.sync
        def _(sp):
            sp.dma_start(cT[:, :, :], A["cT"]).then_inc(in_c, 16)
            sp.dma_start(pv[:, :], A["pv"]).then_inc(in_pv, 16)
            sp.dma_start(cv[:, :], A["cv"]).then_inc(in_cv, 16)
            w = {n: A[n].rearrange("(k p) n -> p k n", p=P) for n in ("ada", "in", "pw", "out")}
            for j, (name, c0) in enumerate(BLOCKS):
                if j >= RING:
                    sp.wait_ge(chunk_done, CPB * (j - RING + 1))
                sp.dma_start(ring[:, j % RING, :, :], w[name][:, :, c0:c0 + BW]).then_inc(ring_in[j % RING], 16)
                if j == 0:
                    sp.dma_start(hT[:, :, :], A["xT"]).then_inc(in_x, 16)
                    sp.dma_start(wba[:, :, :], A["wba"]).then_inc(in_mix, 16)
                    sp.dma_start(xD[:, :, :, :], A["qkv_state"]).then_inc(in_mix, 16)
                    sp.dma_start(uD[:, :, :, :], A["glu_state"]).then_inc(in_mix, 16)
                if j == 8:
                    sp.wait_ge(memset_done, 1)
                    sp.dma_start(A["yrows"][E * CAP:, :].rearrange("(n p) d -> p n d", p=P),
                                 S[:, :, :].rearrange("p h n -> p (h n)").unsqueeze(1).to_broadcast([P, OVF * CAP // P, D])
                                 ).then_inc(zero_out, 16)
            sp.wait_ge(s_ready, NC)
            sp.dma_start(wflat, A["sdn"]).then_inc(in_sd, 16)
            sp.dma_start(O["s_prompt"], S[:, :, :]).then_inc(out_st, 16)
            sp.wait_ge(conv_done, NQKV)
            sp.dma_start(O["q_prompt"], q3[:, :, :]).then_inc(out_st, 16)
            sp.dma_start(O["q_sample"], xD[:, :, :, :]).then_inc(out_st, 16)
            sp.wait_ge(u_ready, KD)
            sp.dma_start(O["g_prompt"], uP[:, :, NPR:]).then_inc(out_st, 16)
            sp.dma_start(O["g_sample"], uD[:, :, :, :]).then_inc(out_st, 16)
            sp.wait_ge(sd_new, 16)
            sp.dma_start(O["s_sample"], wflat).then_inc(out_st, 16)
            sp.wait_ge(outer_done, 16)
            sp.dma_start(qT[:, :, :], A["xT"]).then_inc(in_x2, 16)
            wgu = A["gate_up"].rearrange("e (k p) n -> e p k n", p=P)
            wdn = A["down"].rearrange("e (u a p) n -> e p u a n", p=P, a=2)

            def load(e, i):
                if i < GU:
                    src, dst = wgu[e, :, i, :], raw(i)
                else:
                    src, dst = wdn[e, :, i - GU, :, :], work[:, 2 * (i - GU):2 * (i - GU) + 2, :]
                sp.dma_start(dst, src).then_inc(raw_in[i], 16)
            for i in range(GU):
                sp.wait_ge(chunk_done, CPB * (NB - RING + i // 2 + 1))
                load(0, i)
            sp.wait_ge(out_st, 6 * 16)
            sp.dma_start(cx[:, :], A["cx"]).then_inc(in_moe, 16)
            for i in range(GU, UNITS):
                load(0, i)
            sp.wait_ge(h2_ready, 1)
            sp.dma_start(wr[:, :, :], A["wr"]).then_inc(in_moe, 16)
            sp.dma_start(btab[:, :], A["btab"]).then_inc(in_moe, 16)
            sp.dma_start(bdn[:, :], A["bdn"]).then_inc(in_moe, 16)

            def body(blk, e):
                for i in range(UNITS):
                    sp.wait_ge(unit_used, UNITS * blk - UNITS + i + 1)
                    load(e, i)
            with sp.Fori(1, E) as e:
                body(e, e)
            overflow(sp, lambda blk, b: body(blk, sp.value_load(obi[0:1, bass.ds(b, 1)], min_val=0, max_val=E - 1)))
            sp.wait_ge(all_done, 1)
            for t, (t0, m) in enumerate(TILES):
                for dst, src in ((facc, "fbrows"), (g2t, "g2rows"), (x1t, "x1rows")):
                    sp.dma_start(dst[0:m, t, :], A[src][t0:t0 + m, :]).then_inc(resid_in, 16)
            for t, (t0, m) in enumerate(TILES):
                sp.wait_ge(out_ready, t + 1)
                sp.dma_start(O["y"][t0:t0 + m, :], facc[0:m, t, :]).then_inc(out_st, 16)
            sp.wait_ge(out_st, 16 * (6 + len(TILES)))

        @block.tensor
        def _(pe):
            def chunk(n, cols=NT, rhs=None):
                j = n // CPB
                if n % CPB == 0:
                    pe.wait_ge(ring_in[j % RING], 16 * (j // RING + 1))
                if n >= 2:
                    pe.wait_ge(chunk_taken, n - 1)
                rhs = hT if rhs is None else rhs
                for k in range(KD):
                    mm = pe.matmul(ps[:, n % 2, 0:cols], ring[:, j % RING, k, (n % CPB) * P:(n % CPB + 1) * P],
                                   rhs[:, k, 0:cols], start=(k == 0), stop=(k == KD - 1))
                mm.then_inc(chunk_done, 1)

            pe.wait_ge(memset_done, 1)
            pe.wait_ge(m_sq, 1)
            for k in range(KD):
                mm = pe.matmul(ps[:, 2, 0:NT], ones[:, :], qT[:, k, :], start=(k == 0), stop=(k == KD - 1))
            mm.then_inc(m_ss, 1)
            pe.wait_ge(c_silu, 1)
            for n in range(C_ADA1, C_QKV):
                chunk(n, 1 + NDE, cT)
            pe.wait_ge(h_ready, 1)
            pe.wait_ge(in_mix, 3 * 16)
            for t, (t0, m) in enumerate(((0, P), (P, P), (NPR, NDE))):
                for k in range(KD):
                    mm = pe.matmul(ps[0:m, 3, 2 * H * t:2 * H * (t + 1)], hT[:, k, t0:t0 + m], wba[:, k, :],
                                   start=(k == 0), stop=(k == KD - 1))
            mm.then_inc(logit_done, 1)
            for n in range(C_QKV, C_UV):
                chunk(n)
            def l2(i):
                pe.wait_ge(l2_sq, i + 1)
                if i >= 2:
                    pe.wait_ge(l2_root, i - 1)
                pe.matmul(ps[:, 4 + i % 2, 0:NT], ones[:, :], sq[:, i % 4, :], start=True, stop=True).then_inc(l2_ss, 1)
            for n in range(16):
                chunk(C_UV + n)
                l2(n)
            pe.wait_ge(g_ready, 1)
            pe.wait_ge(logit_copy, 1)
            for c in range(NC):
                mm = pe.matmul(ps[:, 3, 64 + H * c:64 + H * (c + 1)], upper, tk[:, 4, c, :], start=True, stop=True)
            mm.then_inc(gc_done, 1)
            filler = list(range(C_GCV, C_GDN))

            def fill(k):
                for _ in range(min(k, len(filler))):
                    n = filler.pop(0)
                    chunk(n, *((1 + NDE, cT) if C_ADA2 <= n else ()))

            for c in range(NC):
                tok = slice(c * CH, (c + 1) * CH)
                if c > 0:
                    pe.wait_ge(s_ready, c)
                    pe.wait_ge(o_ready, c)
                    pe.wait_ge(vn_ready, c)
                else:
                    pe.wait_ge(gc_ready, 1)
                    pe.wait_ge(l2_done, 16)
                pe.wait_ge(ug_ready, c + 1)
                for g in range(2):
                    mm = pe.matmul(bank(2 + g), ones[:, :], bX[:, 4 * g:4 * g + 4, :], start=True, stop=True)
                mm.then_inc(R_done, 1)
                for h in range(H):
                    mm = pe.matmul(two(4)[:, h, :], kT[:, h, tok], kT[:, h, tok], start=True, stop=True)
                mm.then_inc(kk_done, 1)
                for h in range(H):
                    mm = pe.matmul(two(6)[:, h, :], kT[:, h, tok], qT[:, h, tok], start=True, stop=True)
                mm.then_inc(qk_done, 1)
                fill(2)
                for l in range(LEVELS):
                    s = c * LEVELS + l
                    for g in range(2):
                        pe.wait_ge(b_ready, s + 1)
                        if l > 0:
                            pe.wait_ge(mt_upd, 2 * s + g - 1)
                        else:
                            pe.wait_ge(R_used, c + 1)
                        for h in range(4 * g, 4 * g + 4):
                            mm = pe.matmul(half(2 + g)[:, h % 4, :], bB[s % 2][:, h, :],
                                           ident if l == 0 else bMT[:, h, :], start=True, stop=True)
                        mm.then_inc(z_done, 1)
                    if l == 0:
                        fill(1)
                        continue
                    fill(1)
                    for g in range(2):
                        pe.wait_ge(z_copied, 2 * (c * (LEVELS - 1) + l - 1) + g + 1)
                        pe.wait_ge(m_upd, 2 * (s - c) + g - 1)
                        if l == 1:
                            pe.wait_ge(a_ready, c + 1)
                            pe.wait_ge(intra_ready, c + 1)
                        for h in range(4 * g, 4 * g + 4):
                            mm = pe.matmul(half(4 + g)[:, h % 4, :], bM[:, h, :], bZ[:, h, :], start=True, stop=True)
                        if l < LEVELS - 1:
                            for h in range(4 * g, 4 * g + 4):
                                mm = pe.matmul(half(6 + g)[:, h % 4, :], bZ[:, h, :], bM[:, h, :], start=True, stop=True)
                        mm.then_inc(m_done, 1)
                pe.wait_ge(z_copied, 2 * (c + 1) * (LEVELS - 1))
                for h in range(H):
                    pe.transpose(two(2)[:, h, :], vT[:, h, tok], ident)
                pe.wait_ge(mt_upd, 2 * (c + 1) * LEVELS)
                for h in range(H):
                    mm = pe.transpose(two(4)[:, h, :], kT[:, h, tok], ident)
                mm.then_inc(vk_done, 1)
                fill(1)
                pe.wait_ge(vk_ready, c + 1)
                if c > 0:
                    for h in range(H):
                        mm = pe.matmul(two(2)[:, h, :], bB1[:, h, :], bMT[:, h, :], start=True, stop=True)
                    mm.then_inc(w_done, 1)
                    pe.wait_ge(w_ready, c)
                pe.wait_ge(m_upd, 2 * (c + 1) * (LEVELS - 1))
                for h in range(H):
                    mm = pe.matmul(two(6)[:, h, :], bMT[:, h, :], bB0[:, h, :], start=True, stop=(c == 0))
                    if c > 0:
                        mm = pe.matmul(two(6)[:, h, :], bX[:, h, :], S[:, h, :], start=False, stop=True)
                mm.then_inc(u_done, 1)
                fill(1)
                pe.wait_ge(vn_ready, c + 1)
                for h in range(H):
                    mm = pe.matmul(two(4)[:, h, :], bM[:, h, :], bI[:, h, :], start=True, stop=(c == 0))
                    if c > 0:
                        mm = pe.matmul(two(4)[:, h, :], S[:, h, :], qT[:, h, tok], start=False, stop=True)
                mm.then_inc(o_done, 1)
                for h in range(H):
                    mm = pe.matmul(two(2)[:, h, :], bZ[:, h, :], bM[:, h, :], start=True, stop=True)
                mm.then_inc(s_done, 1)
            fill(99)
            pe.wait_ge(s_ready, NC)
            pe.wait_ge(dec_in, 1)
            pe.matmul(ps[:, 2, 0:2 * H * NDE], ones[0:NDE, :], bc8[:, :, :, :].rearrange("p a h b -> p (a h b)"),
                      start=True, stop=True)
            pe.matmul(ps[:, 2, 2 * H * NDE:3 * H * NDE], ones[:, :], dcol[:, 0, :, :].rearrange("p h b -> p (h b)"),
                      start=True, stop=True).then_inc(dbc_done, 1)
            for n in range(C_GDN, C_GDN + 4):
                chunk(n)
            pe.wait_ge(conf_done, KD + 1)
            pe.wait_ge(o_ready, NC)
            for k in range(KD):
                mm = pe.matmul(ps[:, 4, 0:NT], ones[:, :], cvT[:, k, :], start=(k == 0), stop=(k == KD - 1))
            mm.then_inc(ln_sum, 1)
            for n in range(C_GDN + 4, C_PW):
                chunk(n)
            pe.wait_ge(ln_sq, 1)
            for k in range(KD):
                mm = pe.matmul(ps[:, 5, 0:NT], ones[:, :], qT[:, k, :], start=(k == 0), stop=(k == KD - 1))
            mm.then_inc(ln_var, 1)
            pe.wait_ge(in_sd, 16)
            for b in range(NDE):
                for h in range(H):
                    at = 2 * (h * NDE + b)
                    mm = pe.matmul(ps[:, 3, at:at + 2], Sd[:, b * H + h, :], kq[:, h, b, :], start=True, stop=True)
            mm.then_inc(sk_done, 1)
            pe.wait_ge(delta_ready, 1)
            pe.transpose(ps[0:H * NDE, 2, 192:192 + P], dcol[:, 9, :, :].rearrange("p h b -> p (h b)"), ident)
            pe.transpose(ps[0:H * NDE, 2, 320:320 + P], dcol[:, 6, :, :].rearrange("p h b -> p (h b)"), ident
                         ).then_inc(drow_done, 1)
            pe.wait_ge(og_sq, 1)
            pe.wait_ge(vn_ready, NC)
            for h in range(H):
                if h >= 2:
                    pe.wait_ge(og_root, h - 1)
                pe.matmul(ps[:, 6 + h % 2, 0:NT], ones[:, :], kT[:, h, :], start=True, stop=True).then_inc(og_ss, 1)
            pe.wait_ge(drow_copy, 1)
            pe.wait_ge(ln_root, 1)
            for g in range(16):
                pe.wait_ge(dm_ready, g + 1)
                if g >= 2:
                    pe.wait_ge(sd_new, g - 1)
                pe.matmul(bank(4 + g % 2), drow[:, 0, :], dmask[:, g % 4, :], start=True, stop=True
                          ).then_inc(outer_done, 1)
            pe.wait_ge(conf_ready, 1)
            for n in range(C_PW, C_OUT):
                chunk(n, NT, cvT)
            pe.wait_ge(merged_ready, KD)
            for n in range(C_OUT, NB * CPB):
                chunk(n, NT, vT)
            for i in range(2):
                pe.wait_ge(m_sq, i + 2)
                if i == 0:
                    pe.wait_ge(drow_copy, 1)
                for k in range(KD):
                    mm = pe.matmul(ps[:, 2, 0:NT], ones[:, :], gcvT[:, k, :], start=(k == 0), stop=(k == KD - 1))
                mm.then_inc(m_ss, 1)
            pe.wait_ge(h2_ready, 1)
            pe.wait_ge(in_moe, 4 * 16)
            for t, (t0, m) in enumerate(TILES):
                for k in range(KD):
                    mm = pe.matmul(ps[0:m, 3, E * t:E * (t + 1)], hT[:, k, t0:t0 + m], wr[:, k, :],
                                   start=(k == 0), stop=(k == KD - 1))
            mm.then_inc(rl_done, 1)

            def to_rows(n, src, t0, m):
                if n >= 2:
                    pe.wait_ge(tm_copied, n - 1)
                for k in range(KD):
                    tr = pe.transpose(ps[0:m, 4 + 2 * (n % 2) + k // 4, (k % 4) * P:(k % 4 + 1) * P], src[:, k, t0:t0 + m], ident)
                tr.then_inc(tm_done, 1)
            n = 0
            for src in (hT, qT):
                for t0, m in TILES:
                    to_rows(n, src, t0, m)
                    n += 1
            pe.wait_ge(gt_spread, 1)
            for t0, m in TILES:
                to_rows(n, hT, t0, m)
                n += 1
            pe.wait_ge(sel_ready, 1)
            pe.wait_ge(in_moe, 4 * 16)
            for t in range(3):
                for u in range(t + 1):
                    pe.matmul(ps[:, 2, E * t:E * (t + 1)], cxc("strict_upper") if u == t else ones[:, :], r3[:, 3, u, :],
                              start=(u == 0), stop=(u == t))
            for u in range(3):
                mm = pe.matmul(ps[:, 2, 3 * E:4 * E], ones[:, :], r3[:, 3, u, :], start=(u == 0), stop=(u == 2))
            mm.then_inc(rank_done, 1)
            for g in range(NTAB // 7):
                for t, (t0, m) in enumerate(TILES):
                    pe.wait_ge(hot_ready, 3 * g + t + 1)
                for e in range(7):
                    for t, (t0, m) in enumerate(TILES):
                        mm = pe.matmul(ps[0:CAP, 3, 2 * (7 * g + e):2 * (7 * g + e) + 2], selb[0:m, t, e, :],
                                       tg[0:m, t, 7 * g + e, :], start=(t == 0), stop=(t == 2))
                mm.then_inc(tab_done, 1)
            pe.wait_ge(gate_ready, 1)
            pe.wait_ge(tm_copied, 9)
            for t, (t0, m) in enumerate(TILES):
                mm = pe.transpose(ps[0:E, 4, t0:t0 + m], r3[0:m, 5, t, :], ident[0:m, 0:m])
            mm.then_inc(gt_done, 1)

            def rows_in(blk):
                pe.wait_ge(xg_in, 16 * blk + 16)
                for k in range(KD):
                    tr = pe.matmul(ps[:, 0, CAP * k:CAP * (k + 1)], Xg[:, k * P:(k + 1) * P], ident[0:CAP, 0:CAP],
                                   start=True, stop=True)
                tr.then_inc(xt_done, 1)

            def body(blk, e):
                first = isinstance(blk, int)
                pe.wait_ge(xs_ready, blk + 1)
                if not first:
                    pe.wait_ge(gd_copied, blk)
                    pe.wait_ge(ga_copied, blk)
                for i in range(GU):
                    pe.wait_ge(lo_done, UNITS * blk + i + 1)
                    for n in range(4):
                        for a, part in enumerate((stH[:, i % NSTG, :], low(i))):
                            mm = pe.matmul(bank(n), XS[:, i, :], part[:, n * 512:(n + 1) * 512],
                                           start=(i == 0 and a == 0), stop=(i == GU - 1 and a == 1))
                    mm.then_inc(unit_used, 1)
                pe.wait_ge(ga_copied, blk + 1)
                if not first:
                    pe.wait_ge(act_ready, blk)
                for m in range(2 * KD):
                    if m == KD:
                        pe.wait_ge(gd_copied, blk + 1)
                    mm = pe.matmul(ps[:, 6 + m // KD, CAP * (m % KD):CAP * (m % KD + 1)], G[:, m * P:(m + 1) * P],
                                   cxc("fold"), start=True, stop=True)
                    if m % KD == KD - 1:
                        mm.then_inc(fold_done, 1)
                rows_in(blk + 1)
                pe.wait_ge(as_ready, blk + 1)
                if not first:
                    pe.wait_ge(y_ready, blk)
                for i in range(GU, UNITS):
                    pe.wait_ge(lo_done, UNITS * blk + i + 1)
                    for a in range(2):
                        for n in range(2):
                            for b, part in enumerate((stH[:, i % NSTG, :], low(i))):
                                mm = pe.matmul(bank(4 + n), AS[:, 2 * (i - GU) + a, :],
                                               part[:, a * D + n * 512:a * D + (n + 1) * 512],
                                               start=(i == GU and a == 0 and b == 0),
                                               stop=(i == UNITS - 1 and a == 1 and b == 1))
                    mm.then_inc(unit_used, 1)
            rows_in(0)
            pe.wait_ge(gt_copied, 1)
            pe.wait_ge(in_moe, 4 * 16)
            for t, (t0, m) in enumerate(TILES):
                if t > 0:
                    pe.wait_ge(bias_copied, t)
                for n in range(2):
                    mm = pe.matmul(ps[0:m, 4 + n, :], GT[:, t0:t0 + m], bdn[:, n * 512:(n + 1) * 512], start=True, stop=True)
                mm.then_inc(bias_done, 1)
            pe.wait_ge(bias_copied, 3)
            body(0, 0)
            with pe.Fori(1, E) as e:
                body(e, e)
            overflow(pe, body)

        @block.scalar
        def _(act):
            chain = [act_chain, 0]

            def take(n):
                act.wait_ge(chunk_done, n + 1)

            act.wait_ge(in_c, 16)
            act.activation(cT[:, :, :], cT[:, :, :], ACT.Silu).then_inc(c_silu, 1)
            act.wait_ge(in_pv, 16)
            for n in range(C_ADA1, C_QKV):
                take(n)
                act.activation(adaT[:, n // KD, n % KD, :], ps[:, n % 2, 0:1 + NDE], ACT.Identity,
                               bias=par("b_ada")[:, n:n + 1]).then_inc(chunk_taken, 1)
            act.wait_ge(m_ss, 1)
            act.wait_ge(in_cv, 16)
            act.activation(row[:, 0, :], ps[:, 2, 0:NT], ACT.Sqrt, bias=con("eps")[:, 0:1]).then_inc(m_root, 1)
            act.wait_ge(logit_done, 1)
            act.wait_ge(memset_done, 1)
            act.activation(ba[:, 0:2, :], ps[:, 3, 0:4 * H].rearrange("p (t n) -> p t n", t=2), ACT.Copy)
            act.activation(ba[0:NDE, 2, :], ps[0:NDE, 3, 4 * H:6 * H], ACT.Copy).then_inc(logit_copy, 1)
            act.wait_ge(in_mix, 3 * 16)

            def silu_qkv(m):
                act.wait_ge(conv_done, m + 1)
                act.activation((qT, kT, vT)[m // KD][:, m % KD, :], qc[:, m % 4, :], ACT.Silu).then_inc(qkv_ready, 1)
            for m in range(NQKV):
                n = C_QKV + m
                take(n)
                if m >= 4:
                    act.wait_ge(conv_done, m - 3)
                act.activation(qx[:, m % 4, SC - 1:], ps[:, n % 2, 0:NPR], ACT.Copy)
                act.activation(xD[:, m, :, SC - 1], ps[:, n % 2, NPR:NT], ACT.Copy).then_inc(chunk_taken, 1)
                if m >= 1:
                    silu_qkv(m - 1)
            silu_qkv(NQKV - 1)
            for n in range(C_Z, C_UV):
                take(n)
                act.activation(zT[:, n - C_Z, :], ps[:, n % 2, 0:NT], ACT.Silu).then_inc(chunk_taken, 1)
            act.wait_ge(in_mix, 3 * 16)

            def l2_square(i):
                act.wait_ge(qkv_ready, i + 1)
                if i >= 4:
                    act.wait_ge(l2_ss, i - 3)
                act.activation(sq[:, i % 4, :], (qT, kT)[i // KD][:, i % KD, :], ACT.Square).then_inc(l2_sq, 1)

            def l2_sqrt(i):
                act.wait_ge(l2_ss, i + 1)
                if i >= 4:
                    act.wait_ge(l2_done, i - 3)
                act.activation(rt[:, i % 4, :], ps[:, 4 + i % 2, 0:NT], ACT.Sqrt,
                               bias=con("eps")[:, 1:2]).then_inc(l2_root, 1)
            l2_square(0)
            for i in range(16):
                n = C_UV + i
                take(n)
                if i < KD:
                    act.activation(uP[:, i, CC - 1:], ps[:, n % 2, 0:NPR], ACT.Copy)
                    act.activation(uD[:, i, :, CC - 1], ps[:, n % 2, NPR:NT], ACT.Copy).then_inc(chunk_taken, 1)
                else:
                    act.activation(gdnT[:, i - KD, :], ps[:, n % 2, 0:NT], ACT.Copy).then_inc(chunk_taken, 1)
                if i < 15:
                    l2_square(i + 1)
                l2_sqrt(i)
            act.wait_ge(chunk_taken, C_GCV)
            for i in range(KD):
                act.activation(gdnT[:, i, :], gdnT[:, i, :], ACT.Sigmoid).then_inc(ug_sig, 1)
            act.wait_ge(logit_copy, 1)
            act.activation(tk[:, 0, :, :], ba[:, :, 0:H], ACT.Sigmoid).then_inc(beta_ready, 1)
            act.wait_ge(softplus_in, 1)
            link(act, chain, act.activation(tk[:, 2, :, :], tk[:, 2, :, :], ACT.Exp, scale=-1.0))
            act.activation(tk[:, 3, 0, :], par("a_log"), ACT.Exp)
            act.activation(tk[:, 2, :, :], tk[:, 2, :, :], ACT.Ln, bias=ones[:, 0:1]).then_inc(gate_in, 1)
            fillers = list(range(C_GCV, C_GDN))

            def fill(k):
                for _ in range(min(k, len(fillers))):
                    n = fillers.pop(0)
                    take(n)
                    if n < C_ADA2:
                        act.activation(gcvT[:, n - C_GCV, :], ps[:, n % 2, 0:NT], ACT.Copy).then_inc(chunk_taken, 1)
                    else:
                        a = n - C_ADA2 + 16
                        act.activation(adaT[:, a // KD, a % KD, :], ps[:, n % 2, 0:1 + NDE], ACT.Identity,
                                       bias=par("b_ada")[:, a:a + 1]).then_inc(chunk_taken, 1)

            for c in range(NC):
                tok = slice(c * CH, (c + 1) * CH)
                if c == 0:
                    act.wait_ge(gc_ready, 1)
                act.wait_ge(split_ready, c + 1)
                act.activation(bA[:, :, :], bA[:, :, :], ACT.Exp, scale=-1.0).then_inc(decay_exp, 1)
                act.activation(bI[:, :, :], bI[:, :, :], ACT.Exp).then_inc(decay_exp, 1)
                act.wait_ge(R_done, c + 1)
                act.activation(gl[:, 0, :], two(2)[:, :, CH - 1], ACT.Exp)
                act.activation(tk[:, 7, c, :], tk[:, 5, c, :], ACT.Exp)
                act.activation(tk[:, 8, c, :], bX[:, :, CH - 1], ACT.Exp).then_inc(small_exp, 1)
                if c > 0:
                    act.wait_ge(decay_exp, 4)
                    act.activation(bZ[:, :, :], two(2), ACT.Exp).then_inc(R_used, 1)
                else:
                    act.activation(gl[:, 1, :], two(2)[:, :, CH - 1], ACT.Copy).then_inc(R_used, 1)
                fill(2)
                for l in range(LEVELS):
                    if l == 0:
                        fill(1)
                        continue
                    fill(0)
                    for g in range(2):
                        act.wait_ge(z_done, 2 * (c * LEVELS + l) + g + 1)
                        if l == 1 and c > 0:
                            act.wait_ge(qe_ready, c)
                        if l > 1:
                            act.wait_ge(m_done, 2 * (c * (LEVELS - 1) + l - 2) + g + 1)
                        act.activation(bZ[:, 4 * g:4 * g + 4, :], half(2 + g), ACT.Copy).then_inc(z_copied, 1)
                    fill(1)
                fill(1)
                if c > 0:
                    act.wait_ge(w_done, c)
                    act.activation(bX[:, :, :], two(2), ACT.Copy, scale=-1.0).then_inc(w_ready, 1)
                act.wait_ge(u_done, c + 1)
                act.activation(bM[:, :, :], two(6), ACT.Copy).then_inc(vn_ready, 1)
                fill(1)
                act.wait_ge(o_done, c + 1)
                act.activation(vT[:, :, tok], two(4), ACT.Copy).then_inc(o_ready, 1)
            fill(99)
            d2 = lambda i: dcol[:, i, :, :].rearrange("p h b -> p (h b)")
            act.wait_ge(dbc_done, 1)
            act.activation(d2(1), ps[:, 2, 0:64], ACT.Exp)
            act.activation(dcol[:, 2:4, :, :].rearrange("p a h b -> p (a h b)"), ps[:, 2, 64:192], ACT.Copy
                           ).then_inc(dbc_copy, 1)
            for n in range(C_GDN, C_PW):
                take(n)
                if n == C_GDN:
                    act.wait_ge(u_ready, KD)
                act.activation(gdnT[:, n - C_GDN, :], ps[:, n % 2, 0:NT], ACT.Copy).then_inc(chunk_taken, 1)
            act.wait_ge(chunk_taken, C_PW)
            act.activation(gdnT[:, :, :], gdnT[:, :, :], ACT.Sigmoid).then_inc(mg_sig, 1)
            act.activation(gcvT[:, :, :], gcvT[:, :, :], ACT.Sigmoid).then_inc(mg_sig, 1)
            act.wait_ge(ln_centred, 1)
            act.wait_ge(o_done, NC)
            act.activation(qT[:, :, :], cvT[:, :, :], ACT.Square).then_inc(ln_sq, 1)
            act.wait_ge(ln_var, 1)
            act.activation(row[:, 0, :], ps[:, 5, 0:NT], ACT.Sqrt, scale=1.0 / D, bias=con("eps")[:, 3:4]
                           ).then_inc(ln_root, 1)
            act.wait_ge(drow_done, 1)
            act.activation(drow[:, :, :], ps[0:H * NDE, 2, 192:448].rearrange("p (a n) -> p a n", a=2), ACT.Copy
                           ).then_inc(drow_copy, 1)
            act.wait_ge(delta_ready, 2)
            act.activation(kT[:, :, :], vT[:, :, :], ACT.Square).then_inc(og_sq, 1)
            for h in range(H):
                act.wait_ge(og_ss, h + 1)
                act.activation(kT[:, h, :], ps[:, 6 + h % 2, 0:NT], ACT.Sqrt, bias=con("eps")[:, 2:3]).then_inc(og_root, 1)
            act.wait_ge(ln_norm, 1)
            for k in range(KD):
                ins = act.activation(cvT[:, k, :], cvT[:, k, :], ACT.Silu, scale=par("g_ln")[:, k:k + 1],
                                     bias=par("b_ln")[:, k:k + 1])
            ins.then_inc(conf_ready, 1)
            act.wait_ge(og_ready, 1)
            for n in range(C_PW, C_OUT):
                take(n)
                act.activation(zT[:, n - C_PW, :], ps[:, n % 2, 0:NT], ACT.Identity,
                               bias=par("b_pw")[:, n - C_PW:n - C_PW + 1]).then_inc(chunk_taken, 1)
            for n in range(C_OUT, NB * CPB):
                take(n)
                act.activation(kT[:, n - C_OUT, :], ps[:, n % 2, 0:NT], ACT.Copy).then_inc(chunk_taken, 1)
            act.wait_ge(chunk_taken, NB * CPB)
            act.activation(gcvT[:, :, :], kT[:, :, :], ACT.Square).then_inc(m_sq, 1)
            act.wait_ge(m_ss, 2)
            act.activation(row[:, 0, :], ps[:, 2, 0:NT], ACT.Sqrt, bias=con("eps")[:, 0:1]).then_inc(m_root, 1)
            act.wait_ge(x1_ready, 1)
            act.activation(gcvT[:, :, :], qT[:, :, :], ACT.Square).then_inc(m_sq, 1)
            act.wait_ge(m_ss, 3)
            act.activation(row[:, 0, :], ps[:, 2, 0:NT], ACT.Sqrt, bias=con("eps")[:, 0:1]).then_inc(m_root, 1)
            act.wait_ge(h2_ready, 1)
            for n in range(9):
                t0, m = TILES[n % 3]
                act.wait_ge(tm_done, n + 1)
                dst = rowbuf[n % 4][0:m, :]
                if n >= 4:
                    act.wait_ge(rows_out[n % 4], 16 * (n // 4))
                b0 = 4 + 2 * (n % 2)
                act.activation(dst, ps[0:m, b0:b0 + 2, :].rearrange("p b n -> p (b n)"), ACT.Copy).then_inc(tm_copied, 1)
                act.wait_ge(tm_copied, n + 1)
                act.dma_start((A["h2rows"], A["x1rows"], A["g2rows"])[n // 3][t0:t0 + m, :], dst).then_inc(rows_out[n % 4], 16)
                if n == 4:
                    act.wait_ge(rl_ready, 1)
                    act.activation(r3[:, 4, :, :], r3[:, 4, :, :], ACT.Exp).then_inc(rl_exp, 1)
            act.wait_ge(tab_ready, 1)
            act.activation(tabg[CAP:2 * CAP, :], tabg[0:CAP, :], ACT.Copy).then_inc(tab_dup, 1)
            act.wait_ge(gt_done, 1)
            act.activation(GT[:, :], ps[0:E, 4, 0:NT], ACT.Copy).then_inc(gt_copied, 1)

            def hi(blk, i):
                act.wait_ge(raw_in[i], 16 * blk + 16 + (RING_END if i < RING else 0))
                if not (isinstance(blk, int) and i < NSTG):
                    act.wait_ge(unit_used, UNITS * blk + i - NSTG + 1)
                act.activation(stH[:, i % NSTG, :], raw(i), ACT.Copy).then_inc(hi_done, 1)

            def rows_hi(blk):
                act.wait_ge(xt_done, blk + 1)
                act.activation(XS[:, :, 0:CAP], ps[:, 0, :].rearrange("p (k n) -> p k n", k=KD), ACT.Copy).then_inc(xsh_ready, 1)

            def rows_of(blk):
                act.wait_ge(unit_used, UNITS * blk + UNITS)
                act.activation(yl[:, :], ps[CAP:2 * CAP, 4:6, :].rearrange("p b n -> p (b n)"), ACT.Copy,
                               scale=gcol[CAP:2 * CAP, 0:1]).then_inc(yl_ready, 1)

            def body(blk, e):
                for i in range(GU + 1):
                    hi(blk, i)
                    if i == NSTG - 1 and not isinstance(blk, int):
                        rows_of(blk - 1)
                act.wait_ge(unit_used, UNITS * blk + GU)
                if isinstance(blk, int):
                    act.wait_ge(fb_out, 48)
                act.activation(G[:, 0:D], ps[:, 0:2, :].rearrange("p b n -> p (b n)"), ACT.Copy).then_inc(ga_copied, 1)
                hi(blk, GU + 1)
                act.wait_ge(t1_ready, blk + 1)
                act.activation(nl[:, 3, :, :], nl[:, 0, :, :], ACT.Sigmoid, scale=ALPHA).then_inc(sg_ready, 1)
                hi(blk, GU + 2)
                act.wait_ge(act_ready, blk + 1)
                act.activation(AS[:, :, 0:CAP], nl[:, 2, :, :], ACT.Copy).then_inc(ash_ready, 1)
                rows_hi(blk + 1)
                hi(blk, GU + 3)
            rows_hi(0)
            for t, (t0, m) in enumerate(TILES):
                act.wait_ge(bias_copied, t + 1)
                act.dma_start(A["fbrows"][t0:t0 + m, :], fbt[t][0:m, :]).then_inc(fb_out, 16)
            for i in range(4):
                act.wait_ge(rows_out[i], 16 * (3 if i == 0 else 2))
            act.wait_ge(tab_dup, 1)
            body(0, 0)
            with act.Fori(1, E) as e:
                body(e, e)
            n = overflow(act, body)
            rows_of(n + (E - 1))
            for t, (t0, m) in enumerate(TILES):
                act.wait_ge(f_ready, t + 1)
                act.activation(sqt[0:m, :], facc[0:m, t, :], ACT.Square, accum_out=ss[0:m, t, :]).then_inc(f_sq, 1)
                act.wait_ge(f_sq, 2 * t + 1)
                act.activation(rs[0:m, t, :], ss[0:m, t, :], ACT.Sqrt, bias=con("eps")[0:m, 0:1]).then_inc(f_sq, 1)

        @block.vector
        def _(dve):
            chain = [dve_chain, 0]
            lk = lambda ins: link(dve, chain, ins)
            dve.wait_ge(in_pv, 16)
            dve.wait_ge(chunk_taken, C_QKV)
            lk(dve.scalar_tensor_tensor(out=cg[:, 0, :, :], in0=adaT[:, 1, :, :], scalar=1.0,
                                        in1=par("g_pre_mix").unsqueeze(2).to_broadcast([P, KD, 1 + NDE]),
                                        op0=ALU.add, op1=ALU.mult))
            lk(dve.tensor_scalar(cg[:, 0, :, :], cg[:, 0, :, :], float(D) ** 0.5, None, ALU.mult))
            dve.wait_ge(m_root, 1)
            lk(dve.reciprocal(row[:, 1, :], row[:, 0, :]))
            dve.wait_ge(in_x, 16)
            dve.wait_ge(m_sq, 1)

            def modulate(dst, coef, shift):
                lk(dve.tensor_tensor(dst[:, :, :], dst[:, :, :], row[:, 1:2, :].to_broadcast([P, KD, NT]), ALU.mult))
                lk(dve.tensor_tensor(dst[:, :, NPR:NT], dst[:, :, NPR:NT], coef[:, :, 1:], ALU.mult))
                lk(dve.tensor_tensor(dst[:, :, NPR:NT], dst[:, :, NPR:NT], shift[:, :, 1:], ALU.add))
                for k in range(KD):
                    ins = dve.tensor_scalar(dst[:, k, 0:NPR], dst[:, k, 0:NPR], coef[:, k, 0:1], shift[:, k, 0:1],
                                            ALU.mult, ALU.add)
                return ins
            modulate(hT, cg[:, 0, :, :], adaT[:, 0, :, :]).then_inc(h_ready, 1)
            dve.wait_ge(h_ready, 1)

            dve.wait_ge(in_mix, 3 * 16)
            dve.wait_ge(memset_done, 1)
            wq = par("w_qkv_conv").rearrange("p (m j) -> p m j", j=SC)
            for m in range(NQKV):
                n = C_QKV + m
                dve.wait_ge(chunk_taken, n + 1)
                if m >= 4:
                    dve.wait_ge(qkv_ready, m - 3)
                s = m % 4
                out = qc[:, s, 0:NPR]
                dve.tensor_tensor(tmp[:, s, :, :], xD[:, m, :, :], wq[:, m:m + 1, :].to_broadcast([P, NDE, SC]), ALU.mult)
                dve.tensor_copy(q3[:, m, :], qx[:, s, NPR:NPR + SC - 1])
                lk(dve.tensor_scalar(out, qx[:, s, 0:NPR], wq[:, m, 0:1], None, ALU.mult))
                for j in range(1, SC):
                    lk(dve.scalar_tensor_tensor(out=out, in0=qx[:, s, j:j + NPR], scalar=wq[:, m, j:j + 1], in1=out,
                                                op0=ALU.mult, op1=ALU.add))
                dve.tensor_reduce(qc[:, s, NPR:NT], tmp[:, s, :, :], AX.X, ALU.add).then_inc(conv_done, 1)
            dve.wait_ge(logit_copy, 1)
            dt3 = par("dt_bias").unsqueeze(1).to_broadcast([P, 3, H])
            lk(dve.tensor_tensor(tk[:, 1, :, :], ba[:, :, H:2 * H], dt3, ALU.add))
            lk(dve.tensor_scalar(tk[:, 2, :, :], tk[:, 1, :, :], -1.0, None, ALU.mult))
            dve.tensor_tensor(tk[:, 2, :, :], tk[:, 1, :, :], tk[:, 2, :, :], ALU.max).then_inc(softplus_in, 1)
            for i in range(16):
                dve.wait_ge(l2_root, i + 1)
                lk(dve.reciprocal(rt[:, i % 4, :], rt[:, i % 4, :]))
                t = (qT, kT)[i // KD][:, i % KD, :]
                dve.scalar_tensor_tensor(out=t, in0=t, scalar=float(P) ** -0.5 if i < KD else 1.0, in1=rt[:, i % 4, :],
                                         op0=ALU.mult, op1=ALU.mult).then_inc(l2_done, 1)
            dve.wait_ge(gate_in, 1)
            lk(dve.scalar_tensor_tensor(out=tk[:, 4, :, :], in0=tk[:, 1, :, :], scalar=0.0, in1=tk[:, 2, :, :],
                                        op0=ALU.max, op1=ALU.add))
            dve.scalar_tensor_tensor(out=tk[:, 4, :, :], in0=tk[:, 4, :, :], scalar=-1.0,
                                     in1=tk[:, 3, 0:1, :].to_broadcast([P, 3, H]),
                                     op0=ALU.mult, op1=ALU.mult).then_inc(g_ready, 1)
            for i in range(KD):
                dve.wait_ge(ug_sig, i + 1)
                dve.tensor_tensor(uP[:, i, CC - 1:], uP[:, i, CC - 1:], gdnT[:, i, 0:NPR], ALU.mult)
                dve.tensor_tensor(uD[:, i, :, CC - 1], uD[:, i, :, CC - 1], gdnT[:, i, NPR:NT], ALU.mult).then_inc(u_ready, 1)
            wd = par("w_dw").rearrange("p (k j) -> p k j", j=CC)
            taps = [(k, j) for k in range(KD) for j in range(CC)]

            def conf_conv(n):
                for _ in range(min(n, len(taps))):
                    k, j = taps.pop(0)
                    out, src = cvT[:, k, 0:NPR], uP[:, k, j:j + NPR]
                    if j == 0:
                        dve.wait_ge(u_ready, k + 1)
                        lk(dve.tensor_scalar(out, src, wd[:, k, 0:1], par("b_dw")[:, k:k + 1], ALU.mult, ALU.add))
                    else:
                        ins = dve.scalar_tensor_tensor(out=out, in0=src, scalar=wd[:, k, j:j + 1], in1=out,
                                                       op0=ALU.mult, op1=ALU.add)
                        if j == CC - 1:
                            ins.then_inc(conf_done, 1)
                        else:
                            lk(ins)
            dve.wait_ge(g_ready, 1)
            dve.wait_ge(l2_done, 16)
            for i, src in ((0, kT), (1, qT)):
                dve.tensor_copy(kq[:, :, :, i], src[:, :, NPR:NT])
            dve.tensor_copy(dcol[:, 9, :, :], kT[:, :, NPR:NT])
            dve.tensor_tensor(dcol[:, 0, :, :], kT[:, :, NPR:NT], qT[:, :, NPR:NT], ALU.mult)
            dve.wait_ge(beta_ready, 1)
            for i, src in ((0, 4), (1, 0)):
                ins = dve.tensor_tensor(bc8[:, i, :, :], ident[0:NDE, 0:NDE].unsqueeze(1).to_broadcast([NDE, H, NDE]),
                                        tk[0:NDE, src, 2, :].unsqueeze(2).to_broadcast([NDE, H, NDE]), ALU.mult)
            ins.then_inc(dec_in, 1)
            dve.wait_ge(gc_done, 1)
            dve.tensor_copy(tk[:, 5, 0:2, :], ps[:, 3, 64:64 + 2 * H].rearrange("p (c h) -> p c h", c=2)).then_inc(gc_ready, 1)
            dve.wait_ge(gc_ready, 1)
            dve.wait_ge(beta_ready, 1)

            for c in range(NC):
                tok = slice(c * CH, (c + 1) * CH)
                if c > 0:
                    dve.wait_ge(u_done, c)
                    dve.wait_ge(o_done, c)
                    dve.wait_ge(s_done, c)
                dve.tensor_tensor(bX[:, :, :], upper.unsqueeze(1).to_broadcast([P, H, P]),
                                  tk[:, 4, c, :].unsqueeze(2).to_broadcast([P, H, P]), ALU.mult).then_inc(ug_ready, 1)
                dve.wait_ge(R_done, c + 1)
                gcb = tk[:, 5, c, :].unsqueeze(2).to_broadcast([P, H, P])
                lk(dve.tensor_tensor(bX[:, :, :], two(2), gcb, ALU.subtract))
                lk(dve.tensor_scalar(bA[:, :, :], bX[:, :, :], 0.0, None, ALU.max))
                dve.tensor_tensor(bI[:, :, :], bX[:, :, :], bA[:, :, :], ALU.subtract).then_inc(split_ready, 1)
                dve.wait_ge(kk_done, c + 1)
                dve.wait_ge(decay_exp, 2 * c + 1)
                for h in range(H):
                    ins = dve.scalar_tensor_tensor(out=bA[:, h, :], in0=two(4)[:, h, :], scalar=tk[:, 0, c, h:h + 1],
                                                   in1=bA[:, h, :], op0=ALU.mult, op1=ALU.mult)
                ins.then_inc(a_ready, 1)
                dve.wait_ge(decay_ready, c + 1)
                dve.wait_ge(qk_done, c + 1)
                dve.tensor_tensor(bI[:, :, :], two(6), bI[:, :, :], ALU.mult).then_inc(intra_ready, 1)
                if c > 0:
                    dve.wait_ge(R_used, c + 1)
                    dve.tensor_tensor(qT[:, :, tok], qT[:, :, tok], bZ[:, :, :], ALU.mult).then_inc(qe_ready, 1)
                for l in range(LEVELS):
                    s = c * LEVELS + l
                    conf_conv(16)
                    for g in range(2):
                        hs = slice(4 * g, 4 * g + 4)
                        idb = ident.unsqueeze(1).to_broadcast([P, 4, P])
                        if l == 0:
                            dve.wait_ge(z_done, 2 * s + g + 1)
                            dve.tensor_tensor(bMT[:, hs, :], idb, half(2 + g), ALU.subtract).then_inc(mt_upd, 1)
                            dve.tensor_tensor(bM[:, hs, :], idb, bB[s % 2][:, hs, :], ALU.subtract).then_inc(m_upd, 1)
                        else:
                            dve.wait_ge(m_done, 2 * (c * (LEVELS - 1) + l - 1) + g + 1)
                            dve.wait_ge(mt_upd, 2 * s + g - 1)
                            dve.tensor_tensor(bMT[:, hs, :], bMT[:, hs, :], half(4 + g), ALU.subtract).then_inc(mt_upd, 1)
                            if l < LEVELS - 1:
                                dve.wait_ge(m_upd, 2 * (s - c) + g - 1)
                                dve.tensor_tensor(bM[:, hs, :], bM[:, hs, :], half(6 + g), ALU.subtract).then_inc(m_upd, 1)
                dve.wait_ge(small_exp, c + 1)
                lk(dve.tensor_tensor(tk[:, 9, c, :], tk[:, 7, c, :], tk[:, 0, c, :], ALU.mult))
                dve.wait_ge(vk_done, c + 1)
                sc = lambda i: tk[:, i, c, :].unsqueeze(2).to_broadcast([P, H, P])
                dve.tensor_tensor(bB0[:, :, :], two(2), sc(0), ALU.mult)
                dve.tensor_tensor(bZ[:, :, :], two(4), sc(8), ALU.mult)
                dve.tensor_tensor(bB1[:, :, :], two(4), sc(9), ALU.mult).then_inc(vk_ready, 1)
                dve.wait_ge(s_done, c + 1)
                if c == 0:
                    dve.wait_ge(zero_out, 16)
                    dve.tensor_copy(S[:, :, :], two(2)).then_inc(s_ready, 1)
                else:
                    dve.wait_ge(s_ready, c)
                    for h in range(H):
                        ins = dve.scalar_tensor_tensor(out=S[:, h, :], in0=S[:, h, :], scalar=gl[:, 0, h:h + 1],
                                                       in1=two(2)[:, h, :], op0=ALU.mult, op1=ALU.add)
                    ins.then_inc(s_ready, 1)
            conf_conv(len(taps))
            for k in range(KD):
                dve.wait_ge(u_ready, k + 1)
                lk(dve.tensor_tensor(ctap[:, k % 2, :, :], uD[:, k, :, :], wd[:, k:k + 1, :].to_broadcast([P, NDE, CC]), ALU.mult))
                dve.tensor_reduce(dcv[:, k, :], ctap[:, k % 2, :, :], AX.X, ALU.add).then_inc(dcv_done, 1)
            dve.wait_ge(dcv_done, KD)
            dve.tensor_tensor(cvT[:, :, NPR:NT], dcv[:, :, :], par("b_dw").unsqueeze(2).to_broadcast([P, KD, NDE]),
                              ALU.add).then_inc(conf_done, 1)
            dve.wait_ge(ln_sum, 1)
            lk(dve.tensor_scalar(row[:, 1, :], ps[:, 4, 0:NT], 1.0 / D, None, ALU.mult))
            allrow = row[:, 1:2, :].to_broadcast([P, KD, NT])
            dve.tensor_tensor(cvT[:, :, :], cvT[:, :, :], allrow, ALU.subtract).then_inc(ln_centred, 1)
            dve.wait_ge(sk_done, 1)
            dve.wait_ge(dbc_copy, 1)
            dv = vT[:, :, NPR:NT]
            sk = ps[:, 3, 0:2 * H * NDE].rearrange("p (h b a) -> p h b a", h=H, a=2)
            d = lambda i: dcol[:, i, :, :]
            lk(dve.tensor_tensor(d(4), sk[:, :, :, 0], d(1), ALU.mult))
            dve.tensor_tensor(d(7), sk[:, :, :, 1], d(1), ALU.mult)
            lk(dve.tensor_tensor(d(5), dv, d(4), ALU.subtract))
            dve.tensor_tensor(d(6), d(5), d(2), ALU.mult).then_inc(delta_ready, 1)
            dve.wait_ge(delta_ready, 1)
            lk(dve.tensor_tensor(d(8), d(6), d(3), ALU.mult))
            dve.tensor_tensor(dv, d(7), d(8), ALU.add).then_inc(delta_ready, 1)
            dve.wait_ge(ln_root, 1)
            lk(dve.reciprocal(row[:, 1, :], row[:, 0, :]))
            dve.tensor_tensor(cvT[:, :, :], cvT[:, :, :], allrow, ALU.mult).then_inc(ln_norm, 1)
            for g in range(16):
                dve.wait_ge(outer_done, g + 1)
                dve.wait_ge(sd_decayed, g + 1)
                sg = Sd[:, 4 * g:4 * g + 4, :]
                dve.tensor_tensor(sg, sg, half(4 + g % 2), ALU.add).then_inc(sd_new, 1)
            lk(dve.tensor_scalar(gdn_s[:, :], par("g_dn"), float(P) ** 0.5, None, ALU.mult))
            dve.wait_ge(og_root, H)
            dve.wait_ge(mg_sig, 2)
            lk(dve.reciprocal(kT[:, :, :], kT[:, :, :]))
            lk(dve.scalar_tensor_tensor(out=vT[:, :, :], in0=vT[:, :, :], scalar=gdn_s[:, 0:1], in1=kT[:, :, :],
                                        op0=ALU.mult, op1=ALU.mult))
            lk(dve.tensor_tensor(vT[:, :, :], vT[:, :, :], zT[:, :, :], ALU.mult))
            dve.tensor_tensor(vT[:, :, :], vT[:, :, :], gdnT[:, :, :], ALU.mult).then_inc(og_ready, 1)
            dve.wait_ge(og_ready, 1)
            for k in range(KD):
                dve.wait_ge(chunk_taken, C_PW + k + 1)
                lk(dve.tensor_tensor(zT[:, k, :], zT[:, k, :], gcvT[:, k, :], ALU.mult))
                dve.tensor_tensor(vT[:, k, :], vT[:, k, :], zT[:, k, :], ALU.add).then_inc(merged_ready, 1)
            pb = lambda n: par(n).unsqueeze(2).to_broadcast([P, KD, 1 + NDE])
            root = float(D) ** 0.5
            dve.scalar_tensor_tensor(out=cg[:, 1, :, :], in0=adaT[:, 2, :, :], scalar=root, in1=pb("g_post_mix"),
                                     op0=ALU.mult, op1=ALU.mult)
            lk(dve.scalar_tensor_tensor(out=cg[:, 2, :, :], in0=adaT[:, 4, :, :], scalar=1.0, in1=pb("g_pre_ffn"),
                                        op0=ALU.add, op1=ALU.mult))
            dve.tensor_scalar(cg[:, 2, :, :], cg[:, 2, :, :], root, None, ALU.mult)
            lk(dve.scalar_tensor_tensor(out=cg[:, 3, :, :], in0=adaT[:, 5, :, :], scalar=root, in1=pb("g_post_ffn"),
                                        op0=ALU.mult, op1=ALU.mult))
            dve.wait_ge(m_root, 2)
            lk(dve.reciprocal(row[:, 1, :], row[:, 0, :]))
            lk(dve.tensor_tensor(kT[:, :, :], kT[:, :, :], allrow, ALU.mult))
            dve.wait_ge(in_x2, 16)
            lk(dve.tensor_tensor(kT[:, :, NPR:NT], kT[:, :, NPR:NT], cg[:, 1, :, 1:], ALU.mult))
            dve.tensor_tensor(qT[:, :, NPR:NT], qT[:, :, NPR:NT], kT[:, :, NPR:NT], ALU.add)
            for k in range(KD):
                ins = dve.scalar_tensor_tensor(out=qT[:, k, 0:NPR], in0=kT[:, k, 0:NPR], scalar=cg[:, 1, k, 0:1],
                                               in1=qT[:, k, 0:NPR], op0=ALU.mult, op1=ALU.add)
            ins.then_inc(x1_ready, 1)
            dve.wait_ge(x1_ready, 1)
            dve.wait_ge(m_root, 3)
            lk(dve.reciprocal(row[:, 1, :], row[:, 0, :]))
            lk(dve.tensor_tensor(hT[:, :, :], qT[:, :, :], allrow, ALU.mult))
            lk(dve.tensor_tensor(hT[:, :, NPR:NT], hT[:, :, NPR:NT], cg[:, 2, :, 1:], ALU.mult))
            dve.tensor_tensor(hT[:, :, NPR:NT], hT[:, :, NPR:NT], adaT[:, 3, :, 1:], ALU.add)
            for k in range(KD):
                ins = dve.tensor_scalar(hT[:, k, 0:NPR], hT[:, k, 0:NPR], cg[:, 2, k, 0:1], adaT[:, 3, k, 0:1],
                                        ALU.mult, ALU.add)
            ins.then_inc(h2_ready, 1)
            R = lambda i: r3[:, i, :, :]
            b3 = lambda a: a.unsqueeze(2).to_broadcast([P, 3, E])
            dve.wait_ge(memset_done, 2)
            dve.wait_ge(rl_done, 1)
            br = par("b_router")
            dve.tensor_tensor(r3[:, 0, 0:2, :], ps[:, 3, 0:2 * E].rearrange("p (t e) -> p t e", t=2),
                              br.unsqueeze(1).to_broadcast([P, 2, E]), ALU.add)
            lk(dve.tensor_tensor(r3[0:NDE, 0, 2, :], ps[0:NDE, 3, 2 * E:3 * E], br[0:NDE, :], ALU.add))
            for t in range(3):
                lk(dve.max(top8[:, t, :], r3[:, 0, t, :]))
            lk(dve.tensor_tensor(R(4), R(0), b3(top8[:, :, 0]), ALU.subtract))
            dve.tensor_tensor(R(1), R(0), b3(top8[:, :, TOPK - 1]), ALU.is_gt).then_inc(rl_ready, 1)
            dve.wait_ge(rl_ready, 1)
            lk(dve.tensor_tensor(R(2), R(0), b3(top8[:, :, TOPK - 1]), ALU.is_equal))
            lk(dve.tensor_reduce(s3[:, 0, :], R(1), AX.X, ALU.add))
            lk(dve.tensor_scalar(s3[:, 1, :], s3[:, 0, :], -1.0, float(TOPK), ALU.mult, ALU.add))

            def running(dst, src):
                for t in range(3):
                    ins = dve.tensor_tensor_scan(r3[:, dst, t, :], ones[:, 0:E], r3[:, src, t, :], 0.0, ALU.mult, ALU.add)
                return ins
            lk(running(3, 2))
            lk(dve.tensor_tensor(R(3), R(3), b3(s3[:, 1, :]), ALU.is_le))
            lk(dve.tensor_tensor(R(3), R(3), R(2), ALU.mult))
            lk(dve.tensor_tensor(R(3), R(3), R(1), ALU.add))
            dve.wait_ge(in_moe, 4 * 16)
            dve.tensor_tensor(R(3), R(3), b3(cxc("valid")), ALU.mult).then_inc(sel_ready, 1)
            dve.wait_ge(sel_ready, 1)
            dve.wait_ge(tm_done, 3)
            dve.wait_ge(rl_done, 1)
            dve.tensor_copy(hT[:, :, NPR:NT], cg[:, 3, :, 1:])
            dve.tensor_copy(hT[:, :, 0:NPR], cg[:, 3, :, 0:1].to_broadcast([P, KD, NPR])).then_inc(gt_spread, 1)
            lk(running(6, 3))
            dve.wait_ge(rl_exp, 1)
            lk(dve.tensor_tensor(R(4), R(4), R(3), ALU.mult))
            lk(dve.tensor_reduce(s3[:, 2, :], R(4), AX.X, ALU.add))
            lk(dve.tensor_scalar(s3[:, 2, :], s3[:, 2, :], 0.5, None, ALU.max))
            lk(dve.reciprocal(s3[:, 3, :], s3[:, 2, :]))
            dve.tensor_tensor(R(5), R(4), b3(s3[:, 3, :]), ALU.mult).then_inc(gate_ready, 1)
            dve.wait_ge(gate_ready, 1)
            dve.wait_ge(rank_done, 1)
            lk(dve.tensor_scalar(R(7), ps[:, 2, 0:3 * E].rearrange("p (t e) -> p t e", t=3), 1.0, None, ALU.add))
            lk(dve.tensor_tensor(R(7), R(7), R(3), ALU.mult))
            lk(dve.tensor_scalar(R(7), R(7), -1.0, None, ALU.add))
            cnt = ps[:, 2, 3 * E:4 * E]
            lk(dve.tensor_scalar(eb[:, 0, :], cnt, float(CAP), None, ALU.is_gt))
            for m in range(2, -(-NT // CAP)):
                lk(dve.scalar_tensor_tensor(out=eb[:, 0, :], in0=cnt, scalar=float(CAP * m), in1=eb[:, 0, :],
                                            op0=ALU.is_gt, op1=ALU.add))
            lk(dve.tensor_tensor_scan(eb[:, 1, :], ones[:, 0:E], eb[:, 0, :], 0.0, ALU.mult, ALU.add))
            lk(dve.tensor_tensor(eb[:, 2, :], eb[:, 1, :], eb[:, 0, :], ALU.subtract))
            blocks = cxc("blocks")
            bb = lambda a: a.unsqueeze(2).to_broadcast([P, OVF, E])
            be = lambda a: a.unsqueeze(1).to_broadcast([P, OVF, E])
            lk(dve.tensor_tensor(wsel, bb(blocks), be(eb[:, 2, :]), ALU.is_ge))
            lk(dve.tensor_tensor(prod, bb(blocks), be(eb[:, 1, :]), ALU.is_lt))
            lk(dve.tensor_tensor(wsel, wsel, prod, ALU.mult))
            lk(dve.tensor_tensor(prod, wsel, be(cxc("experts")), ALU.mult))
            lk(dve.tensor_reduce(ob[:, 0, :], prod, AX.X, ALU.add))
            lk(dve.tensor_tensor(prod, wsel, be(eb[:, 2, :]), ALU.mult))
            lk(dve.tensor_reduce(ob[:, 1, :], prod, AX.X, ALU.add))
            dve.tensor_copy(obi[:, 0:OVF], ob[:, 0, :])
            dve.tensor_copy(obi[:, OVF:OVF + 1], eb[:, 1, E - 1:E]).then_inc(novf_ready, 1)
            lk(dve.tensor_tensor(ob[:, 2, :], blocks, ob[:, 1, :], ALU.subtract))
            lk(dve.tensor_scalar(ob[:, 2, :], ob[:, 2, :], float(CAP), float(CAP), ALU.mult, ALU.add))
            lk(dve.tensor_copy(rk[:, :, 0:E], R(7)))
            lk(dve.tensor_copy(tg[:, :, 0:E, 1], R(5)))
            lk(dve.tensor_copy(tg[:, :, :, 0], cxc("tokid").unsqueeze(2).to_broadcast([P, 3, NTAB])))
            for t in range(3):
                lk(dve.tensor_tensor(prod, wsel, be(r3[:, 7, t, :]), ALU.mult))
                lk(dve.tensor_reduce(rk[:, t, E:NBLK], prod, AX.X, ALU.add))
                lk(dve.tensor_tensor(rk[:, t, E:NBLK], rk[:, t, E:NBLK], ob[:, 2, :], ALU.subtract))
                lk(dve.tensor_tensor(prod, wsel, be(r3[:, 5, t, :]), ALU.mult))
                lk(dve.tensor_reduce(tg[:, t, E:NBLK, 1], prod, AX.X, ALU.add))
            for g in range(NTAB // 7):
                for t in range(3):
                    if g > 0:
                        dve.wait_ge(tab_done, g)
                    dve.tensor_tensor(selb[:, t, :, :], cxc("iota").unsqueeze(1).to_broadcast([P, 7, CAP]),
                                      rk[:, t, 7 * g:7 * g + 7].unsqueeze(2).to_broadcast([P, 7, CAP]),
                                      ALU.is_equal).then_inc(hot_ready, 1)
            dve.wait_ge(tab_done, NTAB // 7)
            tab = ps[0:CAP, 3, 0:2 * NTAB].rearrange("p (e a) -> p e a", a=2)
            dve.tensor_copy(tabi[:, :], tab[:, :, 0])
            dve.tensor_copy(tabg[0:CAP, :], tab[:, :, 1]).then_inc(tab_ready, 1)
            lk(dve.tensor_scalar(eb[:, 3, :], eb[:, 2, :], float(CAP), float(CAP * (E - 1)), ALU.mult, ALU.add))
            lk(dve.tensor_scalar(eb[:, 4, :], cxc("experts"), float(CAP), None, ALU.mult))
            lk(dve.tensor_tensor(eb[:, 3, :], eb[:, 3, :], eb[:, 4, :], ALU.subtract))
            b1 = lambda a: a.unsqueeze(1).to_broadcast([P, 3, E])
            lk(dve.tensor_scalar(R(8), R(7), float(CAP), None, ALU.is_ge))
            lk(dve.tensor_tensor(R(8), R(8), b1(eb[:, 3, :]), ALU.mult))
            lk(dve.tensor_tensor(R(8), R(8), b1(eb[:, 4, :]), ALU.add))
            lk(dve.tensor_tensor(R(8), R(8), R(7), ALU.add))
            lk(dve.tensor_tensor(R(8), R(8), R(3), ALU.mult))
            for k in range(TOPK):
                lk(dve.scalar_tensor_tensor(out=r3[:, 9, :, :].rearrange("p t e -> p (t e)"),
                                            in0=r3[:, 6, :, :].rearrange("p t e -> p (t e)"), scalar=float(k + 1),
                                            in1=r3[:, 8, :, :].rearrange("p t e -> p (t e)"),
                                            op0=ALU.is_equal, op1=ALU.mult))
                lk(dve.tensor_reduce(rowk[:, :, k], R(9), AX.X, ALU.add))
            dve.tensor_copy(rowi[:, :, :], rowk[:, :, :]).then_inc(rows_ready, 1)
            dve.wait_ge(in_moe, 4 * 16)

            def lo(blk, i):
                dve.wait_ge(hi_done, UNITS * blk + i + 1)
                dve.tensor_tensor(low(i), raw(i), stH[:, i % NSTG, :].bitcast(F32), ALU.subtract
                                  ).then_inc(lo_done, 1)

            def rows_lo(blk):
                dve.wait_ge(xsh_ready, blk + 1)
                dve.tensor_tensor(XS[:, :, CAP:2 * CAP], ps[:, 0, :].rearrange("p (k n) -> p k n", k=KD),
                                  XS[:, :, 0:CAP].bitcast(F32), ALU.subtract).then_inc(xs_ready, 1)

            def rows_of(blk):
                dve.wait_ge(yl_ready, blk + 1)
                dve.scalar_tensor_tensor(out=yb[:, :], in0=ps[0:CAP, 4:6, :].rearrange("p b n -> p (b n)"),
                                         scalar=gcol[0:CAP, 0:1], in1=yl[:, :], op0=ALU.mult, op1=ALU.add
                                         ).then_inc(y_ready, 1)

            LINKS = 5

            def body(blk, e):
                first = isinstance(blk, int)
                links = [0]

                def lb(ins):
                    links[0] += 1
                    ins.then_inc(block_chain, 1)
                    dve.wait_ge(block_chain, LINKS * blk + links[0])
                for i in range(GU + 1):
                    lo(blk, i)
                    if i == NSTG - 1 and not first:
                        rows_of(blk - 1)
                if not first:
                    dve.wait_ge(y_ready, blk)
                dve.tensor_copy(gcol[:, :], tabg[:, bass.ds(blk, 1)])
                lb(dve.tensor_copy(bcol[:, :], btab[:, bass.ds(e * (2 * KD), 2 * KD)]))
                dve.wait_ge(unit_used, UNITS * blk + GU)
                if first:
                    dve.wait_ge(fb_out, 48)
                dve.tensor_copy(G[:, D:2 * D], ps[:, 2:4, :].rearrange("p b n -> p (b n)")).then_inc(gd_copied, 1)
                lo(blk, GU + 1)
                bias = lambda a: bcol[:, a * KD:(a + 1) * KD].unsqueeze(2).to_broadcast([P, KD, CAP])
                gl_ = nl[:, 0, :, :]
                up = nl[:, 1, :, :]
                dve.wait_ge(fold_done, 2 * blk + 1)
                lb(dve.tensor_tensor(gl_, ps[:, 6, :].rearrange("p (k n) -> p k n", k=KD), bias(0), ALU.add))
                dve.tensor_scalar(gl_, gl_, LIMIT, None, ALU.min).then_inc(t1_ready, 1)
                dve.wait_ge(fold_done, 2 * blk + 2)
                lb(dve.tensor_tensor(up, ps[:, 7, :].rearrange("p (k n) -> p k n", k=KD), bias(1), ALU.add))
                lb(dve.tensor_scalar(up, up, LIMIT, -LIMIT, ALU.min, ALU.max))
                dve.wait_ge(t1_ready, blk + 1)
                lb(dve.scalar_tensor_tensor(out=up, in0=up, scalar=1.0, in1=gl_, op0=ALU.add, op1=ALU.mult))
                dve.wait_ge(sg_ready, blk + 1)
                dve.tensor_tensor(nl[:, 2, :, :], up, nl[:, 3, :, :], ALU.mult).then_inc(act_ready, 1)
                lo(blk, GU + 2)
                dve.wait_ge(ash_ready, blk + 1)
                dve.tensor_tensor(AS[:, :, CAP:2 * CAP], nl[:, 2, :, :], AS[:, :, 0:CAP].bitcast(F32),
                                  ALU.subtract).then_inc(as_ready, 1)
                rows_lo(blk + 1)
                if not first:
                    dve.wait_ge(y_out, 16 * blk)
                lo(blk, GU + 3)
                assert links[0] == LINKS
            for t, (t0, m) in enumerate(TILES):
                dve.wait_ge(bias_done, t + 1)
                dve.tensor_copy(fbt[t][0:m, :], ps[0:m, 4:6, :].rearrange("p b n -> p (b n)")).then_inc(bias_copied, 1)
            rows_lo(0)
            dve.wait_ge(tab_dup, 1)
            body(0, 0)
            with dve.Fori(1, E) as e:
                body(e, e)
            n = overflow(dve, lambda blk, b: body(blk, dve.value_load(obi[0:1, bass.ds(b, 1)], min_val=0, max_val=E - 1)))
            rows_of(n + (E - 1))
            dve.memset(s3[0:1, 0, 0:1], 0.0).then_inc(all_done, 1)
            for t, (t0, m) in enumerate(TILES):
                dve.wait_ge(tail_in[t], 16 * TOPK)
                dve.wait_ge(resid_in, 9 * 16)
                f = facc[0:m, t, :]
                lk(dve.tensor_tensor(f, f, yg[0:m, t, 0, :], ALU.add))
                for k in range(1, TOPK - 1):
                    lk(dve.tensor_tensor(f, f, yg[0:m, t, k, :], ALU.add))
                dve.tensor_tensor(f, f, yg[0:m, t, TOPK - 1, :], ALU.add).then_inc(f_ready, 1)
                dve.wait_ge(f_sq, 2 * t + 2)
                lk(dve.reciprocal(rs[0:m, t, :], rs[0:m, t, :]))
                lk(dve.scalar_tensor_tensor(out=f, in0=f, scalar=rs[0:m, t, :], in1=g2t[0:m, t, :], op0=ALU.mult, op1=ALU.mult))
                dve.tensor_tensor(f, f, x1t[0:m, t, :], ALU.add).then_inc(out_ready, 1)

        @block.gpsimd
        def _(pool):
            pool.memset(ones[:, :], 1.0)
            pool.memset(ba[:, :, :], 0.0)
            pool.memset(S[:, :, :], 0.0)
            pool.memset(qx[:, :, 0:SC - 1], 0.0)
            pool.memset(uP[:, :, 0:CC - 1], 0.0).then_inc(memset_done, 1)
            pool.wait_ge(in_x, 16)
            pool.tensor_tensor(qT[:, :, :], hT[:, :, :], hT[:, :, :], ALU.mult).then_inc(m_sq, 1)
            pool.wait_ge(in_cv, 16)
            masks = con("levels").rearrange("p (l n) -> p l n", l=LEVELS)
            for c in range(NC):
                pool.wait_ge(decay_exp, 2 * c + 2)
                pool.tensor_tensor(bI[:, :, :], bI[:, :, :], upper.unsqueeze(1).to_broadcast([P, H, P]),
                                   ALU.mult).then_inc(decay_ready, 1)
                pool.wait_ge(a_ready, c + 1)
                for l in range(LEVELS):
                    s = c * LEVELS + l
                    if l >= 2:
                        pool.wait_ge(z_done, 2 * (s - 1))
                        pool.wait_ge(m_upd, 2 * (c * (LEVELS - 1)) + 2)
                    if l < 2 and c > 0:
                        pool.wait_ge(u_done, c)
                    pool.tensor_tensor(bB[s % 2][:, :, :], bA[:, :, :], masks[:, l:l + 1, :].to_broadcast([P, H, P]),
                                       ALU.mult).then_inc(b_ready, 1)

            eg = dcol[:, 1, :, :]
            ihb = ident[0:H * NDE, 0:H * NDE].rearrange("p (h b) -> p h b", b=NDE)
            pool.wait_ge(dbc_copy, 1)
            pool.wait_ge(sk_done, 1)
            for g in range(16):
                b, h0 = g // 2, 4 * (g % 2)
                sg = Sd[:, 4 * g:4 * g + 4, :]
                pool.tensor_tensor(sg, sg, eg[:, h0:h0 + 4, b].unsqueeze(2).to_broadcast([P, 4, P]),
                                   ALU.mult).then_inc(sd_decayed, 1)
                if g == 0:
                    pool.wait_ge(drow_copy, 1)
                    pool.wait_ge(ln_var, 1)
                if g >= 4:
                    pool.wait_ge(outer_done, g - 3)
                pool.tensor_tensor(dmask[:, g % 4, :].rearrange("p (h v) -> p h v", h=4),
                                   drow[:, 1:2, :].to_broadcast([H * NDE, 4, P]),
                                   ihb[:, h0:h0 + 4, b].unsqueeze(2).to_broadcast([H * NDE, 4, P]),
                                   ALU.mult).then_inc(dm_ready, 1)
            pool.wait_ge(out_st, 6 * 16)
            pool.wait_ge(h2_ready, 1)
            pool.memset(r3[:, 0, :, :], 0.0)
            pool.memset(tg[:, :, NBLK:, 1], 0.0)
            pool.memset(rk[:, :, NBLK:], -1.0).then_inc(memset_done, 1)

            def gather(blk):
                if not (isinstance(blk, int) and blk == 0):
                    pool.wait_ge(idx_ready, 2 * blk)
                pool.tensor_copy(idxc[:, :], tabi[:, bass.ds(blk, 1)]).then_inc(idx_ready, 1)
                pool.wait_ge(idx_ready, 2 * blk + 1)
                pool.tensor_tensor(idxw[:, 0:1], idxc[0:1, :], idxc[0:1, :], ALU.add).then_inc(idx_ready, 1)
                pool.indirect_dma_start(out=Xg[:, :], out_offset=None, in_=A["h2rows"],
                                        in_offset=bass.IndirectOffsetOnAxis(ap=idxc[:, :], axis=0)).then_inc(xg_in, 16)

            def store(blk):
                pool.wait_ge(y_ready, blk + 1)
                pool.dma_start(A["yrows"][bass.ds(blk * CAP, CAP), :], yb[:, :]).then_inc(y_out, 16)

            def body(blk, e):
                pool.wait_ge(xt_done, blk + 1)
                gather(blk + 1)
                if not isinstance(blk, int):
                    store(blk - 1)
                pool.wait_ge(xg_in, 16 * blk + 32)
            pool.wait_ge(tab_ready, 1)
            pool.wait_ge(zero_out, 16)
            for i in range(3):
                pool.wait_ge(rows_out[i], 16)
            gather(0)
            pool.wait_ge(xg_in, 16)
            body(0, 0)
            with pool.Fori(1, E) as e:
                body(e, e)
            n = overflow(pool, body)
            store(n + (E - 1))
            pool.wait_ge(rows_ready, 1)
            pool.wait_ge(all_done, 1)
            pool.wait_ge(y_out, (n + E) * 16)
            pool.tensor_tensor(idxw[:, 1:2], idxc[0:1, :], idxc[0:1, :], ALU.add)
            for t, (t0, m) in enumerate(TILES):
                for k in range(TOPK):
                    pool.indirect_dma_start(out=yg[0:m, t, k, :], out_offset=None, in_=A["yrows"],
                                            in_offset=bass.IndirectOffsetOnAxis(ap=rowi[0:m, t, k:k + 1], axis=0)
                                            ).then_inc(tail_in[t], 16)


def consts():
    import numpy as np
    c = np.zeros((P, NCV), np.float32)
    i, j = np.arange(P)[:, None], np.arange(P)[None, :]

    def put(name, a):
        c[:, CV[name][0]:CV[name][1]] = a
    put("ident", i == j)
    put("upper", i <= j)
    lv = [(i >> (l + 1) == j >> (l + 1)) & ((i >> l) & 1 == 1) & ((j >> l) & 1 == 0) for l in range(LEVELS)]
    put("levels", np.concatenate(lv, 1))
    put("eps", np.array([[D * EPS, EPS, P * EPS, EPS]]) + 0 * i)
    x = np.zeros((P, NCX), np.float32)

    def put(name, a):
        x[:, CX[name][0]:CX[name][1]] = a
    put("iota", np.arange(CAP)[None, :])
    put("strict_upper", i < j)
    put("tokid", np.arange(3)[None, :] * P + i)
    put("valid", np.arange(3)[None, :] * P + i < NT)
    put("experts", np.arange(E)[None, :])
    put("fold", i % CAP == np.arange(CAP)[None, :])
    put("blocks", np.arange(OVF)[None, :])
    return c, x


def layout(inputs):
    import numpy as np
    f = {k: np.asarray(v) for k, v in inputs.items()}

    def fm(a):
        return np.ascontiguousarray(a.reshape(a.shape[0], -1, P).transpose(2, 1, 0))

    def rep(a):
        return np.broadcast_to(a.reshape(1, -1), (P, a.size))
    x = np.concatenate([f["x_prompt"][0], f["x_sample"][:, 0]], 0)
    c = np.concatenate([f["c_prompt"], f["c_sample"]], 0)
    cols = {"b_ada": fm(f["b_ada"])[:, :, 0], "w_qkv_conv": fm(f["w_qkv_conv"][0]).reshape(P, -1),
            "w_dw": fm(f["w_dw_conv"][0]).reshape(P, -1), "b_dw": fm(f["b_dw_conv"])[:, :, 0],
            "g_ln": fm(f["g_ln_conv"])[:, :, 0], "b_ln": fm(f["b_ln_conv"])[:, :, 0],
            "b_pw": fm(f["b_pw_conv"])[:, :, 0], "g_dn": fm(f["g_dn_norm"])[:, :, 0],
            "a_log": rep(f["a_log"]), "dt_bias": rep(f["dt_bias"]), "b_router": rep(f["b_router"])}
    for n in ("g_pre_mix", "g_post_mix", "g_pre_ffn", "g_post_ffn"):
        cols[n] = fm(f[n])[:, :, 0]
    pvv = np.concatenate([cols[n] for n in PV], 1)
    qs = f["state_qkv_conv"][0].reshape(NDE, SC - 1, NQKV, P).transpose(3, 2, 0, 1)
    us = f["state_glu_conv"][0].reshape(NDE, CC - 1, KD, P).transpose(3, 2, 0, 1)
    w_in = f["w_in"][0]
    return {
        "cT": fm(c), "xT": fm(x), "pv": np.ascontiguousarray(pvv), "cv": consts()[0], "cx": consts()[1],
        "wr": np.ascontiguousarray(f["w_router"][0].reshape(KD, P, E).transpose(1, 0, 2)),
        "btab": np.ascontiguousarray(f["b_gate_up"][0].reshape(E, 2 * KD, P).transpose(2, 0, 1)).reshape(P, -1),
        "bdn": f["b_down"][0], "gate_up": f["w_gate_up"][0], "down": f["w_down"][0],
        "wba": np.ascontiguousarray(w_in[:, 4 * D:GLU0].reshape(KD, P, 2 * H).transpose(1, 0, 2)),
        "qkv_state": np.pad(qs, ((0, 0), (0, 0), (0, 0), (0, 1))),
        "glu_state": np.pad(us, ((0, 0), (0, 0), (0, 0), (0, 1))),
        "sdn": np.ascontiguousarray(f["state_dn"][0].reshape(NDE * H, P, P).transpose(1, 0, 2)).reshape(P, -1),
        "ada": f["w_ada"][0], "in": w_in, "pw": f["w_pw_conv"][0], "out": f["w_out"][0],
    }

OUTS = {"s_prompt": (P, H, P), "q_prompt": (P, NQKV, SC - 1), "q_sample": (P, NQKV, NDE, SC),
        "g_prompt": (P, KD, CC - 1), "g_sample": (P, KD, NDE, CC), "s_sample": (P, NDE * H * P), "y": (NT, D)}
SCRATCH = {"h2rows": (NT, D), "x1rows": (NT, D), "g2rows": (NT, D), "fbrows": (NT, D), "yrows": (NBLK * CAP, D)}


def kernel(**inputs):
    import numpy as np
    import concourse.bacc as _bacc
    from concourse import mybir as _mybir
    from concourse.bass_utils import run_bass_kernel_spmd as _run

    arrays = layout(inputs)
    nc = _bacc.Bacc("TRN2", target_bir_lowering=False, num_devices=1)
    ins, outs = {}, {}
    for n, a in arrays.items():
        ins[n] = nc.dram_tensor(n + "_dram", a.shape, _mybir.dt.from_np(a.dtype), kind="ExternalInput").ap()
    for n, shape in SCRATCH.items():
        ins[n] = nc.dram_tensor(n + "_dram", shape, _mybir.dt.float32, kind="Internal").ap()
    for n, shape in OUTS.items():
        outs[n] = nc.dram_tensor(n + "_dram", shape, _mybir.dt.float32, kind="ExternalOutput").ap()
    build(nc, ins, outs)
    r = _run(nc, [{n + "_dram": a for n, a in arrays.items()}], core_ids=[0])
    got = {n: np.asarray(r.results[0][n + "_dram"]).reshape(shape) for n, shape in OUTS.items()}

    def rows(a):
        a = np.moveaxis(a, (0, 1), (-1, -2))
        return np.ascontiguousarray(a.reshape(a.shape[:-2] + (-1,)))
    y = got["y"]
    return (y[None, :NPR], y[NPR:, None],
            np.ascontiguousarray(got["s_prompt"].transpose(1, 0, 2))[None, None],
            rows(got["q_prompt"])[None, None], rows(got["g_prompt"])[None, None],
            np.ascontiguousarray(got["s_sample"].reshape(P, NDE, H, P).transpose(1, 2, 0, 3))[None],
            rows(got["q_sample"][..., 1:])[None], rows(got["g_sample"][..., 1:])[None])
```

```python
import concourse.bass as bass
from concourse import mybir
from contextlib import ExitStack

F32 = mybir.dt.float32
F32R = mybir.dt.float32r
I32 = mybir.dt.int32
ALU = mybir.AluOpType
ACT = mybir.ActivationFunctionType
AX = mybir.AxisListType

P = 128
D = 1024
KD = D // P
NPR = 256
NDE = 8
NT = NPR + NDE
H = 8
CH = 128
NC = NPR // CH
LEVELS = 7
SC = 4
CC = 31
E = 32
TOPK = 4
CAP = 64
OVF = NT * TOPK // CAP
NBLK = E + OVF
GRP = 10
NTAB = NBLK + 2
UNITS = 12
GU = 8
UW = 2048
NSTG = 6
LIMIT, ALPHA = 7.0, 1.702
EPS = 1e-6
FF = 1024
NQKV = 3 * KD
BW = 512
CPB = BW // P
RING = 4

PV = {}
_at = 0
for _name, _n in (("b_ada", 48), ("g_pre_mix", 8), ("g_post_mix", 8), ("g_pre_ffn", 8), ("g_post_ffn", 8),
                  ("w_qkv_conv", NQKV * SC), ("w_dw", KD * CC), ("b_dw", 8), ("g_ln", 8), ("b_ln", 8),
                  ("b_pw", 8), ("g_dn", 1), ("a_log", 8), ("dt_bias", 8), ("b_router", E)):
    PV[_name] = (_at, _at + _n)
    _at += _n
NPV = _at
CV = {}
_at = 0
for _name, _n in (("ident", P), ("upper", P), ("levels", LEVELS * P), ("eps", 4)):
    CV[_name] = (_at, _at + _n)
    _at += _n
NCV = _at

CX = {}
_at = 0
for _name, _n in (("iota", CAP), ("strict_upper", P), ("tokid", 3), ("valid", 3), ("experts", E), ("fold", CAP),
                  ("blocks", OVF)):
    CX[_name] = (_at, _at + _n)
    _at += _n
NCX = _at

QKV_COLS, GLU0 = 3 * D, 4 * D + 2 * H
MG0 = GLU0 + 2 * D
BLOCKS = ([("ada", BW * n) for n in range(4)]
          + [("in", BW * n) for n in range(8)]
          + [("in", GLU0 + BW * n) for n in range(4)]
          + [("in", MG0 + D + BW * n) for n in range(2)]
          + [("ada", BW * n) for n in range(4, 12)]
          + [("in", MG0 + BW * n) for n in range(2)]
          + [("pw", BW * n) for n in range(2)]
          + [("out", BW * n) for n in range(2)])
NB = len(BLOCKS)
C_ADA1, C_QKV, C_Z, C_UV, C_UG, C_GCV, C_ADA2, C_GDN, C_PW, C_OUT = 0, 16, 40, 48, 56, 64, 72, 104, 112, 120


def build(nc, A, O):
    ctx = ExitStack()
    with ctx:
        def sb(name, shape, dt=F32):
            return ctx.enter_context(nc.sbuf_tensor(name, shape, dt))

        def sem(name):
            return ctx.enter_context(nc.semaphore(name))

        lows = ExitStack()
        ringL = lows.enter_context(nc.sbuf_tensor("ringL", [P, RING, KD, BW], F32R))
        workL = lows.enter_context(nc.sbuf_tensor("workL", [P, 8, D], F32R))
        lows.close()
        ring = sb("ring", [P, RING, KD, BW])
        work = sb("work", [P, 8, D])
        hT = sb("hT", [P, KD, NT])
        qT = sb("qT", [P, KD, NT])
        pv = sb("pv", [P, NPV])
        cv = sb("cv", [P, NCV])
        ones = sb("ones", [P, P])
        row = sb("row", [P, 2, NT])
        cg = sb("cg", [P, 4, KD, 1 + NDE])
        phase1 = ExitStack()

        def sb(name, shape, dt=F32):
            return phase1.enter_context(nc.sbuf_tensor(name, shape, dt))
        kT = sb("kT", [P, KD, NT])
        vT = sb("vT", [P, KD, NT])
        zT = sb("zT", [P, KD, NT])
        gcvT = sb("gcvT", [P, KD, NT])
        gdnT = sb("gdnT", [P, KD, NT])
        cvT = sb("cvT", [P, KD, NT])
        uP = sb("uP", [P, KD, CC - 1 + NPR])
        uD = sb("uD", [P, KD, NDE, CC])
        xD = sb("xD", [P, NQKV, NDE, SC])
        q3 = sb("q3", [P, NQKV, SC - 1])
        cT = sb("cT", [P, KD, 1 + NDE])
        adaT = sb("adaT", [P, 6, KD, 1 + NDE])
        misc = sb("misc", [P, BW])
        arow = misc[0:1 + NDE, :]
        wba = sb("wba", [P, KD, 2 * H])
        ba = sb("ba", [P, 3, 2 * H])
        tk = sb("tk", [P, 14, 3, H])
        S = sb("S", [P, H, P])
        gl = sb("gl", [P, 2, H])
        dcol = sb("dcol", [P, 10, H, NDE])
        ctap = misc[:, 0:2 * NDE * CC].rearrange("p (a b j) -> p a b j", a=2, j=CC)
        dcv = sb("dcv", [P, KD, NDE])
        gdn_s = sb("gdn_s", [P, 1])
        kq = sb("kq", [P, H, NDE, 2])
        bc8 = sb("bc8", [NDE, 2, H, NDE])
        drow = sb("drow", [H * NDE, 2, P])
        phase1.close()
        plain = ExitStack()
        stP = plain.enter_context(nc.sbuf_tensor("stP", [P, NSTG, UW], F32))
        plain.close()
        moe = ExitStack()
        ctx.push(moe)

        def sb(name, shape, dt=F32):
            return moe.enter_context(nc.sbuf_tensor(name, shape, dt))
        stH = sb("stH", [P, NSTG, UW], F32R)
        XS = sb("XS", [P, KD, 2 * CAP], F32R)
        AS = sb("AS", [P, KD, 2 * CAP], F32R)
        G = sb("G", [P, UW])
        nl = hT[:, :, :].rearrange("p k n -> p (k n)")[:, 0:4 * KD * CAP].rearrange(
            "p (i k n) -> p i k n", i=4, n=CAP)
        Xg = sb("Xg", [CAP, D])
        qflat = qT[:, :, :].rearrange("p k n -> p (k n)")
        yl = qflat[0:CAP, 0:D]
        yb = qflat[0:CAP, D:2 * D]
        wr = sb("wr", [P, KD, E])
        cx = sb("cx", [P, NCX])
        btab = sb("btab", [P, E * 2 * KD])
        bdn = sb("bdn", [E, D])
        r3 = sb("r3", [P, 12, 3, E])
        top8 = sb("top8", [P, 3, 8])
        s3 = sb("s3", [P, 4, 3])
        eb = sb("eb", [P, 6, E])
        ob = sb("ob", [P, 4, OVF])
        obi = sb("obi", [P, OVF + 1], I32)
        rk = sb("rk", [P, 3, NTAB])
        tg = sb("tg", [P, 3, NTAB, 3], F32R)
        rowk = sb("rowk", [P, 3, TOPK])
        rowi = sb("rowi", [P, 3, TOPK], I32)
        tabi = sb("tabi", [CAP, NTAB], I32)
        tabg = sb("tabg", [P, NTAB])
        idxc = sb("idxc", [CAP, 1], I32)
        idxw = sb("idxw", [1, 2], I32)
        gcol = sb("gcol", [P, 1])
        bcol = sb("bcol", [P, 2 * KD])
        GT = cg[0:E, :, :, :].rearrange("e a k n -> e (a k n)")[:, 0:NT]
        ss = sb("ss", [P, 3, 1])
        rs = sb("rs", [P, 3, 1])
        ps = ctx.enter_context(nc.psum_tensor("ps", [P, 8, 512], F32))

        def par(name):
            return pv[:, PV[name][0]:PV[name][1]]

        def con(name):
            return cv[:, CV[name][0]:CV[name][1]]

        ident, upper = con("ident"), con("upper")

        def cxc(name):
            return cx[:, CX[name][0]:CX[name][1]]
        wflat = work[:, :, :].rearrange("p a b -> p (a b)")
        qx = wflat[:, 0:4 * (SC - 1 + NPR)].rearrange("p (s n) -> p s n", s=4)
        qc = wflat[:, 1100:1100 + 4 * NT].rearrange("p (s n) -> p s n", s=4)
        sq = wflat[:, 2200:2200 + 4 * NT].rearrange("p (s n) -> p s n", s=4)
        rt = wflat[:, 3300:3300 + 4 * NT].rearrange("p (s n) -> p s n", s=4)
        tmp = wflat[:, 4400:4400 + NDE * SC * 4].rearrange("p (s b j) -> p s b j", s=4, j=SC)
        bA, bI, bM, bMT, bZ, bB0, bB1, bX = (work[:, i, :].rearrange("p (h n) -> p h n", h=H) for i in range(8))
        bB = (bB0, bB1)
        dmask = qT[0:H * NDE, :, :].rearrange("p k n -> p (k n)")[:, 0:4 * 512].rearrange("p (s n) -> p s n", s=4)
        Sd = wflat.rearrange("p (n v) -> p n v", v=P)

        gu_raw = ring[:, :, :, :].rearrange("p s k n -> p (s k n)").rearrange("p (u n) -> p u n", n=UW)
        dn_raw = work[:, :, :].rearrange("p (u a) n -> p u (a n)", a=2)
        raw = lambda i: gu_raw[:, i, :] if i < GU else dn_raw[:, i - GU, :]
        gu_low = ringL[:, :, :, :].rearrange("p s k n -> p (s k n)").rearrange("p (u n) -> p u n", n=UW)
        dn_low = workL[:, :, :].rearrange("p (u a) n -> p u (a n)", a=2)
        low = lambda i: gu_low[:, i, :] if i < GU else dn_low[:, i - GU, :]
        yg = gu_raw.rearrange("p u n -> p (u n)").rearrange("p (t k n) -> p t k n", k=TOPK, n=D)
        facc = work[:, 0:3, :]
        selb = [stH[:, i, 0:3 * GRP * CAP].rearrange("p (t e n) -> p t e n", t=3, e=GRP)
                for i in range(2)]
        prod = stP[:, 3, :][:, 0:OVF * E].rearrange("p (b e) -> p b e", b=OVF)
        gov = stP[:, 3, 1024:1024 + 3 * (NTAB - E)].rearrange("p (t e) -> p t e", t=3)
        wsel = stP[:, 4, :][:, 0:OVF * E].rearrange("p (b e) -> p b e", b=OVF)
        rowbuf = [stP[:, a, i * D:(i + 1) * D] for a in (5, 2) for i in range(2)]
        fbt = [G[:, 0:D], G[:, D:2 * D], nl.rearrange("p i k n -> p (i k n)")[:, 0:D]]
        x1t = work[:, 3:6, :]
        g2t = gu_raw.rearrange("p u n -> p (u n)")[:, 12 * D:15 * D].rearrange("p (t n) -> p t n", n=D)
        sqt = stP[:, 2, 0:D]

        in_c, in_pv, in_cv, in_x, in_mix, in_x2, in_sd = (
            sem(n) for n in ("in_c", "in_pv", "in_cv", "in_x", "in_mix", "in_x2", "in_sd"))
        ring_in = [sem(f"ring_in{i}") for i in range(RING)]
        chunk_done = sem("chunk_done")
        chunk_taken = sem("chunk_taken")
        dve_chain, act_chain, pool_chain = sem("dve_chain"), sem("act_chain"), sem("pool_chain")
        memset_done = sem("memset_done")
        ada_rows = sem("ada_rows"); ada_copied = sem("ada_copied")
        c_silu = sem("c_silu")
        h_ready = sem("h_ready")
        conv_done = sem("conv_done"); qkv_ready = sem("qkv_ready")
        l2_sq = sem("l2_sq"); l2_ss = sem("l2_ss"); l2_root = sem("l2_root"); l2_done = sem("l2_done")
        logit_done = sem("logit_done"); logit_copy = sem("logit_copy")
        softplus_in = sem("softplus_in"); gate_in = sem("gate_in"); beta_ready = sem("beta_ready")
        g_ready = sem("g_ready"); ug_ready = sem("ug_ready"); gc_done = sem("gc_done"); gc_ready = sem("gc_ready")
        R_done = sem("R_done"); split_ready = sem("split_ready"); decay_exp = sem("decay_exp")
        decay_ready = sem("decay_ready"); small_exp = sem("small_exp"); R_used = sem("R_used")
        gram_done = sem("gram_done"); a_ready = sem("a_ready"); intra_ready = sem("intra_ready")
        qe_ready = sem("qe_ready")
        b_ready = sem("b_ready"); z_done = sem("z_done"); z_copied = sem("z_copied")
        m_done = sem("m_done"); mt_upd = sem("mt_upd"); m_upd = sem("m_upd")
        vk_done = sem("vk_done"); vk_ready = sem("vk_ready"); w_done = sem("w_done"); w_ready = sem("w_ready")
        u_done = sem("u_done"); vn_ready = sem("vn_ready"); o_done = sem("o_done"); o_ready = sem("o_ready")
        s_done = sem("s_done"); s_ready = sem("s_ready")
        ug_sig = sem("ug_sig"); u_ready = sem("u_ready"); conf_done = sem("conf_done"); dcv_done = sem("dcv_done")
        out_st = sem("out_st")
        dec_in = sem("dec_in"); dbc_done = sem("dbc_done"); dbc_copy = sem("dbc_copy")
        sk_done = sem("sk_done"); delta_ready = sem("delta_ready"); drow_done = sem("drow_done")
        drow_copy = sem("drow_copy"); dm_ready = sem("dm_ready"); outer_done = sem("outer_done")
        sd_decayed = sem("sd_decayed"); sd_new = sem("sd_new")
        ln_sums = sem("ln_sums"); ln_centred = sem("ln_centred"); ln_power = sem("ln_power")
        ln_norm = sem("ln_norm"); conf_ready = sem("conf_ready")
        og_sq = sem("og_sq"); og_ss = sem("og_ss"); og_root = sem("og_root")
        mg_sig = sem("mg_sig"); merged_ready = sem("merged_ready")
        m_sq = sem("m_sq"); m_ss = sem("m_ss"); m_root = sem("m_root")
        x1_ready = sem("x1_ready")
        h2_ready = sem("h2_ready"); gt_spread = sem("gt_spread")

        in_moe = sem("in_moe")
        on_ring = lambda i: i < GU and i % 2 == 0
        raw_in = [ring_in[i // 2] if on_ring(i) else sem(f"raw_in{i}") for i in range(UNITS)]
        RING_END = 16 * NB // RING
        tm_done = sem("tm_done"); tm_copied = sem("tm_copied"); rows_out = [sem(f"rows_out{i}") for i in range(4)]; fb_out = sem("fb_out")
        rl_done = sem("rl_done"); rl_ready = sem("rl_ready"); rl_exp = sem("rl_exp"); sel_ready = sem("sel_ready")
        rank_done = sem("rank_done"); gate_ready = sem("gate_ready"); gt_done = sem("gt_done"); gt_copied = sem("gt_copied")
        hot_ready = sem("hot_ready"); tab_done = sem("tab_done"); tab_ready = sem("tab_ready"); tab_dup = sem("tab_dup")
        novf_ready = sem("novf_ready"); rows_ready = sem("rows_ready"); bias_done = sem("bias_done"); bias_copied = sem("bias_copied")
        block_chain = sem("block_chain"); zero_out = sem("zero_out")
        hi_done = sem("hi_done"); lo_done = sem("lo_done"); unit_used = sem("unit_used")
        ga_copied = sem("ga_copied"); gd_copied = sem("gd_copied"); fold_done = sem("fold_done")
        t1_ready = sem("t1_ready"); sg_ready = sem("sg_ready"); act_ready = sem("act_ready"); ash_ready = sem("ash_ready")
        as_ready = sem("as_ready"); xt_done = sem("xt_done"); xsh_ready = sem("xsh_ready"); xs_ready = sem("xs_ready")
        idx_ready = sem("idx_ready"); xg_in = sem("xg_in"); yl_ready = sem("yl_ready"); y_ready = sem("y_ready"); y_out = sem("y_out")
        all_done = sem("all_done"); tail_in = [sem(f"tail_in{t}") for t in range(3)]; f_ready = [sem("f_ready0")] * 2 + [sem("f_ready2")]
        resid_in = sem("resid_in")
        f_sq = sem("f_sq"); out_ready = sem("out_ready")
        TILES = ((0, P), (P, P), (NPR, NDE))

        def overflow(eng, body):
            eng.wait_ge(novf_ready, 1)
            n = eng.value_load(obi[0:1, OVF:OVF + 1], min_val=0, max_val=OVF)
            with eng.Fori(0, OVF) as b:
                with eng.If(b < n):
                    body(b + E, b)
            return n

        def link(eng, chain, ins):
            chain[1] += 1
            ins.then_inc(chain[0], 1)
            eng.wait_ge(chain[0], chain[1])

        ADA_BLOCKS = [j for j, (name, c0) in enumerate(BLOCKS) if name == "ada"]
        FILL = ([("chunk", n) for n in range(C_GCV, C_ADA2)] + [("ada", a) for a in range(4, 13)]
                + [("chunk", n) for n in range(C_GDN, C_GDN + CPB)])
        wd = par("w_dw").rearrange("p (k j) -> p k j", j=CC)
        CONV_DVE, CONV_POOL = ((0, 1, 2), (3, 4, 5)), slice(6, 8)


        def add_experts(eng, chain, t):
            m = TILES[t][1]
            f = facc[0:m, t, :]
            eng.wait_ge(tail_in[t], 16 * TOPK)
            eng.wait_ge(resid_in, 9 * 16)
            for k in range(TOPK - 1):
                link(eng, chain, eng.tensor_tensor(f, f, yg[0:m, t, k, :], ALU.add))
            eng.tensor_tensor(f, f, yg[0:m, t, TOPK - 1, :], ALU.add).then_inc(f_ready[t], 1)
        bank = lambda b: ps[:, b, :]
        half = lambda b: ps[:, b, :].rearrange("p (h n) -> p h n", h=4)
        two = lambda b: ps[:, b:b + 2, :].rearrange("p b (h n) -> p (b h) n", h=4)
        block = ctx.enter_context(nc.Block())

        @block.sync
        def _(sp):
            sp.dma_start(cT[:, :, :], A["cT"]).then_inc(in_c, 16)
            w = {n: A[n].rearrange("(k p) n -> p k n", p=P) for n in ("ada", "in", "pw", "out")}
            for j, (name, c0) in enumerate(BLOCKS):
                if j == C_PW // CPB - 1 + RING:
                    sp.wait_ge(s_ready, NC)
                    sp.dma_start(wflat, A["sdn"]).then_inc(in_sd, 16)
                if j >= RING:
                    sp.wait_ge(chunk_done, CPB * (j - RING + 1))
                sp.dma_start(ring[:, j % RING, :, :], w[name][:, :, c0:c0 + BW]).then_inc(ring_in[j % RING], 16)
                if j == 0:
                    sp.dma_start(hT[:, :, :], A["xT"]).then_inc(in_x, 16)
                    sp.dma_start(cv[:, :], A["cv"]).then_inc(in_cv, 16)
                    sp.dma_start(pv[:, :], A["pv"]).then_inc(in_pv, 16)
                if j == 3:
                    sp.dma_start(wba[:, :, :], A["wba"]).then_inc(in_mix, 16)
                    sp.dma_start(xD[:, :, :, :], A["qkv_state"]).then_inc(in_mix, 16)
                    sp.dma_start(uD[:, :, :, :], A["glu_state"]).then_inc(in_mix, 16)
                if j == 8:
                    sp.wait_ge(memset_done, 1)
                    sp.dma_start(A["yrows"][E * CAP:, :].rearrange("(n p) d -> p n d", p=P),
                                 S[:, :, :].rearrange("p h n -> p (h n)").unsqueeze(1).to_broadcast([P, OVF * CAP // P, D])
                                 ).then_inc(zero_out, 16)
            sp.wait_ge(s_ready, NC)
            sp.dma_start(O["s_prompt"], S[:, :, :]).then_inc(out_st, 16)
            sp.wait_ge(conv_done, NQKV)
            sp.dma_start(O["q_prompt"], q3[:, :, :]).then_inc(out_st, 16)
            sp.dma_start(O["q_sample"], xD[:, :, :, :]).then_inc(out_st, 16)
            sp.wait_ge(u_ready, KD)
            sp.dma_start(O["g_prompt"], uP[:, :, NPR:]).then_inc(out_st, 16)
            sp.dma_start(O["g_sample"], uD[:, :, :, :]).then_inc(out_st, 16)
            sp.wait_ge(sd_new, 16)
            sp.dma_start(O["s_sample"], wflat).then_inc(out_st, 16)
            sp.wait_ge(outer_done, 16)
            sp.dma_start(qT[:, :, :], A["xT"]).then_inc(in_x2, 16)
            wgu = A["gate_up"].rearrange("e (k p) n -> e p k n", p=P)
            wdn = A["down"].rearrange("e (u a p) n -> e p u a n", p=P, a=2)

            def load(e, i):
                if i < GU:
                    src, dst = wgu[e, :, i, :], raw(i)
                else:
                    src, dst = wdn[e, :, i - GU, :, :], work[:, 2 * (i - GU):2 * (i - GU) + 2, :]
                sp.dma_start(dst, src).then_inc(raw_in[i], 16)
            for i in range(GU):
                sp.wait_ge(chunk_done, CPB * (NB - RING + i // 2 + 1))
                load(0, i)
            sp.wait_ge(out_st, 6 * 16)
            sp.dma_start(wr[:, :, :], A["wr"]).then_inc(in_moe, 16)
            for i in range(GU, UNITS):
                load(0, i)
            sp.wait_ge(in_moe, 16)
            sp.wait_ge(h2_ready, 1)
            sp.dma_start(cx[:, :], A["cx"]).then_inc(in_moe, 16)
            sp.dma_start(btab[:, :], A["btab"]).then_inc(in_moe, 16)
            sp.dma_start(bdn[:, :], A["bdn"]).then_inc(in_moe, 16)

            def body(blk, e):
                for i in range(UNITS):
                    sp.wait_ge(unit_used, UNITS * blk - UNITS + i + 1)
                    load(e, i)
            with sp.Fori(1, E) as e:
                body(e, e)
            overflow(sp, lambda blk, b: body(blk, sp.value_load(obi[0:1, bass.ds(b, 1)], min_val=0, max_val=E - 1)))
            sp.wait_ge(all_done, 1)
            for t, (t0, m) in enumerate(TILES):
                for dst, src in ((facc, "fbrows"), (g2t, "g2rows"), (x1t, "x1rows")):
                    sp.dma_start(dst[0:m, t, :], A[src][t0:t0 + m, :]).then_inc(resid_in, 16)
            for t, (t0, m) in enumerate(TILES):
                sp.wait_ge(out_ready, t + 1)
                sp.dma_start(O["y"][t0:t0 + m, :], facc[0:m, t, :]).then_inc(out_st, 16)
            sp.wait_ge(out_st, 16 * (6 + len(TILES)))

        @block.tensor
        def _(pe):
            def chunk(n, cols=NT, rhs=None):
                j = n // CPB
                if n % CPB == 0:
                    pe.wait_ge(ring_in[j % RING], 16 * (j // RING + 1))
                pe.wait_ge(chunk_taken, n if n in (C_QKV, C_GDN) else n - 1)
                rhs = hT if rhs is None else rhs
                for k in range(KD):
                    mm = pe.matmul(ps[:, n % 2, 0:cols], ring[:, j % RING, k, (n % CPB) * P:(n % CPB + 1) * P],
                                   rhs[:, k, 0:cols], start=(k == 0), stop=(k == KD - 1))
                mm.then_inc(chunk_done, 1)

            def rows(a):
                j = ADA_BLOCKS[a]
                pe.wait_ge(ring_in[j % RING], 16 * (j // RING + 1))
                if a not in (0, 1):
                    pe.wait_ge(chunk_taken, CPB * (j if a in (4, 5) else j - 1) - (CPB if a == 5 else 0))
                for k in range(KD):
                    mm = pe.matmul(ps[0:1 + NDE, a % 2, :], cT[:, k, :], ring[:, j % RING, k, :],
                                   start=(k == 0), stop=(k == KD - 1))
                mm.then_inc(ada_rows, 1)

            def columns(a):
                pe.wait_ge(ada_copied, a + 1)
                for i in range(CPB):
                    tr = pe.transpose(ps[:, a % 2, (1 + NDE) * i:(1 + NDE) * (i + 1)],
                                      arow[:, i * P:(i + 1) * P], ident[0:1 + NDE, 0:1 + NDE])
                tr.then_inc(chunk_done, CPB)

            pe.wait_ge(c_silu, 1)
            for a in range(4):
                rows(a)
                if a == 0:
                    pe.wait_ge(memset_done, 1)
                    pe.wait_ge(m_sq, 1)
                    for k in range(KD):
                        mm = pe.matmul(ps[:, 2, 0:NT], ones[:, :], qT[:, k, :], start=(k == 0), stop=(k == KD - 1))
                    mm.then_inc(m_ss, 1)
                    pe.wait_ge(in_cv, 16)
                else:
                    columns(a - 1)
            columns(3)
            pe.wait_ge(h_ready, 1)
            pe.wait_ge(in_mix, 3 * 16)
            for t, (t0, m) in enumerate(((0, P), (P, P), (NPR, NDE))):
                for k in range(KD):
                    mm = pe.matmul(ps[0:m, 3, 2 * H * t:2 * H * (t + 1)], hT[:, k, t0:t0 + m], wba[:, k, :],
                                   start=(k == 0), stop=(k == KD - 1))
            mm.then_inc(logit_done, 1)
            for n in range(C_QKV, C_UV):
                chunk(n)
            pe.wait_ge(g_ready, 1)
            pe.wait_ge(logit_copy, 1)
            for c in range(NC):
                mm = pe.matmul(ps[:, 3, 64 + H * c:64 + H * (c + 1)], upper, tk[:, 4, c, :], start=True, stop=True)
            mm.then_inc(gc_done, 1)

            def decay_sums(c):
                pe.wait_ge(ug_ready, c + 1)
                for g in range(2):
                    mm = pe.matmul(bank(2 + g), ones[:, :], bX[:, 4 * g:4 * g + 4, :], start=True, stop=True)
                mm.then_inc(R_done, 1)

            def l2(i):
                pe.wait_ge(l2_sq, i + 1)
                if i >= 2:
                    pe.wait_ge(l2_root, i - 1)
                pe.matmul(ps[:, 4 + i % 2, 0:NT], ones[:, :], sq[:, i % 4, :], start=True, stop=True).then_inc(l2_ss, 1)
            for n in range(16):
                chunk(C_UV + n)
                l2(n)
                if n == 1:
                    pe.wait_ge(gc_ready, 1)
                    decay_sums(0)
            filler = list(FILL)

            def fill(k):
                for _ in range(min(k, len(filler))):
                    what, n = filler.pop(0)
                    if what == "chunk":
                        chunk(n)
                    else:
                        if n < 12:
                            rows(n)
                        if n > 4:
                            columns(n - 1)

            for c in range(NC):
                tok = slice(c * CH, (c + 1) * CH)
                if c > 0:
                    pe.wait_ge(s_ready, c)
                    pe.wait_ge(o_ready, c)
                    pe.wait_ge(vn_ready, c)
                    decay_sums(c)
                else:
                    pe.wait_ge(l2_done, 16)
                    pe.wait_ge(l2_root, 16)
                for h in range(H):
                    mm = pe.matmul(two(4)[:, h, :], kT[:, h, tok], kT[:, h, tok], start=True, stop=True)
                mm.then_inc(gram_done, 1)
                for h in range(H):
                    mm = pe.matmul(two(6)[:, h, :], kT[:, h, tok], qT[:, h, tok], start=True, stop=True)
                mm.then_inc(gram_done, 1)
                fill(2)
                for l in range(LEVELS):
                    s = c * LEVELS + l
                    for g in range(2):
                        pe.wait_ge(b_ready, s + 1)
                        if l > 0:
                            pe.wait_ge(mt_upd, 2 * s + g - 1)
                        else:
                            pe.wait_ge(R_used, c + 1)
                        for h in range(4 * g, 4 * g + 4):
                            mm = pe.matmul(half(2 + g)[:, h % 4, :], bB[s % 2][:, h, :],
                                           ident if l == 0 else bMT[:, h, :], start=True, stop=True)
                        mm.then_inc(z_done, 1)
                    if l == 0:
                        fill(1)
                        continue
                    fill(1)
                    for g in range(2):
                        pe.wait_ge(z_copied, 2 * (c * (LEVELS - 1) + l - 1) + g + 1)
                        pe.wait_ge(m_upd, 2 * (s - c) + g - 1)
                        if l == 1:
                            pe.wait_ge(a_ready, c + 1)
                            pe.wait_ge(intra_ready, c + 1)
                        for h in range(4 * g, 4 * g + 4):
                            mm = pe.matmul(half(4 + g)[:, h % 4, :], bM[:, h, :], bZ[:, h, :], start=True, stop=True)
                        if l < LEVELS - 1:
                            for h in range(4 * g, 4 * g + 4):
                                mm = pe.matmul(half(6 + g)[:, h % 4, :], bZ[:, h, :], bM[:, h, :], start=True, stop=True)
                        mm.then_inc(m_done, 1)
                pe.wait_ge(z_copied, 2 * (c + 1) * (LEVELS - 1))
                for h in range(H):
                    pe.transpose(two(2)[:, h, :], vT[:, h, tok], ident)
                pe.wait_ge(mt_upd, 2 * (c + 1) * LEVELS)
                for h in range(H):
                    mm = pe.transpose(two(4)[:, h, :], kT[:, h, tok], ident)
                mm.then_inc(vk_done, 1)
                fill(1)
                pe.wait_ge(vk_ready, c + 1)
                if c > 0:
                    for h in range(H):
                        mm = pe.matmul(two(2)[:, h, :], bB1[:, h, :], bMT[:, h, :], start=True, stop=True)
                    mm.then_inc(w_done, 1)
                    pe.wait_ge(w_ready, c)
                pe.wait_ge(m_upd, 2 * (c + 1) * (LEVELS - 1))
                for h in range(H):
                    mm = pe.matmul(two(6)[:, h, :], bMT[:, h, :], bB0[:, h, :], start=True, stop=(c == 0))
                    if c > 0:
                        mm = pe.matmul(two(6)[:, h, :], bX[:, h, :], S[:, h, :], start=False, stop=True)
                mm.then_inc(u_done, 1)
                fill(1)
                pe.wait_ge(vn_ready, c + 1)
                for h in range(H):
                    mm = pe.matmul(two(4)[:, h, :], bM[:, h, :], bI[:, h, :], start=True, stop=(c == 0))
                    if c > 0:
                        mm = pe.matmul(two(4)[:, h, :], S[:, h, :], qT[:, h, tok], start=False, stop=True)
                mm.then_inc(o_done, 1)
                for h in range(H):
                    mm = pe.matmul(two(2)[:, h, :], bZ[:, h, :], bM[:, h, :], start=True, stop=True)
                mm.then_inc(s_done, 1)
            fill(99)
            pe.wait_ge(s_ready, NC)
            pe.wait_ge(dec_in, 1)
            pe.matmul(ps[:, 2, 0:2 * H * NDE], ones[0:NDE, :], bc8[:, :, :, :].rearrange("p a h b -> p (a h b)"),
                      start=True, stop=True)
            pe.matmul(ps[:, 2, 2 * H * NDE:3 * H * NDE], ones[:, :], dcol[:, 0, :, :].rearrange("p h b -> p (h b)"),
                      start=True, stop=True).then_inc(dbc_done, 1)
            for n in range(C_GDN + CPB, C_GDN + CPB + 2):
                chunk(n)
            pe.wait_ge(conf_done, KD + 1)
            pe.wait_ge(o_ready, NC)
            for k in range(KD):
                mm = pe.matmul(ps[:, 4, 0:NT], ones[:, :], cvT[:, k, :], start=(k == 0), stop=(k == KD - 1))
            mm.then_inc(ln_sums, 1)
            for n in range(C_GDN + CPB + 2, C_PW):
                chunk(n)
            pe.wait_ge(ln_power, 1)
            for k in range(KD):
                mm = pe.matmul(ps[:, 5, 0:NT], ones[:, :], qT[:, k, :], start=(k == 0), stop=(k == KD - 1))
            mm.then_inc(ln_sums, 1)
            pe.wait_ge(in_sd, 16)
            for b in range(NDE):
                for h in range(H):
                    at = 2 * (h * NDE + b)
                    mm = pe.matmul(ps[:, 3, at:at + 2], Sd[:, b * H + h, :], kq[:, h, b, :], start=True, stop=True)
            mm.then_inc(sk_done, 1)
            pe.wait_ge(delta_ready, 1)
            pe.transpose(ps[0:H * NDE, 2, 192:192 + P], dcol[:, 9, :, :].rearrange("p h b -> p (h b)"), ident)
            pe.transpose(ps[0:H * NDE, 2, 320:320 + P], dcol[:, 6, :, :].rearrange("p h b -> p (h b)"), ident
                         ).then_inc(drow_done, 1)
            pe.wait_ge(og_sq, 1)
            pe.wait_ge(vn_ready, NC)
            for h in range(H):
                if h >= 2:
                    pe.wait_ge(og_root, h - 1)
                pe.matmul(ps[:, 6 + h % 2, 0:NT], ones[:, :], kT[:, h, :], start=True, stop=True).then_inc(og_ss, 1)
            pe.wait_ge(drow_copy, 1)
            pe.wait_ge(ln_power, 2)
            pe.wait_ge(conf_ready, 1)
            for i in range(KD):
                chunk(C_PW + i, NT, cvT)
                for g in (2 * i, 2 * i + 1):
                    pe.wait_ge(dm_ready, g + 1)
                    if g >= 2:
                        pe.wait_ge(sd_new, g - 1)
                    pe.matmul(bank(4 + g % 2), drow[:, 0, :], dmask[:, g % 4, :], start=True, stop=True
                              ).then_inc(outer_done, 1)
            pe.wait_ge(merged_ready, KD)

            def square_sum(i, k):
                pe.wait_ge(m_sq, 2 + KD * i + k)
                if i == 0 and k == 0:
                    pe.wait_ge(drow_copy, 1)
                mm = pe.matmul(ps[:, 2, 0:NT], ones[:, :], gcvT[:, k, :], start=(k == 0), stop=(k == KD - 1))
                if k == KD - 1:
                    mm.then_inc(m_ss, 1)
            for k in range(KD):
                chunk(C_OUT + k, NT, vT)
                if k > 0:
                    square_sum(0, k - 1)
            square_sum(0, KD - 1)
            for k in range(KD):
                square_sum(1, k)
            pe.wait_ge(h2_ready, 1)
            pe.wait_ge(in_moe, 16)
            for t, (t0, m) in enumerate(TILES):
                for k in range(KD):
                    mm = pe.matmul(ps[0:m, 3, E * t:E * (t + 1)], hT[:, k, t0:t0 + m], wr[:, k, :],
                                   start=(k == 0), stop=(k == KD - 1))
            mm.then_inc(rl_done, 1)

            def to_rows(n, src, t0, m):
                if n >= 2:
                    pe.wait_ge(tm_copied, n - 1)
                for k in range(KD):
                    tr = pe.transpose(ps[0:m, 4 + 2 * (n % 2) + k // 4, (k % 4) * P:(k % 4 + 1) * P], src[:, k, t0:t0 + m], ident)
                tr.then_inc(tm_done, 1)
            for n in range(3):
                to_rows(n, hT, *TILES[n])
            pe.wait_ge(sel_ready, 1)
            pe.wait_ge(in_moe, 4 * 16)
            for t in range(3):
                for u in range(t + 1):
                    pe.matmul(ps[:, 2, E * t:E * (t + 1)], cxc("strict_upper") if u == t else ones[:, :], r3[:, 3, u, :],
                              start=(u == 0), stop=(u == t))
            for u in range(3):
                mm = pe.matmul(ps[:, 2, 3 * E:4 * E], ones[:, :], r3[:, 3, u, :], start=(u == 0), stop=(u == 2))
            mm.then_inc(rank_done, 1)
            for n in range(3, 6):
                to_rows(n, qT, *TILES[n - 3])
            pe.wait_ge(gt_spread, 1)
            for n in range(6, 9):
                to_rows(n, hT, *TILES[n - 6])
            def tables(g):
                pe.wait_ge(hot_ready, g + 1)
                for e in range(0, GRP, 2):
                    b = GRP * g + e
                    for t, (t0, m) in enumerate(TILES):
                        mm = pe.matmul(ps[:, 3, 3 * b:3 * b + 6],
                                       selb[g % 2][0:m, t, e:e + 2, :].rearrange("p e n -> p (e n)"),
                                       tg[0:m, t, b:b + 2, :].rearrange("p e a -> p (e a)"), start=(t == 0), stop=(t == 2))
                mm.then_inc(tab_done, 1)
            for g in range(2):
                tables(g)
            pe.wait_ge(gate_ready, 1)
            pe.wait_ge(tm_copied, 9)
            for t, (t0, m) in enumerate(TILES):
                mm = pe.transpose(ps[0:E, 4, t0:t0 + m], r3[0:m, 5, t, :], ident[0:m, 0:m])
            mm.then_inc(gt_done, 1)

            pe.wait_ge(gt_copied, 1)
            pe.wait_ge(in_moe, 4 * 16)
            for t, (t0, m) in enumerate(TILES):
                if t > 1:
                    pe.wait_ge(bias_copied, t - 1)
                for n in range(2):
                    mm = pe.matmul(ps[0:m, 4 + 2 * (t % 2) + n, :], GT[:, t0:t0 + m], bdn[:, n * 512:(n + 1) * 512], start=True, stop=True)
                mm.then_inc(bias_done, 1)
            def rows_in(blk):
                pe.wait_ge(xg_in, 16 * blk + 16)
                for k in range(KD):
                    tr = pe.matmul(ps[:, 0, CAP * k:CAP * (k + 1)], Xg[:, k * P:(k + 1) * P], ident[0:CAP, 0:CAP],
                                   start=True, stop=True)
                tr.then_inc(xt_done, 1)

            def body(blk, e):
                first = isinstance(blk, int)
                pe.wait_ge(xs_ready, blk + 1)
                if not first:
                    pe.wait_ge(gd_copied, blk)
                    pe.wait_ge(ga_copied, blk)
                for i in range(GU):
                    pe.wait_ge(lo_done, UNITS * blk + i + 1)
                    for n in range(4):
                        for a, part in enumerate((stH[:, i % NSTG, :], low(i))):
                            mm = pe.matmul(bank(n), XS[:, i, :], part[:, n * 512:(n + 1) * 512],
                                           start=(i == 0 and a == 0), stop=(i == GU - 1 and a == 1))
                    mm.then_inc(unit_used, 1)
                pe.wait_ge(ga_copied, blk + 1)
                if not first:
                    pe.wait_ge(act_ready, blk)
                for m in range(2 * KD):
                    if m == KD:
                        pe.wait_ge(gd_copied, blk + 1)
                    mm = pe.matmul(ps[:, 6 + m // KD, CAP * (m % KD):CAP * (m % KD + 1)], G[:, m * P:(m + 1) * P],
                                   cxc("fold"), start=True, stop=True)
                    if m % KD == KD - 1:
                        mm.then_inc(fold_done, 1)
                rows_in(blk + 1)
                pe.wait_ge(as_ready, blk + 1)
                if not first:
                    pe.wait_ge(y_ready, blk)
                for i in range(GU, UNITS):
                    pe.wait_ge(lo_done, UNITS * blk + i + 1)
                    for a in range(2):
                        for n in range(2):
                            for b, part in enumerate((stH[:, i % NSTG, :], low(i))):
                                mm = pe.matmul(bank(4 + n), AS[:, 2 * (i - GU) + a, :],
                                               part[:, a * D + n * 512:a * D + (n + 1) * 512],
                                               start=(i == GU and a == 0 and b == 0),
                                               stop=(i == UNITS - 1 and a == 1 and b == 1))
                    mm.then_inc(unit_used, 1)
            rows_in(0)
            for g in range(2, NTAB // GRP):
                tables(g)
            pe.wait_ge(bias_copied, 3)
            body(0, 0)
            with pe.Fori(1, E) as e:
                body(e, e)
            overflow(pe, body)

        @block.scalar
        def _(act):
            chain = [act_chain, 0]

            def take(n):
                act.wait_ge(chunk_done, n + 1)

            act.wait_ge(in_c, 16)
            act.activation(cT[:, :, :], cT[:, :, :], ACT.Silu).then_inc(c_silu, 1)

            def rows(a):
                act.wait_ge(ada_rows, a + 1)
                if a >= 1:
                    act.wait_ge(chunk_done, CPB * (ADA_BLOCKS[a - 1] + 1))
                act.activation(arow[:, :], ps[0:1 + NDE, a % 2, :], ACT.Copy).then_inc(ada_copied, 1)

            def columns(a):
                take(CPB * ADA_BLOCKS[a] + CPB - 1)
                if a == 0:
                    act.wait_ge(in_pv, 16)
                for i in range(CPB):
                    n = CPB * a + i
                    act.activation(adaT[:, n // KD, n % KD, :], ps[:, a % 2, (1 + NDE) * i:(1 + NDE) * (i + 1)],
                                   ACT.Identity, bias=par("b_ada")[:, n:n + 1]).then_inc(chunk_taken, 1)
            for a in range(4):
                if a > 0:
                    columns(a - 1)
                rows(a)
                if a == 0:
                    act.wait_ge(m_ss, 1)
                    act.wait_ge(in_cv, 16)
                    act.activation(row[:, 0, :], ps[:, 2, 0:NT], ACT.Sqrt, bias=con("eps")[:, 0:1]).then_inc(m_root, 1)
            columns(3)
            act.wait_ge(logit_done, 1)
            act.wait_ge(memset_done, 1)
            act.activation(ba[:, 0:2, :], ps[:, 3, 0:4 * H].rearrange("p (t n) -> p t n", t=2), ACT.Copy)
            act.activation(ba[0:NDE, 2, :], ps[0:NDE, 3, 4 * H:6 * H], ACT.Copy).then_inc(logit_copy, 1)
            act.wait_ge(logit_copy, 1)
            act.activation(tk[:, 0, :, :], ba[:, :, 0:H], ACT.Sigmoid).then_inc(beta_ready, 1)
            act.wait_ge(softplus_in, 1)
            link(act, chain, act.activation(tk[:, 2, :, :], tk[:, 2, :, :], ACT.Exp, scale=-1.0))
            act.activation(tk[:, 3, 0, :], par("a_log"), ACT.Exp)
            act.activation(tk[:, 2, :, :], tk[:, 2, :, :], ACT.Ln, bias=ones[:, 0:1]).then_inc(gate_in, 1)
            act.wait_ge(in_mix, 3 * 16)

            def silu_qkv(m):
                act.wait_ge(conv_done, m + 1)
                act.activation((qT, kT, vT)[m // KD][:, m % KD, :], qc[:, m % 4, :], ACT.Silu).then_inc(qkv_ready, 1)
            for m in range(NQKV):
                n = C_QKV + m
                take(n)
                if m >= 4:
                    act.wait_ge(conv_done, m - 3)
                act.activation(qx[:, m % 4, SC - 1:], ps[:, n % 2, 0:NPR], ACT.Copy)
                act.activation(xD[:, m, :, SC - 1], ps[:, n % 2, NPR:NT], ACT.Copy).then_inc(chunk_taken, 1)
                if m >= 1:
                    silu_qkv(m - 1)
            silu_qkv(NQKV - 1)
            for n in range(C_Z, C_UV):
                take(n)
                act.activation(zT[:, n - C_Z, :], ps[:, n % 2, 0:NT], ACT.Silu).then_inc(chunk_taken, 1)
            act.wait_ge(in_mix, 3 * 16)

            def l2_square(i):
                act.wait_ge(qkv_ready, i + 1)
                if i >= 4:
                    act.wait_ge(l2_ss, i - 3)
                act.activation(sq[:, i % 4, :], (qT, kT)[i // KD][:, i % KD, :], ACT.Square).then_inc(l2_sq, 1)

            def l2_sqrt(i):
                act.wait_ge(l2_ss, i + 1)
                if i >= 4:
                    act.wait_ge(l2_done, i - 3)
                act.activation(rt[:, i % 4, :], ps[:, 4 + i % 2, 0:NT], ACT.Sqrt,
                               bias=con("eps")[:, 1:2]).then_inc(l2_root, 1)

            def decays(c):
                act.wait_ge(split_ready, c + 1)
                act.activation(bA[:, :, :], bA[:, :, :], ACT.Exp, scale=-1.0).then_inc(decay_exp, 1)
                act.activation(bI[:, :, :], bI[:, :, :], ACT.Exp).then_inc(decay_exp, 1)
                act.wait_ge(R_done, c + 1)
                act.activation(gl[:, 0, :], two(2)[:, :, CH - 1], ACT.Exp)
                act.activation(tk[:, 7, c, :], tk[:, 5, c, :], ACT.Exp)
                act.activation(tk[:, 8, c, :], bX[:, :, CH - 1], ACT.Exp).then_inc(small_exp, 1)
            l2_square(0)
            for i in range(16):
                n = C_UV + i
                take(n)
                if i < KD:
                    act.activation(uP[:, i, CC - 1:], ps[:, n % 2, 0:NPR], ACT.Copy)
                    act.activation(uD[:, i, :, CC - 1], ps[:, n % 2, NPR:NT], ACT.Copy).then_inc(chunk_taken, 1)
                else:
                    act.activation(gdnT[:, i - KD, :], ps[:, n % 2, 0:NT], ACT.Copy).then_inc(chunk_taken, 1)
                if i < 15:
                    l2_square(i + 1)
                l2_sqrt(i)
                if i == 8:
                    decays(0)
                    act.activation(gl[:, 1, :], two(2)[:, :, CH - 1], ACT.Copy).then_inc(R_used, 1)
            act.wait_ge(chunk_taken, C_GCV)
            for i in range(KD):
                act.activation(gdnT[:, i, :], gdnT[:, i, :], ACT.Sigmoid).then_inc(ug_sig, 1)
            filler = list(FILL)

            def fill(k):
                for _ in range(min(k, len(filler))):
                    what, n = filler.pop(0)
                    if what == "chunk":
                        take(n)
                        if n == C_GDN:
                            act.wait_ge(u_ready, KD)
                        dst = gcvT[:, n - C_GCV, :] if n < C_ADA2 else gdnT[:, n - C_GDN, :]
                        act.activation(dst, ps[:, n % 2, 0:NT], ACT.Copy).then_inc(chunk_taken, 1)
                    else:
                        if n > 4:
                            columns(n - 1)
                        if n < 12:
                            rows(n)

            for c in range(NC):
                tok = slice(c * CH, (c + 1) * CH)
                if c > 0:
                    decays(c)
                    act.wait_ge(decay_exp, 4)
                    act.activation(bZ[:, :, :], two(2), ACT.Exp).then_inc(R_used, 1)
                fill(2)
                for l in range(LEVELS):
                    if l == 0:
                        fill(1)
                        continue
                    fill(0)
                    for g in range(2):
                        act.wait_ge(z_done, 2 * (c * LEVELS + l) + g + 1)
                        if l == 1 and c > 0:
                            act.wait_ge(qe_ready, c)
                        if l > 1:
                            act.wait_ge(m_done, 2 * (c * (LEVELS - 1) + l - 2) + g + 1)
                        act.activation(bZ[:, 4 * g:4 * g + 4, :], half(2 + g), ACT.Copy).then_inc(z_copied, 1)
                    fill(1)
                fill(1)
                if c > 0:
                    act.wait_ge(w_done, c)
                    act.activation(bX[:, :, :], two(2), ACT.Copy, scale=-1.0).then_inc(w_ready, 1)
                act.wait_ge(u_done, c + 1)
                act.activation(bM[:, :, :], two(6), ACT.Copy).then_inc(vn_ready, 1)
                fill(1)
                act.wait_ge(o_done, c + 1)
                act.activation(vT[:, :, tok], two(4), ACT.Copy).then_inc(o_ready, 1)
            fill(99)
            d2 = lambda i: dcol[:, i, :, :].rearrange("p h b -> p (h b)")
            act.wait_ge(dbc_done, 1)
            act.activation(d2(1), ps[:, 2, 0:64], ACT.Exp)
            act.activation(dcol[:, 2:4, :, :].rearrange("p a h b -> p (a h b)"), ps[:, 2, 64:192], ACT.Copy
                           ).then_inc(dbc_copy, 1)
            for n in range(C_GDN + CPB, C_PW):
                take(n)
                act.activation(gdnT[:, n - C_GDN, :], ps[:, n % 2, 0:NT], ACT.Copy).then_inc(chunk_taken, 1)
                if n == C_GDN + CPB + 2:
                    act.wait_ge(ln_centred, 1)
                    act.wait_ge(o_done, NC)
                    act.activation(qT[:, :, :], cvT[:, :, :], ACT.Square).then_inc(ln_power, 1)
            act.wait_ge(chunk_taken, C_PW)
            act.activation(gdnT[:, :, :], gdnT[:, :, :], ACT.Sigmoid).then_inc(mg_sig, 1)
            act.activation(gcvT[:, :, :], gcvT[:, :, :], ACT.Sigmoid).then_inc(mg_sig, 1)
            act.wait_ge(ln_sums, 2)
            act.activation(row[:, 0, :], ps[:, 5, 0:NT], ACT.Sqrt, scale=1.0 / D, bias=con("eps")[:, 3:4]
                           ).then_inc(ln_power, 1)
            act.wait_ge(ln_norm, 1)
            for k in range(KD):
                ins = act.activation(cvT[:, k, :], cvT[:, k, :], ACT.Silu, scale=par("g_ln")[:, k:k + 1],
                                     bias=par("b_ln")[:, k:k + 1])
            ins.then_inc(conf_ready, 1)
            act.wait_ge(drow_done, 1)
            act.activation(drow[:, :, :], ps[0:H * NDE, 2, 192:448].rearrange("p (a n) -> p a n", a=2), ACT.Copy
                           ).then_inc(drow_copy, 1)
            act.wait_ge(delta_ready, 2)
            act.activation(kT[:, :, :], vT[:, :, :], ACT.Square).then_inc(og_sq, 1)
            for h in range(H):
                act.wait_ge(og_ss, h + 1)
                act.activation(kT[:, h, :], ps[:, 6 + h % 2, 0:NT], ACT.Sqrt, bias=con("eps")[:, 2:3]).then_inc(og_root, 1)
            for n in range(C_PW, C_OUT):
                take(n)
                act.activation(hT[:, n - C_PW, :], ps[:, n % 2, 0:NT], ACT.Identity,
                               bias=par("b_pw")[:, n - C_PW:n - C_PW + 1]).then_inc(chunk_taken, 1)
            for n in range(C_OUT, NB * CPB):
                take(n)
                act.activation(kT[:, n - C_OUT, :], ps[:, n % 2, 0:NT], ACT.Copy).then_inc(chunk_taken, 1)
                if n == C_OUT:
                    act.wait_ge(merged_ready, KD)
                act.wait_ge(chunk_taken, n + 1)
                act.activation(gcvT[:, n - C_OUT, :], kT[:, n - C_OUT, :], ACT.Square).then_inc(m_sq, 1)
            act.wait_ge(m_ss, 2)
            act.activation(row[:, 0, :], ps[:, 2, 0:NT], ACT.Sqrt, bias=con("eps")[:, 0:1]).then_inc(m_root, 1)
            for k in range(KD):
                act.wait_ge(x1_ready, k + 1)
                act.activation(gcvT[:, k, :], qT[:, k, :], ACT.Square).then_inc(m_sq, 1)
            act.wait_ge(m_ss, 3)
            act.activation(row[:, 0, :], ps[:, 2, 0:NT], ACT.Sqrt, bias=con("eps")[:, 0:1]).then_inc(m_root, 1)
            act.wait_ge(rl_ready, 1)
            act.activation(r3[:, 4, :, :], r3[:, 4, :, :], ACT.Exp).then_inc(rl_exp, 1)
            act.wait_ge(h2_ready, 1)
            for n in range(9):
                t0, m = TILES[n % 3]
                act.wait_ge(tm_done, n + 1)
                dst = rowbuf[n % 4][0:m, :]
                if n >= 4:
                    act.wait_ge(rows_out[n % 4], 16 * (n // 4))
                b0 = 4 + 2 * (n % 2)
                act.activation(dst, ps[0:m, b0:b0 + 2, :].rearrange("p b n -> p (b n)"), ACT.Copy).then_inc(tm_copied, 1)
                act.wait_ge(tm_copied, n + 1)
                act.dma_start((A["h2rows"], A["x1rows"], A["g2rows"])[n // 3][t0:t0 + m, :], dst).then_inc(rows_out[n % 4], 16)
            act.wait_ge(gt_done, 1)
            act.activation(GT[:, :], ps[0:E, 4, 0:NT], ACT.Copy).then_inc(gt_copied, 1)
            for t, (t0, m) in enumerate(TILES):
                act.wait_ge(bias_done, t + 1)
                b0 = 4 + 2 * (t % 2)
                act.activation(fbt[t][0:m, :], ps[0:m, b0:b0 + 2, :].rearrange("p b n -> p (b n)"), ACT.Copy).then_inc(bias_copied, 1)
                act.wait_ge(bias_copied, t + 1)
                act.dma_start(A["fbrows"][t0:t0 + m, :], fbt[t][0:m, :]).then_inc(fb_out, 16)

            def rows_hi(blk):
                act.wait_ge(xt_done, blk + 1)
                act.activation(XS[:, :, 0:CAP], ps[:, 0, :].rearrange("p (k n) -> p k n", k=KD), ACT.Copy).then_inc(xsh_ready, 1)
            rows_hi(0)
            act.wait_ge(tab_ready, 2)
            act.activation(tabg[CAP:2 * CAP, :], tabg[0:CAP, :], ACT.Copy).then_inc(tab_dup, 1)

            def hi(blk, i):
                act.wait_ge(raw_in[i], 16 * blk + 16 + (RING_END if on_ring(i) else 0))
                if not (isinstance(blk, int) and i < NSTG):
                    act.wait_ge(unit_used, UNITS * blk + i - NSTG + 1)
                act.activation(stH[:, i % NSTG, :], raw(i), ACT.Copy).then_inc(hi_done, 1)

            def rows_of(blk):
                act.wait_ge(unit_used, UNITS * blk + UNITS)
                act.activation(yl[:, :], ps[CAP:2 * CAP, 4:6, :].rearrange("p b n -> p (b n)"), ACT.Copy,
                               scale=gcol[CAP:2 * CAP, 0:1]).then_inc(yl_ready, 1)

            def body(blk, e):
                for i in range(GU + 1):
                    hi(blk, i)
                    if i == NSTG - 1 and not isinstance(blk, int):
                        rows_of(blk - 1)
                act.wait_ge(unit_used, UNITS * blk + GU)
                if isinstance(blk, int):
                    act.wait_ge(fb_out, 48)
                act.activation(G[:, 0:D], ps[:, 0:2, :].rearrange("p b n -> p (b n)"), ACT.Copy).then_inc(ga_copied, 1)
                hi(blk, GU + 1)
                act.wait_ge(t1_ready, blk + 1)
                act.activation(nl[:, 3, :, :], nl[:, 0, :, :], ACT.Sigmoid, scale=ALPHA).then_inc(sg_ready, 1)
                hi(blk, GU + 2)
                act.wait_ge(act_ready, blk + 1)
                act.activation(AS[:, :, 0:CAP], nl[:, 2, :, :], ACT.Copy).then_inc(ash_ready, 1)
                rows_hi(blk + 1)
                hi(blk, GU + 3)
            for i in range(4):
                act.wait_ge(rows_out[i], 16 * (3 if i == 0 else 2))
            act.wait_ge(tab_dup, 1)
            body(0, 0)
            with act.Fori(1, E) as e:
                body(e, e)
            n = overflow(act, body)
            rows_of(n + (E - 1))
            for t, (t0, m) in enumerate(TILES):
                act.wait_ge(f_ready[t], 1 + t % 2)
                act.activation(sqt[0:m, :], facc[0:m, t, :], ACT.Square, accum_out=ss[0:m, t, :]).then_inc(f_sq, 1)
                act.wait_ge(f_sq, 2 * t + 1)
                act.activation(rs[0:m, t, :], ss[0:m, t, :], ACT.Sqrt, bias=con("eps")[0:m, 0:1]).then_inc(f_sq, 1)

        @block.vector
        def _(dve):
            chain = [dve_chain, 0]
            lk = lambda ins: link(dve, chain, ins)
            dve.wait_ge(in_pv, 16)
            allrow = row[:, 1:2, :].to_broadcast([P, KD, NT])
            dve.wait_ge(m_root, 1)
            lk(dve.reciprocal(row[:, 1, :], row[:, 0, :]))
            dve.wait_ge(in_x, 16)
            dve.wait_ge(m_sq, 1)
            lk(dve.tensor_tensor(hT[:, :, :], hT[:, :, :], allrow, ALU.mult))
            dve.wait_ge(chunk_taken, C_QKV)
            lk(dve.scalar_tensor_tensor(out=cg[:, 0, :, :], in0=adaT[:, 1, :, :], scalar=1.0,
                                        in1=par("g_pre_mix").unsqueeze(2).to_broadcast([P, KD, 1 + NDE]),
                                        op0=ALU.add, op1=ALU.mult))
            lk(dve.tensor_scalar(cg[:, 0, :, :], cg[:, 0, :, :], float(D) ** 0.5, None, ALU.mult))

            def modulate(dst, coef, shift):
                lk(dve.tensor_tensor(dst[:, :, NPR:NT], dst[:, :, NPR:NT], coef[:, :, 1:], ALU.mult))
                lk(dve.tensor_tensor(dst[:, :, NPR:NT], dst[:, :, NPR:NT], shift[:, :, 1:], ALU.add))
                for k in range(KD):
                    ins = dve.tensor_scalar(dst[:, k, 0:NPR], dst[:, k, 0:NPR], coef[:, k, 0:1], shift[:, k, 0:1],
                                            ALU.mult, ALU.add)
                return ins
            modulate(hT, cg[:, 0, :, :], adaT[:, 0, :, :]).then_inc(h_ready, 1)
            dve.wait_ge(h_ready, 1)

            dve.wait_ge(in_mix, 3 * 16)
            dve.wait_ge(memset_done, 1)
            dve.wait_ge(logit_copy, 1)
            dt3 = par("dt_bias").unsqueeze(1).to_broadcast([P, 3, H])
            lk(dve.tensor_tensor(tk[:, 1, :, :], ba[:, :, H:2 * H], dt3, ALU.add))
            lk(dve.tensor_scalar(tk[:, 2, :, :], tk[:, 1, :, :], -1.0, None, ALU.mult))
            dve.tensor_tensor(tk[:, 2, :, :], tk[:, 1, :, :], tk[:, 2, :, :], ALU.max).then_inc(softplus_in, 1)
            wq = par("w_qkv_conv").rearrange("p (m j) -> p m j", j=SC)
            for m in range(NQKV):
                n = C_QKV + m
                dve.wait_ge(chunk_taken, n + 1)
                if m >= 4:
                    dve.wait_ge(qkv_ready, m - 3)
                s = m % 4
                out = qc[:, s, 0:NPR]
                dve.tensor_tensor(tmp[:, s, :, :], xD[:, m, :, :], wq[:, m:m + 1, :].to_broadcast([P, NDE, SC]), ALU.mult)
                dve.tensor_copy(q3[:, m, :], qx[:, s, NPR:NPR + SC - 1])
                lk(dve.tensor_scalar(out, qx[:, s, 0:NPR], wq[:, m, 0:1], None, ALU.mult))
                for j in range(1, SC):
                    lk(dve.scalar_tensor_tensor(out=out, in0=qx[:, s, j:j + NPR], scalar=wq[:, m, j:j + 1], in1=out,
                                                op0=ALU.mult, op1=ALU.add))
                dve.tensor_reduce(qc[:, s, NPR:NT], tmp[:, s, :, :], AX.X, ALU.add).then_inc(conv_done, 1)
            dve.wait_ge(gate_in, 1)
            lk(dve.scalar_tensor_tensor(out=tk[:, 4, :, :], in0=tk[:, 1, :, :], scalar=0.0, in1=tk[:, 2, :, :],
                                        op0=ALU.max, op1=ALU.add))
            dve.scalar_tensor_tensor(out=tk[:, 4, :, :], in0=tk[:, 4, :, :], scalar=-1.0,
                                     in1=tk[:, 3, 0:1, :].to_broadcast([P, 3, H]),
                                     op0=ALU.mult, op1=ALU.mult).then_inc(g_ready, 1)
            dve.wait_ge(gc_done, 1)
            dve.tensor_copy(tk[:, 5, 0:2, :], ps[:, 3, 64:64 + 2 * H].rearrange("p (c h) -> p c h", c=2)).then_inc(gc_ready, 1)
            dve.wait_ge(gc_ready, 1)
            dve.wait_ge(beta_ready, 1)


            def spread_g(c):
                dve.tensor_tensor(bX[:, :, :], upper.unsqueeze(1).to_broadcast([P, H, P]),
                                  tk[:, 4, c, :].unsqueeze(2).to_broadcast([P, H, P]), ALU.mult).then_inc(ug_ready, 1)

            def differences(c):
                dve.wait_ge(R_done, c + 1)
                gcb = tk[:, 5, c, :].unsqueeze(2).to_broadcast([P, H, P])
                lk(dve.tensor_tensor(bX[:, :, :], two(2), gcb, ALU.subtract))
                lk(dve.tensor_scalar(bA[:, :, :], bX[:, :, :], 0.0, None, ALU.max))
                dve.tensor_tensor(bI[:, :, :], bX[:, :, :], bA[:, :, :], ALU.subtract).then_inc(split_ready, 1)
            spread_g(0)
            for i in range(16):
                if i == 4:
                    dve.wait_ge(qkv_ready, NQKV)
                    differences(0)
                dve.wait_ge(l2_root, i + 1)
                lk(dve.reciprocal(rt[:, i % 4, :], rt[:, i % 4, :]))
                t = (qT, kT)[i // KD][:, i % KD, :]
                dve.scalar_tensor_tensor(out=t, in0=t, scalar=float(P) ** -0.5 if i < KD else 1.0, in1=rt[:, i % 4, :],
                                         op0=ALU.mult, op1=ALU.mult).then_inc(l2_done, 1)
            taps = [(k, j) for g in CONV_DVE for j in range(CC) for k in g]
            last = {}

            def conf_conv(n):
                for _ in range(min(n, len(taps))):
                    k, j = taps.pop(0)
                    out, src = cvT[:, k, 0:NPR], uP[:, k, j:j + NPR]
                    if j == 0:
                        dve.wait_ge(u_ready, k + 1)
                        ins = dve.tensor_scalar(out, src, wd[:, k, 0:1], par("b_dw")[:, k:k + 1], ALU.mult, ALU.add)
                    else:
                        dve.wait_ge(dve_chain, last[k])
                        ins = dve.scalar_tensor_tensor(out=out, in0=src, scalar=wd[:, k, j:j + 1], in1=out,
                                                       op0=ALU.mult, op1=ALU.add)
                    if j == CC - 1:
                        ins.then_inc(conf_done, 1)
                    else:
                        ins.then_inc(dve_chain, 1)
                        chain[1] += 1
                        last[k] = chain[1]
            for c in range(NC):
                tok = slice(c * CH, (c + 1) * CH)
                if c > 0:
                    dve.wait_ge(u_done, c)
                    dve.wait_ge(o_done, c)
                    dve.wait_ge(s_done, c)
                    spread_g(c)
                    differences(c)
                dve.wait_ge(gram_done, 2 * c + 1)
                dve.wait_ge(decay_exp, 2 * c + 1)
                for h in range(H):
                    ins = dve.scalar_tensor_tensor(out=bA[:, h, :], in0=two(4)[:, h, :], scalar=tk[:, 0, c, h:h + 1],
                                                   in1=bA[:, h, :], op0=ALU.mult, op1=ALU.mult)
                ins.then_inc(a_ready, 1)
                dve.wait_ge(decay_ready, c + 1)
                dve.wait_ge(gram_done, 2 * c + 2)
                dve.tensor_tensor(bI[:, :, :], two(6), bI[:, :, :], ALU.mult).then_inc(intra_ready, 1)
                if c == 0:
                    for i in range(KD):
                        dve.wait_ge(ug_sig, i + 1)
                        dve.tensor_tensor(uP[:, i, CC - 1:], uP[:, i, CC - 1:], gdnT[:, i, 0:NPR], ALU.mult)
                        dve.tensor_tensor(uD[:, i, :, CC - 1], uD[:, i, :, CC - 1], gdnT[:, i, NPR:NT], ALU.mult).then_inc(u_ready, 1)
                    dve.wait_ge(g_ready, 1)
                    dve.wait_ge(l2_done, 16)
                    for i, src in ((0, kT), (1, qT)):
                        dve.tensor_copy(kq[:, :, :, i], src[:, :, NPR:NT])
                    dve.tensor_copy(dcol[:, 9, :, :], kT[:, :, NPR:NT])
                    dve.tensor_tensor(dcol[:, 0, :, :], kT[:, :, NPR:NT], qT[:, :, NPR:NT], ALU.mult)
                    dve.wait_ge(beta_ready, 1)
                    for i, src in ((0, 4), (1, 0)):
                        ins = dve.tensor_tensor(bc8[:, i, :, :], ident[0:NDE, 0:NDE].unsqueeze(1).to_broadcast([NDE, H, NDE]),
                                                tk[0:NDE, src, 2, :].unsqueeze(2).to_broadcast([NDE, H, NDE]), ALU.mult)
                    ins.then_inc(dec_in, 1)
                if c > 0:
                    dve.wait_ge(R_used, c + 1)
                    dve.tensor_tensor(qT[:, :, tok], qT[:, :, tok], bZ[:, :, :], ALU.mult).then_inc(qe_ready, 1)
                for l in range(LEVELS):
                    s = c * LEVELS + l
                    conf_conv(13)
                    for g in range(2):
                        hs = slice(4 * g, 4 * g + 4)
                        idb = ident.unsqueeze(1).to_broadcast([P, 4, P])
                        if l == 0:
                            dve.wait_ge(z_done, 2 * s + g + 1)
                            dve.tensor_tensor(bMT[:, hs, :], idb, half(2 + g), ALU.subtract).then_inc(mt_upd, 1)
                            dve.tensor_tensor(bM[:, hs, :], idb, bB[s % 2][:, hs, :], ALU.subtract).then_inc(m_upd, 1)
                        else:
                            dve.wait_ge(m_done, 2 * (c * (LEVELS - 1) + l - 1) + g + 1)
                            dve.wait_ge(mt_upd, 2 * s + g - 1)
                            dve.tensor_tensor(bMT[:, hs, :], bMT[:, hs, :], half(4 + g), ALU.subtract).then_inc(mt_upd, 1)
                            if l < LEVELS - 1:
                                dve.wait_ge(m_upd, 2 * (s - c) + g - 1)
                                dve.tensor_tensor(bM[:, hs, :], bM[:, hs, :], half(6 + g), ALU.subtract).then_inc(m_upd, 1)
                dve.wait_ge(small_exp, c + 1)
                lk(dve.tensor_tensor(tk[:, 9, c, :], tk[:, 7, c, :], tk[:, 0, c, :], ALU.mult))
                dve.wait_ge(vk_done, c + 1)
                sc = lambda i: tk[:, i, c, :].unsqueeze(2).to_broadcast([P, H, P])
                dve.tensor_tensor(bB0[:, :, :], two(2), sc(0), ALU.mult)
                dve.tensor_tensor(bZ[:, :, :], two(4), sc(8), ALU.mult)
                dve.tensor_tensor(bB1[:, :, :], two(4), sc(9), ALU.mult).then_inc(vk_ready, 1)
                dve.wait_ge(s_done, c + 1)
                if c == 0:
                    dve.wait_ge(zero_out, 16)
                    dve.tensor_copy(S[:, :, :], two(2)).then_inc(s_ready, 1)
                else:
                    dve.wait_ge(s_ready, c)
                    for h in range(H):
                        ins = dve.scalar_tensor_tensor(out=S[:, h, :], in0=S[:, h, :], scalar=gl[:, 0, h:h + 1],
                                                       in1=two(2)[:, h, :], op0=ALU.mult, op1=ALU.add)
                    ins.then_inc(s_ready, 1)
            conf_conv(len(taps))
            dve.wait_ge(chunk_done, C_GDN)
            for k in range(KD):
                dve.wait_ge(u_ready, k + 1)
                lk(dve.tensor_tensor(ctap[:, k % 2, :, :], uD[:, k, :, :], wd[:, k:k + 1, :].to_broadcast([P, NDE, CC]), ALU.mult))
                dve.tensor_reduce(dcv[:, k, :], ctap[:, k % 2, :, :], AX.X, ALU.add).then_inc(dcv_done, 1)
            dve.wait_ge(dcv_done, KD)
            dve.tensor_tensor(cvT[:, :, NPR:NT], dcv[:, :, :], par("b_dw").unsqueeze(2).to_broadcast([P, KD, NDE]),
                              ALU.add).then_inc(conf_done, 1)
            dve.wait_ge(ln_sums, 1)
            lk(dve.tensor_scalar(row[:, 1, :], ps[:, 4, 0:NT], 1.0 / D, None, ALU.mult))
            dve.tensor_tensor(cvT[:, :, :], cvT[:, :, :], allrow, ALU.subtract).then_inc(ln_centred, 1)
            dve.wait_ge(ln_power, 2)
            lk(dve.reciprocal(row[:, 1, :], row[:, 0, :]))
            dve.tensor_tensor(cvT[:, :, :], cvT[:, :, :], allrow, ALU.mult).then_inc(ln_norm, 1)
            dve.wait_ge(sk_done, 1)
            dve.wait_ge(dbc_copy, 1)
            dv = vT[:, :, NPR:NT]
            sk = ps[:, 3, 0:2 * H * NDE].rearrange("p (h b a) -> p h b a", h=H, a=2)
            d = lambda i: dcol[:, i, :, :]
            lk(dve.tensor_tensor(d(4), sk[:, :, :, 0], d(1), ALU.mult))
            dve.tensor_tensor(d(7), sk[:, :, :, 1], d(1), ALU.mult)
            lk(dve.tensor_tensor(d(5), dv, d(4), ALU.subtract))
            dve.tensor_tensor(d(6), d(5), d(2), ALU.mult).then_inc(delta_ready, 1)
            dve.wait_ge(delta_ready, 1)
            lk(dve.tensor_tensor(d(8), d(6), d(3), ALU.mult))
            dve.tensor_tensor(dv, d(7), d(8), ALU.add).then_inc(delta_ready, 1)
            lk(dve.tensor_scalar(gdn_s[:, :], par("g_dn"), float(P) ** 0.5, None, ALU.mult))
            dve.wait_ge(mg_sig, 2)
            for k in range(KD):
                dve.wait_ge(og_root, k + 1)
                lk(dve.reciprocal(kT[:, k, :], kT[:, k, :]))
                lk(dve.scalar_tensor_tensor(out=vT[:, k, :], in0=vT[:, k, :], scalar=gdn_s[:, 0:1], in1=kT[:, k, :],
                                            op0=ALU.mult, op1=ALU.mult))
                lk(dve.tensor_tensor(vT[:, k, :], vT[:, k, :], zT[:, k, :], ALU.mult))
                lk(dve.tensor_tensor(vT[:, k, :], vT[:, k, :], gdnT[:, k, :], ALU.mult))
                for g in (2 * k, 2 * k + 1):
                    dve.wait_ge(outer_done, g + 1)
                    dve.wait_ge(sd_decayed, g + 1)
                    sg = Sd[:, 4 * g:4 * g + 4, :]
                    dve.tensor_tensor(sg, sg, half(4 + g % 2), ALU.add).then_inc(sd_new, 1)
                dve.wait_ge(chunk_taken, C_PW + k + 1)
                lk(dve.tensor_tensor(hT[:, k, :], hT[:, k, :], gcvT[:, k, :], ALU.mult))
                dve.tensor_tensor(vT[:, k, :], vT[:, k, :], hT[:, k, :], ALU.add).then_inc(merged_ready, 1)
            pb = lambda n: par(n).unsqueeze(2).to_broadcast([P, KD, 1 + NDE])
            root = float(D) ** 0.5
            dve.scalar_tensor_tensor(out=cg[:, 1, :, :], in0=adaT[:, 2, :, :], scalar=root, in1=pb("g_post_mix"),
                                     op0=ALU.mult, op1=ALU.mult)
            lk(dve.scalar_tensor_tensor(out=cg[:, 2, :, :], in0=adaT[:, 4, :, :], scalar=1.0, in1=pb("g_pre_ffn"),
                                        op0=ALU.add, op1=ALU.mult))
            dve.tensor_scalar(cg[:, 2, :, :], cg[:, 2, :, :], root, None, ALU.mult)
            lk(dve.scalar_tensor_tensor(out=cg[:, 3, :, :], in0=adaT[:, 5, :, :], scalar=root, in1=pb("g_post_ffn"),
                                        op0=ALU.mult, op1=ALU.mult))
            dve.wait_ge(m_root, 2)
            lk(dve.reciprocal(row[:, 1, :], row[:, 0, :]))
            lk(dve.tensor_tensor(kT[:, :, :], kT[:, :, :], allrow, ALU.mult))
            dve.wait_ge(in_x2, 16)
            lk(dve.tensor_tensor(kT[:, :, NPR:NT], kT[:, :, NPR:NT], cg[:, 1, :, 1:], ALU.mult))
            dve.tensor_tensor(qT[:, :, NPR:NT], qT[:, :, NPR:NT], kT[:, :, NPR:NT], ALU.add)
            for k in range(KD):
                dve.scalar_tensor_tensor(out=qT[:, k, 0:NPR], in0=kT[:, k, 0:NPR], scalar=cg[:, 1, k, 0:1],
                                         in1=qT[:, k, 0:NPR], op0=ALU.mult, op1=ALU.add).then_inc(x1_ready, 1)
            dve.wait_ge(x1_ready, KD)
            dve.wait_ge(m_root, 3)
            lk(dve.reciprocal(row[:, 1, :], row[:, 0, :]))
            lk(dve.tensor_tensor(hT[:, :, :], qT[:, :, :], allrow, ALU.mult))
            lk(dve.tensor_tensor(hT[:, :, NPR:NT], hT[:, :, NPR:NT], cg[:, 2, :, 1:], ALU.mult))
            dve.tensor_tensor(hT[:, :, NPR:NT], hT[:, :, NPR:NT], adaT[:, 3, :, 1:], ALU.add)
            for k in range(KD):
                ins = dve.tensor_scalar(hT[:, k, 0:NPR], hT[:, k, 0:NPR], cg[:, 2, k, 0:1], adaT[:, 3, k, 0:1],
                                        ALU.mult, ALU.add)
            ins.then_inc(h2_ready, 1)
            R = lambda i: r3[:, i, :, :]
            b3 = lambda a: a.unsqueeze(2).to_broadcast([P, 3, E])
            dve.wait_ge(memset_done, 2)
            dve.wait_ge(rl_done, 1)
            br = par("b_router")
            dve.tensor_tensor(r3[:, 0, 0:2, :], ps[:, 3, 0:2 * E].rearrange("p (t e) -> p t e", t=2),
                              br.unsqueeze(1).to_broadcast([P, 2, E]), ALU.add)
            lk(dve.tensor_tensor(r3[0:NDE, 0, 2, :], ps[0:NDE, 3, 2 * E:3 * E], br[0:NDE, :], ALU.add))
            for t in range(3):
                lk(dve.max(top8[:, t, :], r3[:, 0, t, :]))
            lk(dve.tensor_tensor(R(4), R(0), b3(top8[:, :, 0]), ALU.subtract))
            dve.tensor_tensor(R(1), R(0), b3(top8[:, :, TOPK - 1]), ALU.is_gt).then_inc(rl_ready, 1)
            dve.wait_ge(rl_ready, 1)
            lk(dve.tensor_tensor(R(2), R(0), b3(top8[:, :, TOPK - 1]), ALU.is_equal))
            lk(dve.tensor_reduce(s3[:, 0, :], R(1), AX.X, ALU.add))
            lk(dve.tensor_scalar(s3[:, 1, :], s3[:, 0, :], -1.0, float(TOPK), ALU.mult, ALU.add))

            def running(dst, src):
                for t in range(3):
                    ins = dve.tensor_tensor_scan(r3[:, dst, t, :], ones[:, 0:E], r3[:, src, t, :], 0.0, ALU.mult, ALU.add)
                return ins
            lk(running(3, 2))
            lk(dve.tensor_tensor(R(3), R(3), b3(s3[:, 1, :]), ALU.is_le))
            lk(dve.tensor_tensor(R(3), R(3), R(2), ALU.mult))
            lk(dve.tensor_tensor(R(3), R(3), R(1), ALU.add))
            dve.wait_ge(in_moe, 4 * 16)
            dve.tensor_tensor(R(3), R(3), b3(cxc("valid")), ALU.mult).then_inc(sel_ready, 1)
            dve.wait_ge(sel_ready, 1)
            dve.wait_ge(tm_done, 3)
            dve.wait_ge(rl_done, 1)
            dve.tensor_copy(hT[:, :, NPR:NT], cg[:, 3, :, 1:])
            dve.tensor_copy(hT[:, :, 0:NPR], cg[:, 3, :, 0:1].to_broadcast([P, KD, NPR])).then_inc(gt_spread, 1)
            lk(running(6, 3))
            dve.wait_ge(rl_exp, 1)
            lk(dve.tensor_tensor(R(4), R(4), R(3), ALU.mult))
            lk(dve.tensor_reduce(s3[:, 2, :], R(4), AX.X, ALU.add))
            lk(dve.tensor_scalar(s3[:, 2, :], s3[:, 2, :], 0.5, None, ALU.max))
            lk(dve.reciprocal(s3[:, 3, :], s3[:, 2, :]))
            dve.tensor_tensor(R(5), R(4), b3(s3[:, 3, :]), ALU.mult).then_inc(gate_ready, 1)
            dve.wait_ge(gate_ready, 1)
            dve.wait_ge(rank_done, 1)
            lk(dve.tensor_scalar(R(7), ps[:, 2, 0:3 * E].rearrange("p (t e) -> p t e", t=3), 1.0, None, ALU.add))
            lk(dve.tensor_tensor(R(7), R(7), R(3), ALU.mult))
            lk(dve.tensor_scalar(R(7), R(7), -1.0, None, ALU.add))
            lk(dve.tensor_copy(rk[:, :, 0:E], R(7)))

            def gates(cols, src):
                lk(dve.tensor_copy(tg[:, :, cols, 1], src))
                lk(dve.tensor_tensor(tg[:, :, cols, 2], src, tg[:, :, cols, 1].bitcast(F32), ALU.subtract))
            gates(slice(0, E), R(5))

            def copy_tables(e0, e1):
                for i in range(2):
                    tab = ps[CAP * i:CAP * (i + 1), 3, 3 * e0:3 * e1].rearrange("p (e b a) -> p e b a", b=2, a=3)
                    pair = lambda a: a[:, e0:e1].rearrange("p (e b) -> p e b", b=2)[:, :, i]
                    dve.tensor_copy(pair(tabi[:, :]), tab[:, :, i, 0])
                    lk(dve.tensor_copy(pair(tabg[0:CAP, :]), tab[:, :, i, 1]))
                    ins = dve.tensor_tensor(pair(tabg[0:CAP, :]), pair(tabg[0:CAP, :]), tab[:, :, i, 2], ALU.add)
                ins.then_inc(tab_ready, 1)
            lk(dve.tensor_copy(tg[:, :, :, 0], cxc("tokid").unsqueeze(2).to_broadcast([P, 3, NTAB])))

            def hot(g):
                if g > 1:
                    dve.wait_ge(tab_done, g - 1)
                for t in range(3):
                    ins = dve.tensor_tensor(selb[g % 2][:, t, :, :], cxc("iota").unsqueeze(1).to_broadcast([P, GRP, CAP]),
                                            rk[:, t, GRP * g:GRP * g + GRP].unsqueeze(2).to_broadcast([P, GRP, CAP]),
                                            ALU.is_equal)
                ins.then_inc(hot_ready, 1)
            for g in range(2):
                hot(g)
            cnt = ps[:, 2, 3 * E:4 * E]
            lk(dve.tensor_scalar(eb[:, 0, :], cnt, float(CAP), None, ALU.is_gt))
            for m in range(2, -(-NT // CAP)):
                lk(dve.scalar_tensor_tensor(out=eb[:, 0, :], in0=cnt, scalar=float(CAP * m), in1=eb[:, 0, :],
                                            op0=ALU.is_gt, op1=ALU.add))
            lk(dve.tensor_tensor_scan(eb[:, 1, :], ones[:, 0:E], eb[:, 0, :], 0.0, ALU.mult, ALU.add))
            lk(dve.tensor_tensor(eb[:, 2, :], eb[:, 1, :], eb[:, 0, :], ALU.subtract))
            blocks = cxc("blocks")
            bb = lambda a: a.unsqueeze(2).to_broadcast([P, OVF, E])
            be = lambda a: a.unsqueeze(1).to_broadcast([P, OVF, E])
            lk(dve.tensor_tensor(wsel, bb(blocks), be(eb[:, 2, :]), ALU.is_ge))
            lk(dve.tensor_tensor(prod, bb(blocks), be(eb[:, 1, :]), ALU.is_lt))
            lk(dve.tensor_tensor(wsel, wsel, prod, ALU.mult))
            lk(dve.tensor_tensor(prod, wsel, be(cxc("experts")), ALU.mult))
            lk(dve.tensor_reduce(ob[:, 0, :], prod, AX.X, ALU.add))
            lk(dve.tensor_tensor(prod, wsel, be(eb[:, 2, :]), ALU.mult))
            lk(dve.tensor_reduce(ob[:, 1, :], prod, AX.X, ALU.add))
            dve.tensor_copy(obi[:, 0:OVF], ob[:, 0, :])
            dve.tensor_copy(obi[:, OVF:OVF + 1], eb[:, 1, E - 1:E]).then_inc(novf_ready, 1)
            dve.wait_ge(tab_done, 2)
            copy_tables(0, 2 * GRP)
            lk(dve.tensor_tensor(ob[:, 2, :], blocks, ob[:, 1, :], ALU.subtract))
            lk(dve.tensor_scalar(ob[:, 2, :], ob[:, 2, :], float(CAP), float(CAP), ALU.mult, ALU.add))
            for t in range(3):
                lk(dve.tensor_tensor(prod, wsel, be(r3[:, 7, t, :]), ALU.mult))
                lk(dve.tensor_reduce(rk[:, t, E:NBLK], prod, AX.X, ALU.add))
                lk(dve.tensor_tensor(rk[:, t, E:NBLK], rk[:, t, E:NBLK], ob[:, 2, :], ALU.subtract))
                lk(dve.tensor_tensor(prod, wsel, be(r3[:, 5, t, :]), ALU.mult))
                lk(dve.tensor_reduce(gov[:, t, 0:OVF], prod, AX.X, ALU.add))
            gates(slice(E, NTAB), gov)
            for g in range(2, NTAB // GRP):
                hot(g)
            lk(dve.tensor_scalar(eb[:, 3, :], eb[:, 2, :], float(CAP), float(CAP * (E - 1)), ALU.mult, ALU.add))
            lk(dve.tensor_scalar(eb[:, 4, :], cxc("experts"), float(CAP), None, ALU.mult))
            lk(dve.tensor_tensor(eb[:, 3, :], eb[:, 3, :], eb[:, 4, :], ALU.subtract))
            b1 = lambda a: a.unsqueeze(1).to_broadcast([P, 3, E])
            lk(dve.tensor_scalar(R(8), R(7), float(CAP), None, ALU.is_ge))
            lk(dve.tensor_tensor(R(8), R(8), b1(eb[:, 3, :]), ALU.mult))
            lk(dve.tensor_tensor(R(8), R(8), b1(eb[:, 4, :]), ALU.add))
            lk(dve.tensor_tensor(R(8), R(8), R(7), ALU.add))
            lk(dve.tensor_tensor(R(8), R(8), R(3), ALU.mult))
            for k in range(TOPK):
                lk(dve.scalar_tensor_tensor(out=r3[:, 9, :, :].rearrange("p t e -> p (t e)"),
                                            in0=r3[:, 6, :, :].rearrange("p t e -> p (t e)"), scalar=float(k + 1),
                                            in1=r3[:, 8, :, :].rearrange("p t e -> p (t e)"),
                                            op0=ALU.is_equal, op1=ALU.mult))
                lk(dve.tensor_reduce(rowk[:, :, k], R(9), AX.X, ALU.add))
            dve.tensor_copy(rowi[:, :, :], rowk[:, :, :]).then_inc(rows_ready, 1)
            dve.wait_ge(tab_done, NTAB // GRP)
            copy_tables(2 * GRP, NTAB)
            dve.wait_ge(in_moe, 4 * 16)

            def lo(blk, i):
                dve.wait_ge(hi_done, UNITS * blk + i + 1)
                dve.tensor_tensor(low(i), raw(i), stH[:, i % NSTG, :].bitcast(F32), ALU.subtract
                                  ).then_inc(lo_done, 1)

            def rows_lo(blk):
                dve.wait_ge(xsh_ready, blk + 1)
                dve.tensor_tensor(XS[:, :, CAP:2 * CAP], ps[:, 0, :].rearrange("p (k n) -> p k n", k=KD),
                                  XS[:, :, 0:CAP].bitcast(F32), ALU.subtract).then_inc(xs_ready, 1)

            def rows_of(blk):
                dve.wait_ge(yl_ready, blk + 1)
                dve.scalar_tensor_tensor(out=yb[:, :], in0=ps[0:CAP, 4:6, :].rearrange("p b n -> p (b n)"),
                                         scalar=gcol[0:CAP, 0:1], in1=yl[:, :], op0=ALU.mult, op1=ALU.add
                                         ).then_inc(y_ready, 1)

            LINKS = 5

            def body(blk, e):
                first = isinstance(blk, int)
                links = [0]

                def lb(ins):
                    links[0] += 1
                    ins.then_inc(block_chain, 1)
                    dve.wait_ge(block_chain, LINKS * blk + links[0])
                for i in range(GU + 1):
                    lo(blk, i)
                    if i == NSTG - 1 and not first:
                        rows_of(blk - 1)
                if not first:
                    dve.wait_ge(y_ready, blk)
                dve.tensor_copy(gcol[:, :], tabg[:, bass.ds(blk, 1)])
                lb(dve.tensor_copy(bcol[:, :], btab[:, bass.ds(e * (2 * KD), 2 * KD)]))
                dve.wait_ge(unit_used, UNITS * blk + GU)
                if first:
                    dve.wait_ge(fb_out, 48)
                dve.tensor_copy(G[:, D:2 * D], ps[:, 2:4, :].rearrange("p b n -> p (b n)")).then_inc(gd_copied, 1)
                lo(blk, GU + 1)
                bias = lambda a: bcol[:, a * KD:(a + 1) * KD].unsqueeze(2).to_broadcast([P, KD, CAP])
                gl_ = nl[:, 0, :, :]
                up = nl[:, 1, :, :]
                dve.wait_ge(fold_done, 2 * blk + 1)
                lb(dve.tensor_tensor(gl_, ps[:, 6, :].rearrange("p (k n) -> p k n", k=KD), bias(0), ALU.add))
                dve.tensor_scalar(gl_, gl_, LIMIT, None, ALU.min).then_inc(t1_ready, 1)
                dve.wait_ge(fold_done, 2 * blk + 2)
                lb(dve.tensor_tensor(up, ps[:, 7, :].rearrange("p (k n) -> p k n", k=KD), bias(1), ALU.add))
                lb(dve.tensor_scalar(up, up, LIMIT, -LIMIT, ALU.min, ALU.max))
                dve.wait_ge(t1_ready, blk + 1)
                lb(dve.scalar_tensor_tensor(out=up, in0=up, scalar=1.0, in1=gl_, op0=ALU.add, op1=ALU.mult))
                dve.wait_ge(sg_ready, blk + 1)
                dve.tensor_tensor(nl[:, 2, :, :], up, nl[:, 3, :, :], ALU.mult).then_inc(act_ready, 1)
                lo(blk, GU + 2)
                dve.wait_ge(ash_ready, blk + 1)
                dve.tensor_tensor(AS[:, :, CAP:2 * CAP], nl[:, 2, :, :], AS[:, :, 0:CAP].bitcast(F32),
                                  ALU.subtract).then_inc(as_ready, 1)
                rows_lo(blk + 1)
                if not first:
                    dve.wait_ge(y_out, 16 * blk)
                lo(blk, GU + 3)
                assert links[0] == LINKS
            rows_lo(0)
            dve.wait_ge(tab_dup, 1)
            body(0, 0)
            with dve.Fori(1, E) as e:
                body(e, e)
            n = overflow(dve, lambda blk, b: body(blk, dve.value_load(obi[0:1, bass.ds(b, 1)], min_val=0, max_val=E - 1)))
            rows_of(n + (E - 1))
            dve.memset(s3[0:1, 0, 0:1], 0.0).then_inc(all_done, 1)

            def finish(t):
                m = TILES[t][1]
                f = facc[0:m, t, :]
                dve.wait_ge(f_sq, 2 * t + 2)
                lk(dve.reciprocal(rs[0:m, t, :], rs[0:m, t, :]))
                lk(dve.scalar_tensor_tensor(out=f, in0=f, scalar=rs[0:m, t, :], in1=g2t[0:m, t, :], op0=ALU.mult, op1=ALU.mult))
                dve.tensor_tensor(f, f, x1t[0:m, t, :], ALU.add).then_inc(out_ready, 1)
            for t in range(2):
                add_experts(dve, chain, t)
            for t in range(3):
                finish(t)

        @block.gpsimd
        def _(pool):
            pool.memset(ones[:, :], 1.0)
            pool.memset(ba[:, :, :], 0.0)
            pool.memset(S[:, :, :], 0.0)
            pool.memset(qx[:, :, 0:SC - 1], 0.0)
            pool.memset(uP[:, :, 0:CC - 1], 0.0).then_inc(memset_done, 1)
            pool.wait_ge(in_x, 16)
            pool.tensor_tensor(qT[:, :, :], hT[:, :, :], hT[:, :, :], ALU.mult).then_inc(m_sq, 1)
            pool.wait_ge(in_cv, 16)
            chain = [pool_chain, 0]
            taps = list(range(CC))
            tap = row[:, :, :].rearrange("p a n -> p (a n)")[:, 0:2 * NPR].rearrange("p (k n) -> p k n", k=2)

            def conf_conv(n):
                for _ in range(min(n, len(taps))):
                    j = taps.pop(0)
                    out, src = cvT[:, CONV_POOL, 0:NPR], uP[:, CONV_POOL, j:j + NPR]
                    if j == 0:
                        pool.wait_ge(u_ready, KD)
                    link(pool, chain, pool.tensor_tensor(tap, src, wd[:, CONV_POOL, j:j + 1].to_broadcast([P, 2, NPR]),
                                                         ALU.mult))
                    if j == 0:
                        link(pool, chain, pool.tensor_tensor(
                            out, tap, par("b_dw")[:, CONV_POOL].unsqueeze(2).to_broadcast([P, 2, NPR]), ALU.add))
                    elif j < CC - 1:
                        link(pool, chain, pool.tensor_tensor(out, out, tap, ALU.add))
                    else:
                        pool.tensor_tensor(out, out, tap, ALU.add).then_inc(conf_done, 2)
            masks = con("levels").rearrange("p (l n) -> p l n", l=LEVELS)
            for c in range(NC):
                pool.wait_ge(decay_exp, 2 * c + 2)
                pool.tensor_tensor(bI[:, :, :], bI[:, :, :], upper.unsqueeze(1).to_broadcast([P, H, P]),
                                   ALU.mult).then_inc(decay_ready, 1)
                pool.wait_ge(a_ready, c + 1)
                for l in range(LEVELS):
                    s = c * LEVELS + l
                    if l >= 2:
                        pool.wait_ge(z_done, 2 * (s - 1))
                        pool.wait_ge(m_upd, 2 * (c * (LEVELS - 1)) + 2)
                    if l < 2 and c > 0:
                        pool.wait_ge(u_done, c)
                    pool.tensor_tensor(bB[s % 2][:, :, :], bA[:, :, :], masks[:, l:l + 1, :].to_broadcast([P, H, P]),
                                       ALU.mult).then_inc(b_ready, 1)
                    if l >= 1:
                        conf_conv(3)
            conf_conv(len(taps))

            eg = dcol[:, 1, :, :]
            ihb = ident[0:H * NDE, 0:H * NDE].rearrange("p (h b) -> p h b", b=NDE)
            pool.wait_ge(dbc_copy, 1)
            pool.wait_ge(sk_done, 1)
            for g in range(16):
                b, h0 = g // 2, 4 * (g % 2)
                sg = Sd[:, 4 * g:4 * g + 4, :]
                pool.tensor_tensor(sg, sg, eg[:, h0:h0 + 4, b].unsqueeze(2).to_broadcast([P, 4, P]),
                                   ALU.mult).then_inc(sd_decayed, 1)
                if g == 0:
                    pool.wait_ge(drow_copy, 1)
                    pool.wait_ge(ln_sums, 2)
                if g >= 4:
                    pool.wait_ge(outer_done, g - 3)
                pool.tensor_tensor(dmask[:, g % 4, :].rearrange("p (h v) -> p h v", h=4),
                                   drow[:, 1:2, :].to_broadcast([H * NDE, 4, P]),
                                   ihb[:, h0:h0 + 4, b].unsqueeze(2).to_broadcast([H * NDE, 4, P]),
                                   ALU.mult).then_inc(dm_ready, 1)
            pool.wait_ge(out_st, 6 * 16)
            pool.wait_ge(h2_ready, 1)
            pool.memset(r3[:, 0, :, :], 0.0)
            pool.memset(gov[:, :, OVF:], 0.0)
            pool.memset(rk[:, :, NBLK:], -1.0).then_inc(memset_done, 1)

            def gather(blk):
                if not (isinstance(blk, int) and blk == 0):
                    pool.wait_ge(idx_ready, 2 * blk)
                pool.tensor_copy(idxc[:, :], tabi[:, bass.ds(blk, 1)]).then_inc(idx_ready, 1)
                pool.wait_ge(idx_ready, 2 * blk + 1)
                pool.tensor_tensor(idxw[:, 0:1], idxc[0:1, :], idxc[0:1, :], ALU.add).then_inc(idx_ready, 1)
                pool.indirect_dma_start(out=Xg[:, :], out_offset=None, in_=A["h2rows"],
                                        in_offset=bass.IndirectOffsetOnAxis(ap=idxc[:, :], axis=0)).then_inc(xg_in, 16)

            def store(blk):
                pool.wait_ge(y_ready, blk + 1)
                pool.dma_start(A["yrows"][bass.ds(blk * CAP, CAP), :], yb[:, :]).then_inc(y_out, 16)

            def body(blk, e):
                pool.wait_ge(xt_done, blk + 1)
                gather(blk + 1)
                if not isinstance(blk, int):
                    store(blk - 1)
                pool.wait_ge(xg_in, 16 * blk + 32)
            pool.wait_ge(tab_ready, 1)
            pool.wait_ge(zero_out, 16)
            for i in range(3):
                pool.wait_ge(rows_out[i], 16)
            gather(0)
            pool.wait_ge(xg_in, 16)
            pool.wait_ge(tab_ready, 2)
            body(0, 0)
            with pool.Fori(1, E) as e:
                body(e, e)
            n = overflow(pool, body)
            store(n + (E - 1))
            pool.wait_ge(rows_ready, 1)
            pool.wait_ge(all_done, 1)
            pool.wait_ge(y_out, (n + E) * 16)
            pool.tensor_tensor(idxw[:, 1:2], idxc[0:1, :], idxc[0:1, :], ALU.add)
            for t, (t0, m) in enumerate(TILES):
                for k in range(TOPK):
                    pool.indirect_dma_start(out=yg[0:m, t, k, :], out_offset=None, in_=A["yrows"],
                                            in_offset=bass.IndirectOffsetOnAxis(ap=rowi[0:m, t, k:k + 1], axis=0)
                                            ).then_inc(tail_in[t], 16)
            add_experts(pool, chain, 2)


def consts():
    import numpy as np
    c = np.zeros((P, NCV), np.float32)
    i, j = np.arange(P)[:, None], np.arange(P)[None, :]

    def put(name, a):
        c[:, CV[name][0]:CV[name][1]] = a
    put("ident", i == j)
    put("upper", i <= j)
    lv = [(i >> (l + 1) == j >> (l + 1)) & ((i >> l) & 1 == 1) & ((j >> l) & 1 == 0) for l in range(LEVELS)]
    put("levels", np.concatenate(lv, 1))
    put("eps", np.array([[D * EPS, EPS, P * EPS, EPS]]) + 0 * i)
    x = np.zeros((P, NCX), np.float32)

    def put(name, a):
        x[:, CX[name][0]:CX[name][1]] = a
    put("iota", np.arange(CAP)[None, :])
    put("strict_upper", i < j)
    put("tokid", np.arange(3)[None, :] * P + i)
    put("valid", np.arange(3)[None, :] * P + i < NT)
    put("experts", np.arange(E)[None, :])
    put("fold", i % CAP == np.arange(CAP)[None, :])
    put("blocks", np.arange(OVF)[None, :])
    return c, x


def layout(inputs):
    import numpy as np
    f = {k: np.asarray(v) for k, v in inputs.items()}

    def fm(a):
        return np.ascontiguousarray(a.reshape(a.shape[0], -1, P).transpose(2, 1, 0))

    def rep(a):
        return np.broadcast_to(a.reshape(1, -1), (P, a.size))
    x = np.concatenate([f["x_prompt"][0], f["x_sample"][:, 0]], 0)
    c = np.concatenate([f["c_prompt"], f["c_sample"]], 0)
    cols = {"b_ada": fm(f["b_ada"])[:, :, 0], "w_qkv_conv": fm(f["w_qkv_conv"][0]).reshape(P, -1),
            "w_dw": fm(f["w_dw_conv"][0]).reshape(P, -1), "b_dw": fm(f["b_dw_conv"])[:, :, 0],
            "g_ln": fm(f["g_ln_conv"])[:, :, 0], "b_ln": fm(f["b_ln_conv"])[:, :, 0],
            "b_pw": fm(f["b_pw_conv"])[:, :, 0], "g_dn": fm(f["g_dn_norm"])[:, :, 0],
            "a_log": rep(f["a_log"]), "dt_bias": rep(f["dt_bias"]), "b_router": rep(f["b_router"])}
    for n in ("g_pre_mix", "g_post_mix", "g_pre_ffn", "g_post_ffn"):
        cols[n] = fm(f[n])[:, :, 0]
    pvv = np.concatenate([cols[n] for n in PV], 1)
    qs = f["state_qkv_conv"][0].reshape(NDE, SC - 1, NQKV, P).transpose(3, 2, 0, 1)
    us = f["state_glu_conv"][0].reshape(NDE, CC - 1, KD, P).transpose(3, 2, 0, 1)
    w_in = f["w_in"][0]
    return {
        "cT": fm(c), "xT": fm(x), "pv": np.ascontiguousarray(pvv), "cv": consts()[0], "cx": consts()[1],
        "wr": np.ascontiguousarray(f["w_router"][0].reshape(KD, P, E).transpose(1, 0, 2)),
        "btab": np.ascontiguousarray(f["b_gate_up"][0].reshape(E, 2 * KD, P).transpose(2, 0, 1)).reshape(P, -1),
        "bdn": f["b_down"][0], "gate_up": f["w_gate_up"][0], "down": f["w_down"][0],
        "wba": np.ascontiguousarray(w_in[:, 4 * D:GLU0].reshape(KD, P, 2 * H).transpose(1, 0, 2)),
        "qkv_state": np.pad(qs, ((0, 0), (0, 0), (0, 0), (0, 1))),
        "glu_state": np.pad(us, ((0, 0), (0, 0), (0, 0), (0, 1))),
        "sdn": np.ascontiguousarray(f["state_dn"][0].reshape(NDE * H, P, P).transpose(1, 0, 2)).reshape(P, -1),
        "ada": f["w_ada"][0], "in": w_in, "pw": f["w_pw_conv"][0], "out": f["w_out"][0],
    }

OUTS = {"s_prompt": (P, H, P), "q_prompt": (P, NQKV, SC - 1), "q_sample": (P, NQKV, NDE, SC),
        "g_prompt": (P, KD, CC - 1), "g_sample": (P, KD, NDE, CC), "s_sample": (P, NDE * H * P), "y": (NT, D)}
SCRATCH = {"h2rows": (NT, D), "x1rows": (NT, D), "g2rows": (NT, D), "fbrows": (NT, D), "yrows": (NBLK * CAP, D)}


def kernel(**inputs):
    import numpy as np
    import concourse.bacc as _bacc
    from concourse import mybir as _mybir
    from concourse.bass_utils import run_bass_kernel_spmd as _run

    arrays = layout(inputs)
    nc = _bacc.Bacc("TRN2", target_bir_lowering=False, num_devices=1)
    ins, outs = {}, {}
    for n, a in arrays.items():
        ins[n] = nc.dram_tensor(n + "_dram", a.shape, _mybir.dt.from_np(a.dtype), kind="ExternalInput").ap()
    for n, shape in SCRATCH.items():
        ins[n] = nc.dram_tensor(n + "_dram", shape, _mybir.dt.float32, kind="Internal").ap()
    for n, shape in OUTS.items():
        outs[n] = nc.dram_tensor(n + "_dram", shape, _mybir.dt.float32, kind="ExternalOutput").ap()
    build(nc, ins, outs)
    r = _run(nc, [{n + "_dram": a for n, a in arrays.items()}], core_ids=[0])
    got = {n: np.asarray(r.results[0][n + "_dram"]).reshape(shape) for n, shape in OUTS.items()}

    def rows(a):
        a = np.moveaxis(a, (0, 1), (-1, -2))
        return np.ascontiguousarray(a.reshape(a.shape[:-2] + (-1,)))
    y = got["y"]
    return (y[None, :NPR], y[NPR:, None],
            np.ascontiguousarray(got["s_prompt"].transpose(1, 0, 2))[None, None],
            rows(got["q_prompt"])[None, None], rows(got["g_prompt"])[None, None],
            np.ascontiguousarray(got["s_sample"].reshape(P, NDE, H, P).transpose(1, 2, 0, 3))[None],
            rows(got["q_sample"][..., 1:])[None], rows(got["g_sample"][..., 1:])[None])
```
